# Optimizing a Trainium2 kernel written in Bass

```python
import math
import jax, jax.numpy as jnp
from jax import lax
import numpy as np

D_MODEL = 1024
BATCH = 1
SEQ = 128
DEPTH = 2
DEC_BATCH = 1
DEC_SEQ = 256
PAST_LEN = 128

GRID_W = 64
Q_BLOCK = 128
RET_CHUNK = 128
ROPE_BASE = 10000.0
EPS = 1e-6

MLA_HEADS = 8
MLA_NOPE = 64
MLA_ROPE = 32
MLA_V = 64
MLA_Q_LORA = 384
MLA_KV_LORA = 256
GQA_HEADS = 8
GQA_KV_HEADS = 2
GQA_HD = 64
RET_HEADS = 4
RET_DK = 64
RET_DV = 128
DIFF_HEADS = 4
DIFF_D = 64
DIFF_DV = 128
N_BRANCH = 4
BRANCH_W = 512
N_EXPERTS = 32
TOP_K = 4
N_GROUPS = 4
TOPK_GROUPS = 2
EXPERT_FF = 256
SHARED_FF = 256
ROUTE_SCALE = 2.5

IN_COLS = (MLA_Q_LORA + MLA_KV_LORA + MLA_ROPE
           + (GQA_HEADS + 2 * GQA_KV_HEADS) * GQA_HD
           + RET_HEADS * (2 * RET_DK + 2 * RET_DV)
           + DIFF_HEADS * (4 * DIFF_D + DIFF_DV)
           + N_BRANCH * D_MODEL)

kernel_name = "hybrid_diffusion_prefix_trunk_step"

def rms_norm(x, g):
    xf = x.astype(jnp.float32)
    y = xf * lax.rsqrt(jnp.mean(xf * xf, axis=-1, keepdims=True) + EPS)
    return (y * g.astype(jnp.float32)).astype(x.dtype)

def head_group_norm(o, g):
    mu = jnp.mean(o, axis=-1, keepdims=True)
    oc = o - mu
    y = oc * lax.rsqrt(jnp.mean(oc * oc, axis=-1, keepdims=True) + EPS)
    B, T = o.shape[:2]
    return y.reshape(B, T, -1) * g.astype(jnp.float32)

def _rope_1d(x, pos):
    half = x.shape[-1] // 2
    freq = ROPE_BASE ** (-jnp.arange(half, dtype=jnp.float32) / half)
    ang = pos.astype(jnp.float32)[:, None] * freq[None, :]
    shape = (1, pos.shape[0]) + (1,) * (x.ndim - 3) + (half,)
    cos = jnp.cos(ang).reshape(shape)
    sin = jnp.sin(ang).reshape(shape)
    xf = x.astype(jnp.float32)
    x1, x2 = xf[..., :half], xf[..., half:]
    return jnp.concatenate([x1 * cos - x2 * sin, x2 * cos + x1 * sin], axis=-1).astype(x.dtype)

def axial_rope(x, row, col):
    r = x.shape[-1] // 2
    return jnp.concatenate([_rope_1d(x[..., :r], row), _rope_1d(x[..., r:], col)], axis=-1)

def _attend_block(q, k, v, scale):
    s = jnp.einsum('bqkrd,bskd->bkrqs', q, k).astype(jnp.float32) * scale
    p = jax.nn.softmax(s, axis=-1).astype(v.dtype)
    return jnp.einsum('bkrqs,bske->bqkre', p, v)

def attend(q, k, v, scale):
    B, T = q.shape[:2]
    nb = T // Q_BLOCK
    qb = jnp.moveaxis(q.reshape((B, nb, Q_BLOCK) + q.shape[2:]), 1, 0)
    ob = lax.map(lambda qi: _attend_block(qi, k, v, scale), qb)
    return jnp.moveaxis(ob, 0, 1).reshape((B, T) + ob.shape[3:])

def retention_scan(q, k, v, log_gamma, s0):
    B, T, H, dk = q.shape
    dv = v.shape[-1]
    C = RET_CHUNK
    n = T // C
    f32 = jnp.float32
    idx = jnp.arange(C, dtype=f32)
    lg = log_gamma.astype(f32)[:, None]
    dist = idx[:, None] - idx[None, :]
    dmask = jnp.where(dist[None] >= 0, jnp.exp(lg[..., None] * jnp.maximum(dist, 0.0)[None]), 0.0)
    q_dec = jnp.exp(lg * (idx + 1.0)).T[None, :, :, None]
    k_dec = jnp.exp(lg * (C - 1.0 - idx)).T[None, :, :, None]
    chunk_dec = jnp.exp(lg[:, 0] * C)[None, :, None, None]
    qc = jnp.swapaxes(q.astype(f32).reshape(B, n, C, H, dk), 0, 1)
    kc = jnp.swapaxes(k.astype(f32).reshape(B, n, C, H, dk), 0, 1)
    vc = jnp.swapaxes(v.astype(f32).reshape(B, n, C, H, dv), 0, 1)

    def step(S, xs):
        qi, ki, vi = xs
        inner = jnp.einsum('bhij,bjhe->bihe', jnp.einsum('bihd,bjhd->bhij', qi, ki) * dmask[None], vi)
        cross = jnp.einsum('bihd,bhde->bihe', qi, S) * q_dec
        S_new = S * chunk_dec + jnp.einsum('bjhd,bjhe->bhde', ki * k_dec, vi)
        return S_new, inner + cross

    S, out = lax.scan(step, s0.astype(f32), (qc, kc, vc))
    return jnp.swapaxes(out, 0, 1).reshape(B, T, H, dv), S

def _split_cols(z):
    sizes = (MLA_Q_LORA, MLA_KV_LORA, MLA_ROPE,
             GQA_HEADS * GQA_HD, GQA_KV_HEADS * GQA_HD, GQA_KV_HEADS * GQA_HD,
             RET_HEADS * RET_DK, RET_HEADS * RET_DK, RET_HEADS * RET_DV, RET_HEADS * RET_DV,
             DIFF_HEADS * 2 * DIFF_D, DIFF_HEADS * 2 * DIFF_D, DIFF_HEADS * DIFF_DV,
             N_BRANCH * D_MODEL)
    offs = []
    acc = 0
    for s in sizes[:-1]:
        acc += s
        offs.append(acc)
    return jnp.split(z, offs, axis=-1)

def token_mixers(h, lp, lam_init, ctx, row, col):
    B, T, _ = h.shape
    dt = h.dtype
    latent = ctx is not None
    (cq, ckv, kpe, gq, gk, gv, rq, rk, rv, rg, dq, dk, dv, gl) = _split_cols(h @ lp['w_in'])

    qm = (rms_norm(cq, lp['g_mla_q']) @ lp['w_mla_uq']).reshape(B, T, MLA_HEADS, MLA_NOPE + MLA_ROPE)
    q_nope, q_pe = qm[..., :MLA_NOPE], qm[..., MLA_NOPE:]
    ckv = rms_norm(ckv, lp['g_mla_kv'])
    if latent:
        q_pe = axial_rope(q_pe, row, col)
        kpe_lat = axial_rope(kpe[:, :, None, :], row, col)[:, :, 0]
        ckv_all = jnp.concatenate([ctx['mla_ckv'].astype(dt), ckv], axis=1)
        kpe_all = jnp.concatenate([ctx['mla_kpe'].astype(dt), kpe_lat], axis=1)
    else:
        ckv_all, kpe_all = ckv, kpe
    S = ckv_all.shape[1]
    kv = (ckv_all @ lp['w_mla_ukv']).reshape(B, S, MLA_HEADS, MLA_NOPE + MLA_V)
    k_m = jnp.concatenate([kv[..., :MLA_NOPE],
                           jnp.broadcast_to(kpe_all[:, :, None, :], (B, S, MLA_HEADS, MLA_ROPE))], axis=-1)
    q_m = jnp.concatenate([q_nope, q_pe], axis=-1)[:, :, :, None, :]
    o_mla = attend(q_m, k_m, kv[..., MLA_NOPE:], (MLA_NOPE + MLA_ROPE) ** -0.5).reshape(B, T, BRANCH_W)

    gq = rms_norm(gq.reshape(B, T, GQA_HEADS, GQA_HD), lp['g_gqa_q'])
    gk = rms_norm(gk.reshape(B, T, GQA_KV_HEADS, GQA_HD), lp['g_gqa_k'])
    gv = gv.reshape(B, T, GQA_KV_HEADS, GQA_HD)
    if latent:
        gq = axial_rope(gq, row, col)
        gk_all = jnp.concatenate([ctx['gqa_k'].astype(dt), axial_rope(gk, row, col)], axis=1)
        gv_all = jnp.concatenate([ctx['gqa_v'].astype(dt), gv], axis=1)
    else:
        gk_all, gv_all = gk, gv
    o_gqa = attend(gq.reshape(B, T, GQA_KV_HEADS, GQA_HEADS // GQA_KV_HEADS, GQA_HD),
                   gk_all, gv_all, GQA_HD ** -0.5).reshape(B, T, BRANCH_W)

    rq = rq.reshape(B, T, RET_HEADS, RET_DK)
    rk = rk.reshape(B, T, RET_HEADS, RET_DK) * (RET_DK ** -0.5)
    rv = rv.reshape(B, T, RET_HEADS, RET_DV)
    lg = jax.nn.log_sigmoid(lp['ret_decay'].astype(jnp.float32))
    if latent:
        s_f0, s_b0 = ctx['ret'][:, 0], ctx['ret'][:, 1]
    else:
        s_f0 = jnp.zeros((B, RET_HEADS, RET_DK, RET_DV), jnp.float32)
        s_b0 = s_f0
    o_f, s_f = retention_scan(rq, rk, rv, lg[0], s_f0)
    o_b, s_b = retention_scan(jnp.flip(rq, 1), jnp.flip(rk, 1), jnp.flip(rv, 1), lg[1], s_b0)
    o_r = (head_group_norm(o_f + jnp.flip(o_b, 1), lp['g_ret'])
           * jax.nn.silu(rg.astype(jnp.float32))).astype(dt)

    dq = dq.reshape(B, T, DIFF_HEADS, 2, DIFF_D)
    dk = dk.reshape(B, T, DIFF_HEADS, 2, DIFF_D)
    dv = dv.reshape(B, T, DIFF_HEADS, DIFF_DV)
    if latent:
        dq = axial_rope(dq, row, col)
        dk_all = jnp.concatenate([ctx['diff_k'].astype(dt), axial_rope(dk, row, col)], axis=1)
        dv_all = jnp.concatenate([ctx['diff_v'].astype(dt), dv], axis=1)
    else:
        dk_all, dv_all = dk, dv
    lam_p = lp['diff_lambda'].astype(jnp.float32)
    lam = jnp.exp(jnp.sum(lam_p[0] * lam_p[1])) - jnp.exp(jnp.sum(lam_p[2] * lam_p[3])) + lam_init
    sc = DIFF_D ** -0.5
    a1 = attend(dq[:, :, :, 0:1, :], dk_all[:, :, :, 0, :], dv_all, sc)
    a2 = attend(dq[:, :, :, 1:2, :], dk_all[:, :, :, 1, :], dv_all, sc)
    o_d = (a1.astype(jnp.float32) - lam * a2.astype(jnp.float32))[:, :, :, 0, :]
    o_d = (rms_norm(o_d, lp['g_diff']) * (1.0 - lam_init)).reshape(B, T, BRANCH_W).astype(dt)

    br = jnp.stack([o_mla, o_gqa, o_r, o_d], axis=2)
    gates = jax.nn.sigmoid(gl.reshape(B, T, N_BRANCH, D_MODEL))
    merged = jnp.sum(gates * jnp.einsum('btnw,nwd->btnd', br, lp['w_br']), axis=2)
    out = merged @ lp['w_out']
    if latent:
        return out, None
    new_ret = jnp.stack([s_f, s_b], axis=1).astype(dt)
    return out, (ckv, kpe, gk, gv, dk, dv, new_ret)

def moe(h, lp):
    B, T, D = h.shape
    t = h.reshape(B * T, D)
    scores = jax.nn.sigmoid((t @ lp['w_router']).astype(jnp.float32))
    sel = scores + lp['b_router'].astype(jnp.float32)
    sel_g = sel.reshape(-1, N_GROUPS, N_EXPERTS // N_GROUPS)
    grp = jnp.sum(lax.top_k(sel_g, 2)[0], axis=-1)
    _, gidx = lax.top_k(grp, TOPK_GROUPS)
    gmask = jnp.any(gidx[:, :, None] == jnp.arange(N_GROUPS)[None, None, :], axis=1)
    masked = jnp.where(gmask[:, :, None], sel_g, -jnp.inf).reshape(-1, N_EXPERTS)
    _, eidx = lax.top_k(masked, TOP_K)
    w = jnp.take_along_axis(scores, eidx, axis=-1)
    w = w / jnp.sum(w, axis=-1, keepdims=True) * ROUTE_SCALE
    combine = jnp.sum(jax.nn.one_hot(eidx, N_EXPERTS, dtype=jnp.float32) * w[..., None], axis=1)
    gu = jnp.einsum('nd,edf->nef', t, lp['w_exp_gu'])
    a = jax.nn.silu(gu[..., :EXPERT_FF]) * gu[..., EXPERT_FF:]
    a = (a * combine[..., None].astype(a.dtype)).reshape(-1, N_EXPERTS * EXPERT_FF)
    routed = a @ lp['w_exp_down'].reshape(N_EXPERTS * EXPERT_FF, D_MODEL)
    sgu = t @ lp['w_sh_gu']
    shared = (jax.nn.silu(sgu[:, :SHARED_FF]) * sgu[:, SHARED_FF:]) @ lp['w_sh_down']
    return (routed + shared).reshape(B, T, D)

def trunk_layer(x, cvec, l, lp, ctx, row, col):
    mod = jax.nn.silu(cvec) @ lp['w_mod'] + lp['b_mod']
    sh1, sc1, g1, sh2, sc2, g2 = jnp.split(mod[:, None, :], 6, axis=-1)
    lam_init = 0.8 - 0.6 * math.exp(-0.3 * l)
    h = rms_norm(x, lp['g_pre1']) * (1.0 + sc1) + sh1
    m, new_cache = token_mixers(h, lp, lam_init, ctx, row, col)
    x = x + g1 * rms_norm(m, lp['g_post1'])
    h = rms_norm(x, lp['g_pre2']) * (1.0 + sc2) + sh2
    x = x + g2 * rms_norm(moe(h, lp), lp['g_post2'])
    return x, new_cache

def setup_inputs(seed: int = 0) -> dict:
    key = jax.random.key(seed)
    ks = iter(jax.random.split(key, 48))
    f32 = jnp.float32

    def nrm(shape, scale=1.0):
        return jax.random.normal(next(ks), shape, f32) * scale

    def gain(shape):
        return 1.0 + 0.02 * jax.random.normal(next(ks), shape, f32)

    L = DEPTH
    D = D_MODEL
    decay_base = jnp.log(2.0 ** (5.0 + jnp.arange(RET_HEADS, dtype=f32)) - 1.0)
    return {
        'x_prompt': nrm((BATCH, SEQ, D)),
        'x_sample': nrm((DEC_BATCH, DEC_SEQ, D)),
        'cache_mla_ckv': nrm((DEC_BATCH, L, PAST_LEN, MLA_KV_LORA)),
        'cache_mla_kpe': nrm((DEC_BATCH, L, PAST_LEN, MLA_ROPE)),
        'cache_gqa_k': nrm((DEC_BATCH, L, PAST_LEN, GQA_KV_HEADS, GQA_HD)),
        'cache_gqa_v': nrm((DEC_BATCH, L, PAST_LEN, GQA_KV_HEADS, GQA_HD)),
        'cache_diff_k': nrm((DEC_BATCH, L, PAST_LEN, DIFF_HEADS, 2, DIFF_D)),
        'cache_diff_v': nrm((DEC_BATCH, L, PAST_LEN, DIFF_HEADS, DIFF_DV)),
        'state_ret': nrm((DEC_BATCH, L, 2, RET_HEADS, RET_DK, RET_DV), 0.5),
        'c': nrm((DEC_BATCH, D)),
        'c_ctx': nrm((D,)),
        'w_mod': nrm((L, D, 6 * D), 0.5 * D ** -0.5),
        'b_mod': nrm((L, 6 * D), 0.02),
        'g_pre1': gain((L, D)),
        'g_post1': gain((L, D)),
        'g_pre2': gain((L, D)),
        'g_post2': gain((L, D)),
        'w_in': nrm((L, D, IN_COLS), D ** -0.5),
        'g_mla_q': gain((L, MLA_Q_LORA)),
        'w_mla_uq': nrm((L, MLA_Q_LORA, MLA_HEADS * (MLA_NOPE + MLA_ROPE)), MLA_Q_LORA ** -0.5),
        'g_mla_kv': gain((L, MLA_KV_LORA)),
        'w_mla_ukv': nrm((L, MLA_KV_LORA, MLA_HEADS * (MLA_NOPE + MLA_V)), MLA_KV_LORA ** -0.5),
        'g_gqa_q': gain((L, GQA_HD)),
        'g_gqa_k': gain((L, GQA_HD)),
        'ret_decay': decay_base + nrm((L, 2, RET_HEADS), 0.05),
        'g_ret': gain((L, RET_HEADS * RET_DV)),
        'diff_lambda': nrm((L, 4, DIFF_D), 0.1),
        'g_diff': gain((L, DIFF_DV)),
        'w_br': nrm((L, N_BRANCH, BRANCH_W, D), BRANCH_W ** -0.5),
        'w_out': nrm((L, D, D), D ** -0.5),
        'w_router': nrm((L, D, N_EXPERTS), D ** -0.5),
        'b_router': nrm((L, N_EXPERTS), 0.01),
        'w_exp_gu': nrm((L, N_EXPERTS, D, 2 * EXPERT_FF), D ** -0.5),
        'w_exp_down': nrm((L, N_EXPERTS, EXPERT_FF, D), EXPERT_FF ** -0.5),
        'w_sh_gu': nrm((L, D, 2 * SHARED_FF), D ** -0.5),
        'w_sh_down': nrm((L, SHARED_FF, D), SHARED_FF ** -0.5),
    }

def reference(x_prompt, x_sample, cache_mla_ckv, cache_mla_kpe, cache_gqa_k, cache_gqa_v,
              cache_diff_k, cache_diff_v, state_ret, c, c_ctx,
              w_mod, b_mod, g_pre1, g_post1, g_pre2, g_post2, w_in,
              g_mla_q, w_mla_uq, g_mla_kv, w_mla_ukv, g_gqa_q, g_gqa_k,
              ret_decay, g_ret, diff_lambda, g_diff, w_br, w_out,
              w_router, b_router, w_exp_gu, w_exp_down, w_sh_gu, w_sh_down):
    T_lat = x_sample.shape[1]
    rows = T_lat // GRID_W
    rr, cc = jnp.meshgrid(jnp.arange(rows), jnp.arange(GRID_W), indexing='ij')
    row, col = rr.reshape(-1), cc.reshape(-1)
    yp, ys = x_prompt, x_sample
    l_ckv, l_kpe, l_gk, l_gv, l_dk, l_dv, l_ret = [], [], [], [], [], [], []
    for l in range(DEPTH):
        lp = {
            'w_mod': w_mod[l], 'b_mod': b_mod[l],
            'g_pre1': g_pre1[l], 'g_post1': g_post1[l], 'g_pre2': g_pre2[l], 'g_post2': g_post2[l],
            'w_in': w_in[l],
            'g_mla_q': g_mla_q[l], 'w_mla_uq': w_mla_uq[l], 'g_mla_kv': g_mla_kv[l], 'w_mla_ukv': w_mla_ukv[l],
            'g_gqa_q': g_gqa_q[l], 'g_gqa_k': g_gqa_k[l],
            'ret_decay': ret_decay[l], 'g_ret': g_ret[l],
            'diff_lambda': diff_lambda[l], 'g_diff': g_diff[l],
            'w_br': w_br[l], 'w_out': w_out[l],
            'w_router': w_router[l], 'b_router': b_router[l],
            'w_exp_gu': w_exp_gu[l], 'w_exp_down': w_exp_down[l],
            'w_sh_gu': w_sh_gu[l], 'w_sh_down': w_sh_down[l],
        }
        yp, (n_ckv, n_kpe, n_gk, n_gv, n_dk, n_dv, n_ret) = trunk_layer(yp, c_ctx[None, :], l, lp, None, None, None)
        l_ckv.append(n_ckv); l_kpe.append(n_kpe); l_gk.append(n_gk); l_gv.append(n_gv)
        l_dk.append(n_dk); l_dv.append(n_dv); l_ret.append(n_ret)
        ctx = {
            'mla_ckv': cache_mla_ckv[:, l], 'mla_kpe': cache_mla_kpe[:, l],
            'gqa_k': cache_gqa_k[:, l], 'gqa_v': cache_gqa_v[:, l],
            'diff_k': cache_diff_k[:, l], 'diff_v': cache_diff_v[:, l],
            'ret': state_ret[:, l],
        }
        ys, _ = trunk_layer(ys, c, l, lp, ctx, row, col)
    new_mla_ckv = jnp.stack(l_ckv, axis=1)
    new_mla_kpe = jnp.stack(l_kpe, axis=1)
    new_gqa_k = jnp.stack(l_gk, axis=1)
    new_gqa_v = jnp.stack(l_gv, axis=1)
    new_diff_k = jnp.stack(l_dk, axis=1)
    new_diff_v = jnp.stack(l_dv, axis=1)
    new_state_ret = jnp.stack(l_ret, axis=1)
    return (yp, ys, new_mla_ckv, new_mla_kpe, new_gqa_k, new_gqa_v, new_diff_k, new_diff_v, new_state_ret)


_drawn_inputs = setup_inputs


def setup_inputs(seed=0):
    import zlib

    import numpy as np

    out = dict(_drawn_inputs(seed))
    spreads = {}
    factors = {'g_post2': 2.853, 'g_mla_q': 8.0, 'g_mla_kv': 2.842, 'g_gqa_q': 8.0}
    for name, (base, spread) in spreads.items():
        noise = np.random.default_rng([zlib.crc32(name.encode()), seed]).standard_normal(out[name].shape)
        drawn = base * np.exp(spread * noise) if base else spread * noise
        out[name] = __import__('jax').numpy.asarray(drawn.astype(out[name].dtype))
    for name, factor in factors.items():
        out[name] = (out[name] * factor).astype(out[name].dtype)
    return out
```

```python
import math
from contextlib import ExitStack

import numpy as np

import concourse.bass as bass
from concourse import mybir

P = 128
D = 1024
KD = D // P
T = 3
DEPTH = 2
F32 = mybir.dt.float32
ALU = mybir.AluOpType
ACT = mybir.ActivationFunctionType
AX = mybir.AxisListType.X
EPS = 1e-6
C = 512

Q_LORA, KV_LORA, M_ROPE, M_NOPE, M_V, M_HEADS = 384, 256, 32, 64, 64, 8
M_HD = M_NOPE + M_ROPE
HALF = M_HEADS // 2
HD, G_HEADS, G_KV = 64, 8, 2
R_HEADS, R_DK, R_DV = 4, 64, 128
F_HEADS, F_DV = 4, 128
NE, TOPK, NG, TOPG, FF = 32, 4, 4, 2, 256
EG = NE // NG
ROUTE_SCALE = 2.5
NBR = 4
BW = 512

SEG = {}
_at = 0
for _name, _n in (("cq", Q_LORA), ("ckv", KV_LORA + M_ROPE), ("gq", G_HEADS * HD), ("gkv", 2 * G_KV * HD),
                  ("rqk", 2 * R_HEADS * R_DK), ("rv", R_HEADS * R_DV), ("rg", R_HEADS * R_DV),
                  ("dq", F_HEADS * 2 * HD), ("dk", F_HEADS * 2 * HD), ("dv", F_HEADS * F_DV)):
    SEG[_name] = (_at, _n)
    _at += _n
ZC = _at
SEGS = list(SEG)
Z_CQ, Z_CKV, Z_KPE = 0, Q_LORA, Q_LORA + KV_LORA
Z_GQ, Z_GK = SEG["gq"][0], SEG["gkv"][0]
Z_GV = Z_GK + G_KV * HD
Z_RQ = SEG["rqk"][0]
Z_RK = Z_RQ + R_HEADS * R_DK
Z_RV, Z_RG = SEG["rv"][0], SEG["rg"][0]
Z_DQ, Z_DK, Z_DV = SEG["dq"][0], SEG["dk"][0], SEG["dv"][0]
OUT_COLS = [Z_CQ, Z_GQ, Z_RQ, Z_DQ]
Z_MERGED = Z_RV
Z_M = Z_DQ

GAIN = {}
_at = 0
for _name, _n in (("q", Q_LORA), ("kv", KV_LORA), ("gq", HD), ("gk", HD), ("ret", R_HEADS * R_DV), ("diff", F_DV)):
    GAIN[_name] = slice(_at, _at + _n)
    _at += _n
GAINS = _at

K_ID, K_DF, K_DB, K_MF, K_MB, K_C64 = 0, 128, 256, 384, 512, 640
K_S64, K_C32, K_S32, K_POS, K_N = 768, 896, 960, 1024, 1028
RANK_COLS = NE * NE


def constants():
    k = np.zeros((P, K_N), np.float32)
    k[:, K_ID:K_ID + P] = np.eye(P)
    j, i = np.meshgrid(np.arange(P), np.arange(P), indexing="ij")
    k[:, K_DF:K_DF + P] = np.maximum(i - j, 0)
    k[:, K_DB:K_DB + P] = np.maximum(j - i, 0)
    k[:, K_MF:K_MF + P] = i >= j
    k[:, K_MB:K_MB + P] = j >= i
    n = np.arange(2 * P)
    for d, at_c, at_s in ((64, K_C64, K_S64), (32, K_C32, K_S32)):
        quarter = d // 4
        freq = np.float32(10000.0) ** (-np.arange(quarter, dtype=np.float32) / np.float32(quarter))
        cos = np.zeros((2 * P, 2, 2, quarter), np.float32)
        sin = np.zeros_like(cos)
        for a, pos in enumerate((n // 64, n % 64)):
            ang = pos.astype(np.float32)[:, None] * freq[None]
            cos[:, a] = np.cos(ang)[:, None]
            sin[:, a, 0], sin[:, a, 1] = -np.sin(ang), np.sin(ang)
        for t in range(2):
            k[:, at_c + t * d:at_c + (t + 1) * d] = cos[t * P:(t + 1) * P].reshape(P, d)
            k[:, at_s + t * d:at_s + (t + 1) * d] = sin[t * P:(t + 1) * P].reshape(P, d)
    p = np.arange(P)
    k[:, K_POS:K_POS + 4] = np.stack([p + 1, P - p, P - 1 - p, p], 1)
    earlier = np.broadcast_to((np.arange(NE)[None, :] < np.arange(NE)[:, None]).reshape(1, -1), (P, NE * NE))
    lam = np.zeros((DEPTH, P, 2), np.float32)
    for layer in range(DEPTH):
        init = 0.8 - 0.6 * math.exp(-0.3 * layer)
        lam[layer] = [init, 1.0 - init]
    return k, np.ascontiguousarray(earlier.astype(np.float32)), lam


class PsumJobs:

    def __init__(self):
        self.number, self.taker, self.rank, self.order = {}, {}, {}, []
        self.taken = {"act": 0, "dve": 0}

    def add(self, key, taker):
        assert key not in self.number
        self.number[key] = len(self.order)
        self.order.append(key)
        self.taker[key] = taker
        self.taken[taker] += 1
        self.rank[key] = self.taken[taker]

    def filled(self, key):
        return self.number[key] + 1

    def bank(self, key):
        return self.number[key] % 8


def attention_maps():
    maps = {}
    for g, heads in (("ma", HALF), ("mb", HALF), ("g", G_HEADS), ("d", F_HEADS)):
        maps[g] = [(g, h, t) for h in range(heads) for t in range(T)]
    return maps


MAPS = attention_maps()


def plan_jobs():
    jobs = PsumJobs()
    for m in range(12):
        jobs.add(("mod", m), "dve")
    jobs.add(("modT",), "dve")
    for k in range(KD):
        jobs.add(("h1", k), "act")
    for s in SEGS:
        for t in range(T):
            jobs.add(("z", s, t), "act")
    for k in range(3):
        jobs.add(("cqT", k), "dve")
    for k in range(2):
        jobs.add(("ckvT", k), "dve")

    def softmax_maps(g):
        m = MAPS[g]
        for i in range(len(m) + 3):
            if i < len(m):
                jobs.add(("S",) + m[i], "act")
            if 2 <= i < len(m) + 2:
                jobs.add(("PT",) + m[i - 2], "act" if i % 2 else "dve")
            if i >= 3:
                jobs.add(("O",) + m[i - 3], "dve")

    for c, g in enumerate(("ma", "mb")):
        for t in range(T):
            jobs.add(("qm", c, t), "act")
        for kt in range(4):
            jobs.add(("kv", c, kt), "dve")
        for h in range(HALF):
            jobs.add(("mkT", c, h), "dve")
        for h in range(HALF):
            jobs.add(("mqT", c, h), "act")
        softmax_maps(g)
    for b in range(4):
        jobs.add(("gqT", b), "act")
    for b in range(2):
        jobs.add(("gkT", b), "dve")
    softmax_maps("g")
    for b in range(4):
        jobs.add(("dqT", b), "act")
    for b in range(4):
        jobs.add(("dkT", b), "dve")
    m = MAPS["d"]
    for i in range(len(m) + 2):
        if i < len(m):
            jobs.add(("S1",) + m[i], "act")
            jobs.add(("S2",) + m[i], "act")
        if 1 <= i < len(m) + 1:
            jobs.add(("PT",) + m[i - 1], "act")
        if i >= 2:
            jobs.add(("O",) + m[i - 2], "act")
    for b in range(2):
        jobs.add(("rqT", b), "act")
    for b in range(2):
        jobs.add(("rkT", b), "act")
    for h in range(R_HEADS):
        jobs.add(("qfbT", h), "act")
    for t in range(T):
        jobs.add(("KV", t), "dve")
    for t in range(T):
        for odd in range(2):
            jobs.add(("A", t, odd), "dve")
    for t in range(T):
        jobs.add(("R", t), "act")
    for n in range(NBR):
        for k in range(4):
            jobs.add(("oT", n, k), "dve")
        for c in range(2):
            for t in range(T):
                jobs.add(("gl", n, c, t), "act")
                jobs.add(("br", n, c, t), "dve")
    for k in range(KD):
        jobs.add(("mgT", k), "act" if k % 2 else "dve")
    for c in range(2):
        for t in range(T):
            jobs.add(("out", c, t), "act")
    for k in range(KD):
        jobs.add(("h2", k), "act")
    jobs.add(("route",), "act")
    jobs.add(("gu", "s", 0), "dve")
    for t in range(T):
        jobs.add(("gu", "s", t + 1) if t + 1 < T else ("gu", 0, 0), "dve")
        jobs.add(("aT", "s", t), "act")
        jobs.add(("y", "s", t, 0), "dve")
        jobs.add(("y", "s", t, 1), "dve")
    for e in range(2):
        for t in range(T):
            jobs.add(("gu", e, t + 1) if t + 1 < T else ("gu", e + 1, 0), "dve")
            jobs.add(("aT", e, t), "act")
            jobs.add(("y", e, t, 0), "dve")
            jobs.add(("y", e, t, 1), "dve")
    return jobs


JOBS = plan_jobs()
TURN_JOBS, TURN_ACT, TURN_DVE = 2 * T * 4, 2 * T, 2 * T * 3
assert TURN_JOBS % 8 == 0
TURNS = NE // 2

FILLS = ([("mod", m) for m in range(12)] + [("z", s) for s in SEGS] + [("uq",), ("ukv",)]
         + [f for n in range(NBR) for c in range(2) for f in (("gl", n, c), ("br", n, c))] + [("out", 0), ("out", 1)])
SLOTS = 3
SLOT = KD * C
FILL = {key: i for i, key in enumerate(FILLS)}


def last_user(key):
    if key[0] == "mod":
        return key
    return {"uq": ("qm", 1, T - 1), "ukv": ("kv", 1, 3)}.get(key[0], (*key, T - 1))


MAX_AT = {}
for _g in ("ma", "mb", "g", "d"):
    for _m in MAPS[_g]:
        for _key in ((("S1", *_m), ("S2", *_m)) if _g == "d" else (_m,)):
            MAX_AT[_key] = len(MAX_AT) + 1
GATES = [(n, c, t) for n in range(NBR) for c in range(2) for t in range(T)]
N_PARAMS = 21
LAST_DVE = JOBS.rank[("y", 1, T - 1, 1)] + (TURNS - 1) * TURN_DVE - 1
ESLOT = SLOTS * SLOT // 2


def trunk(nc, a):
    J = JOBS
    with ExitStack() as ctx:
        def sb(name, n, parts=P):
            return ctx.enter_context(nc.sbuf_tensor(name, [parts, n], F32))

        const = sb("const", K_N)
        x = sb("x", T * D)
        hT = sb("hT", KD * T * P)
        zf = sb("zf", 13824)
        W = sb("W", SLOTS * SLOT)
        silT = sb("silT", KD * 2)
        gains = sb("gains", GAINS)
        wr = sb("wr", KD * NE)
        brt = sb("brt", NE)
        gpre = sb("gpre", 2 * KD)
        modT = sb("modT", 4 * KD * 2)
        lamp = sb("lamp", 4 * HD)
        lamv = sb("lamv", 8)
        rdec = sb("rdec", 8)
        small = sb("small", 64)
        mu = sb("mu", 12)
        rrec = sb("rrec", 8)
        grow = sb("grow", 40)
        stat = sb("stat", 36)
        rs = sb("rs", 36)
        dec = sb("dec", 32)
        km = sb("km", 4 * HALF * M_HD)
        qm = sb("qm", T * HALF * M_HD)
        vm = sb("vm", 4 * M_HEADS * M_V)
        qT = sb("qT", 2 * 4 * T * P)
        kT = sb("kT", 2 * 4 * 4 * P)
        Pb = sb("Pb", 3 * T * P)
        PTb = sb("PTb", 2 * T * P)
        nmax = sb("nmax", 4)
        rsum = sb("rsum", 8)
        c_ckv = sb("c_ckv", KV_LORA)
        c_kpe = sb("c_kpe", M_ROPE)
        c_gk = sb("c_gk", G_KV * HD)
        c_gv = sb("c_gv", G_KV * HD)
        c_dk = sb("c_dk", 2 * F_HEADS * HD)
        c_dv = sb("c_dv", F_HEADS * F_DV)
        state0 = sb("state0", R_HEADS * R_DV)
        kdup = sb("kdup", 4 * G_KV * 2 * HD)
        rtmp = sb("rtmp", (G_HEADS + G_KV) * HD)
        psum = ctx.enter_context(nc.psum_tensor("psum", [P, 8, C], F32))

        names = ["psum_filled", "act_emptied", "dve_emptied", "params_in", "bmod_in", 
                 "x_squared", "var_ready", "head_rs", "earlier_in", "root_ready", "xn_ready", "modT_ready", 
                 "gp_ready", "dve_link", "act_link", "pool_link", "cq_ready", "ckv_ready",
                 "gqa_ready", "kdup_ready", "diff_roped", "qm_roped", "km_ready", "max_ready",
                 "pd_ready", "lam_ready", "absx_ready", "expx_ready", "u_ready", "ln_ready", "lg_ready",
                 "dec_ready", "qkfb_ready", "masks_raw", "mask_ready", "state_ready", "state_out", "ro_ready",
                 "do_ready", "gate_ready", "merged_ready", "m_squared", "x_ready", "comb_ready", "silu_ready",
                 "lam_dots", "lam_exps", "head_normed"]
        landed_names = [f"w_landed{i}" for i in range(SLOTS)] + ["e_landed0", "e_landed1"]
        sems = [nc.alloc_semaphore(n) for n in names + landed_names]
        S = dict(zip(names + landed_names, sems))
        POOL_COUNTS = {"gates_out": 2 * 16, "gates_in": 6 * 16, "cache_out": 8 * 16}
        for n in POOL_COUNTS:
            S[n] = nc.alloc_semaphore(n)
        const_in = nc.alloc_semaphore("const_in")
        silc_in = nc.alloc_semaphore("silc_in")
        silc_ready = nc.alloc_semaphore("silc_ready")
        y_out = nc.alloc_semaphore("y_out")

        def cview(at, n):
            return const[:, at:at + n]

        ident = cview(K_ID, P)
        xv = x[:, :].rearrange("p (t n) -> p t n", t=T)
        hTv = hT[:, :].rearrange("p (k n) -> p k n", k=KD)
        z = zf[:, 0:T * ZC].rearrange("p (t n) -> p t n", t=T)
        modrow = zf[0:2, 0:6 * D]
        xn = zf[:, 6 * D:9 * D].rearrange("p (t n) -> p t n", t=T)
        junk = zf[:, 9 * D:12 * D].rearrange("p (t n) -> p t n", t=T)
        silTv = silT[:, :].rearrange("p (k v) -> p k v", v=2)
        modTv = modT[:, :].rearrange("p (q k v) -> p q k v", q=4, v=2)
        qmv = qm[:, :].rearrange("p (t h d) -> p t h d", t=T, h=HALF)
        kmv = km[:, :].rearrange("p (t h d) -> p t h d", t=4, h=HALF)
        vmv = vm[:, :].rearrange("p (t h d) -> p t h d", t=4, h=M_HEADS)
        qTv = qT[:, :].rearrange("p (s b n) -> p s b n", s=2, b=4)
        kTv = kT[:, :].rearrange("p (s b n) -> p s b n", s=2, b=4)
        rsv = rs[:, :].rearrange("p (t n) -> p t n", t=T)
        statv = stat[:, :].rearrange("p (t n) -> p t n", t=T)
        kdv = kdup[:, :].rearrange("p (t k c d) -> p t k c d", t=4, k=G_KV, c=2)
        cqT = kT[:, 2048:2048 + 3 * T * P].rearrange("p (k n) -> p k n", k=3)
        ckvT = qT[:, 1536:1536 + 2 * 4 * P].rearrange("p (k n) -> p k n", k=2)
        qfb = vm[:, 0:T * R_HEADS * 2 * R_DK].rearrange("p (t h f d) -> p t h f d", t=T, h=R_HEADS, f=2)
        kfb = km[:, :].rearrange("p (t h f d) -> p t h f d", t=T, h=R_HEADS, f=2)
        qfbT = kTv[:, 0].rearrange("p b n -> p (b n)")[:, 0:4 * T * P].rearrange("p (h n) -> p h n", h=4)
        state1 = kTv[:, 0].rearrange("p b n -> p (b n)")[:, 1536:2048].rearrange("p (h v) -> p h v", h=R_HEADS)
        state2 = vm[:, 1536:2048].rearrange("p (h v) -> p h v", h=R_HEADS)
        state0v = state0[:, :].rearrange("p (h v) -> p h v", h=R_HEADS)
        state_ctx = c_dk
        mask = kdup[:, 0:512].rearrange("p (h n) -> p h n", h=R_HEADS)
        AT = [r.rearrange("p (h n) -> p h n", h=R_HEADS) for r in (PTb[:, 0:512], Pb[:, 0:512], Pb[:, 512:1024])]
        maskb = kdup[:, 512:1024].rearrange("p (h n) -> p h n", h=R_HEADS)
        oT = qTv[:, 0]
        gs = [kTv[:, 0, 0], kTv[:, 0, 1]]
        gtmp = kTv[:, 0, 2]
        gp = kT[:, 0:2 * D].rearrange("p (v n) -> p v n", v=2)
        gpost = kT[:, 2 * D:3 * D]
        merged = z[:, :, Z_MERGED:Z_MERGED + D]
        m_row = z[:, :, Z_M:Z_M + D]
        acc = zf[:, 0:3 * D].rearrange("p (t n) -> p t n", t=T)
        xn2 = zf[:, 3 * D:6 * D].rearrange("p (t n) -> p t n", t=T)
        av = zf[:, 6144:6656].rearrange("p (s n) -> p s n", s=2)
        silu = zf[:, 6656:7168].rearrange("p (s n) -> p s n", s=2)
        aT = zf[:, 7168:7680].rearrange("p (s f n) -> p s f n", s=2, f=2)
        cmp1 = zf[:, 7680:10752].rearrange("p (t i j) -> p t i j", t=T, i=NE)
        cmp2 = zf[:, 10752:13824].rearrange("p (t i j) -> p t i j", t=T, i=NE)
        cmpj = zf[:, 7680:10752].rearrange("p (t n) -> p t n", t=T)
        earlier = vm[:, 0:RANK_COLS]
        before = earlier.rearrange("p (i j) -> p i j", i=NE)
        rt = Pb[:, :].rearrange("p (s t e) -> p s t e", s=12, t=T)
        R_EXP, R_SC, R_SEL, R_RANK, R_COMB, R_MSEL, R_TOP, R_GRP = range(8)

        def slot(i):
            return W[:, (i % SLOTS) * SLOT:(i % SLOTS + 1) * SLOT]

        def weights(key, k, n):
            return slot(FILL[key])[:, 0:k * n].rearrange("p (k n) -> p k n", k=k)

        def expert_gu(s):
            return W[:, s * ESLOT:s * ESLOT + SLOT].rearrange("p (k n) -> p k n", k=KD)

        def expert_dn(s):
            return W[:, s * ESLOT + SLOT:(s + 1) * ESLOT].rearrange("p (k n) -> p k n", k=2)

        def landed(key):
            i = FILL[key]
            return S[f"w_landed{i % SLOTS}"], 16 * (i // SLOTS + 1)

        def filled(key):
            return S["psum_filled"], J.filled(key)

        def emptied(key):
            return S["act_emptied" if J.taker[key] == "act" else "dve_emptied"], J.rank[key]

        def bank(key, n=C, parts=slice(0, P)):
            return psum[parts, J.bank(key), 0:n]

        def rows(ap, l):
            r = ap[bass.ds(l, 1)]
            n = len(ap.shape)
            if n == 2:
                return r.rearrange("o n -> (o n)")
            return r.rearrange("o a b -> (o a) b") if n == 3 else r.rearrange("o a b c -> (o a) b c")

        def spread(ap1):
            return ap1.partition_broadcast(P)

        def linker(eng, sem):
            n = [0]

            def link(ins):
                n[0] += 1
                ins.then_inc(sem, 1)
                eng.wait_ge(sem, n[0])
            return link

        def rope(eng, link, t, v, tmp, heads, d, at_c, at_s):
            q = d // 4
            cos = cview(at_c + (t - 1) * d, d)
            sin = cview(at_s + (t - 1) * d, d).rearrange("p (a j i) -> p a j i", a=2, j=2)
            v4 = v.rearrange("p h (a j i) -> p h a j i", a=2, j=2)
            tm = tmp[:, 0:heads * d].rearrange("p (h d) -> p h d", d=d)
            t4 = tm.rearrange("p h (a j i) -> p h a j i", a=2, j=2)
            for j in range(2):
                ins = eng.tensor_tensor(t4[:, :, :, j, :], v4[:, :, :, 1 - j, :],
                                        sin[:, None, :, j, :].to_broadcast([P, heads, 2, q]), ALU.mult)
            link(ins)
            link(eng.tensor_tensor(v, v, cos[:, None, :].to_broadcast([P, heads, d]), ALU.mult))
            return eng.tensor_tensor(v, v, tm, ALU.add)

        def tile_rows(cache, col, n, kt):
            return cache[:, 0:n] if kt == 1 else z[:, (0, None, 1, 2)[kt], col:col + n]

        def keys_of(t):
            return (0,) if t == 0 else (1, 2, 3)

        def queries(g, h, t):
            if g in ("ma", "mb"):
                return qTv[0:M_HD, 0 if g == "ma" else 1, h, t * P:(t + 1) * P]
            return qTv[64 * (h % 2):64 * (h % 2) + 64, 0, h // 2, t * P:(t + 1) * P]

        def keys(g, h, t):
            cols = slice(0, P) if t == 0 else slice(P, 4 * P)
            if g in ("ma", "mb"):
                return kTv[0:M_HD, 0 if g == "ma" else 1, h, cols]
            return kTv[64 * (h % 2):64 * (h % 2) + 64, 0, h // (G_HEADS // G_KV), cols]

        def values(g, h, kt):
            if g in ("ma", "mb"):
                return vmv[:, kt, h + (HALF if g == "mb" else 0), :]
            if g == "g":
                return tile_rows(c_gv, Z_GV, P, kt)[:, HD * (h // 4):HD * (h // 4) + HD]
            return tile_rows(c_dv, Z_DV, 4 * P, kt)[:, F_DV * h:F_DV * (h + 1)]

        def out_cols(g, h, t):
            if g in ("ma", "mb"):
                h = h + (HALF if g == "mb" else 0)
                return z[:, t, Z_CQ + M_V * h:Z_CQ + M_V * (h + 1)]
            if g == "g":
                return z[:, t, Z_GQ + HD * h:Z_GQ + HD * (h + 1)]
            return z[:, t, Z_DQ + F_DV * h:Z_DQ + F_DV * (h + 1)]

        with nc.Block() as block:
            @block.sync
            def _(sp):
                sp.dma_start(const[:, :], a["consts"]).then_inc(const_in, 16)
                sp.dma_start(xv[:, 0, :], a["x_prompt"][0]).then_inc(const_in, 16)
                sp.dma_start(xv[:, 1:3, :], a["x_sample"][0].rearrange("(t p) n -> p t n", p=P)).then_inc(const_in, 16)
                sp.dma_start(silTv[:, :, 0], a["c_ctx"].rearrange("(k p) -> p k", p=P), allow_slow_non_contiguous=True).then_inc(silc_in, 16)
                sp.dma_start(silTv[:, :, 1], a["c"][0].rearrange("(k p) -> p k", p=P), allow_slow_non_contiguous=True).then_inc(silc_in, 16)
                sp.wait_ge(const_in, 48)

            @block.scalar
            def _(act):
                act.wait_ge(silc_in, 32)
                nc.scalar.activation(silT[:, :], silT[:, :], ACT.Silu).then_inc(silc_ready, 1)
                act.wait_ge(silc_ready, 1)

        with nc.Fori(0, DEPTH) as l:
            with nc.Block() as block:
                @block.sync
                def _(sp):
                    def source(key):
                        kind = key[0]
                        if kind == "mod":
                            return rows(a["w_mod"], l)[:, key[1] * C:(key[1] + 1) * C], KD, C
                        if kind == "z":
                            at, n = SEG[key[1]]
                            return rows(a["w_in"], l)[:, at:at + n], KD, n
                        if kind == "gl":
                            at = ZC + key[1] * D + key[2] * C
                            return rows(a["w_in"], l)[:, at:at + C], KD, C
                        if kind == "uq":
                            return rows(a["w_mla_uq"], l), 3, M_HEADS * M_HD
                        if kind == "ukv":
                            return rows(a["w_mla_ukv"], l), 2, D
                        if kind == "br":
                            return rows(a["w_br"], l)[key[1]][:, key[2] * C:(key[2] + 1) * C], 4, C
                        return rows(a["w_out"], l)[:, key[1] * C:(key[1] + 1) * C], KD, C

                    for i, key in enumerate(FILLS):
                        src, k, n = source(key)
                        if i >= SLOTS:
                            sp.wait_ge(*filled(last_user(FILLS[i - SLOTS])))
                        sp.dma_start(weights(key, k, n), src.rearrange("(k p) n -> p k n", p=P)).then_inc(landed(key)[0], 16)

                    def load_expert(s, gu, dn):
                        sp.dma_start(expert_gu(s), gu.rearrange("(k p) n -> p k n", p=P)).then_inc(S[f"e_landed{s}"], 16)
                        sp.dma_start(expert_dn(s), dn.rearrange("(k p) n -> p k n", p=P)).then_inc(S[f"e_landed{s}"], 16)

                    def expert(e):
                        gu = a["w_exp_gu"].rearrange("l e d n -> (l e) d n")[bass.ds(l * NE + e, 1)].rearrange("o d n -> (o d) n")
                        dn = a["w_exp_down"].rearrange("l e f d -> (l e) f d")[bass.ds(l * NE + e, 1)].rearrange("o f d -> (o f) d")
                        return gu, dn

                    sp.wait_ge(*filled(("out", 1, T - 1)))
                    load_expert(1, rows(a["w_sh_gu"], l), rows(a["w_sh_down"], l))
                    load_expert(0, *expert(0))
                    sp.wait_ge(*filled(("y", "s", T - 1, 1)))
                    load_expert(1, *expert(1))
                    with sp.Fori(0, TURNS - 1) as turn:
                        for e in range(2):
                            sp.wait_ge(S["psum_filled"], turn * TURN_JOBS + J.filled(("y", e, T - 1, 1)))
                            load_expert(e, *expert(turn * 2 + e + 2))

                @block.gpsimd
                def _(pool):
                    link = linker(pool, S["pool_link"])
                    out = a["outs"]

                    def row(name):
                        r = out[name][0][bass.ds(l, 1)]
                        return r.rearrange({3: "o s n -> (o s) n", 4: "o s k d -> (o s) (k d)",
                                            5: "o s h c d -> (o s) (h c d)"}[len(r.shape)])

                    pool.wait_ge(*emptied(("mod", 11)))
                    for n, at in enumerate((2 * D, 5 * D)):
                        pool.dma_start(a["gate_rows"][n], modrow[:, at:at + D]).then_inc(S["gates_out"], 16)
                    pool.wait_ge(*emptied(("z", "gkv", 0)))
                    pool.dma_start(row("mla_kpe"), z[:, 0, Z_KPE:Z_KPE + M_ROPE]).then_inc(S["cache_out"], 16)
                    pool.dma_start(row("gqa_v"), z[:, 0, Z_GV:Z_GV + P]).then_inc(S["cache_out"], 16)
                    pool.wait_ge(*emptied(("z", "dv", T - 1)))
                    pool.dma_start(row("diff_k"), z[:, 0, Z_DK:Z_DK + 512]).then_inc(S["cache_out"], 16)
                    pool.dma_start(row("diff_v"), z[:, 0, Z_DV:Z_DV + 512]).then_inc(S["cache_out"], 16)
                    heads = G_HEADS + G_KV
                    pool.wait_ge(S["head_rs"], 1)
                    qk = z[:, :, Z_GQ:Z_GQ + heads * HD].rearrange("p t (h d) -> p t h d", d=HD)
                    link(nc.gpsimd.tensor_tensor(qk, qk, rsv[:, :, 2:2 + heads, None].to_broadcast([P, T, heads, HD]), ALU.mult))
                    for g, h0, h1 in (("gq", 0, G_HEADS), ("gk", G_HEADS, heads)):
                        gain = gains[:, None, None, GAIN[g]].to_broadcast([P, T, h1 - h0, HD])
                        link(nc.gpsimd.tensor_tensor(qk[:, :, h0:h1], qk[:, :, h0:h1], gain, ALU.mult))
                    pool.wait_ge(S["ckv_ready"], 1)
                    pool.dma_start(row("mla_ckv"), z[:, 0, Z_CKV:Z_CKV + KV_LORA]).then_inc(S["cache_out"], 16)
                    pool.dma_start(row("gqa_k"), z[:, 0, Z_GK:Z_GK + P]).then_inc(S["cache_out"], 16)
                    for t in (1, 2):
                        link(rope(nc.gpsimd, link, t, qk[:, t], rtmp[:, :], heads, HD, K_C64, K_S64))
                    for kt in range(4):
                        src = tile_rows(c_gk, Z_GK, G_KV * HD, kt).rearrange("p (k d) -> p k d", d=HD)
                        if kt == 1:
                            pool.wait_ge(S["params_in"], 16 * N_PARAMS)
                        for c in range(2):
                            ins = nc.gpsimd.tensor_copy(kdv[:, kt, :, c, :], src)
                    ins.then_inc(S["kdup_ready"], 1)
                    for t in (1, 2):
                        for at in (Z_DQ, Z_DK):
                            ins = rope(nc.gpsimd, link, t, z[:, t, at:at + 512].rearrange("p (h d) -> p h d", d=HD), rtmp[:, :],
                                       2 * F_HEADS, HD, K_C64, K_S64)
                            if (t, at) != (2, Z_DK):
                                link(ins)
                    ins.then_inc(S["diff_roped"], 1)
                    pool.wait_ge(*emptied(("KV", 0)))
                    for r in range(2):
                        so = out["state_ret"][0][bass.ds(l, 1)].rearrange("o r h k v -> (o r) k h v")[r]
                        pool.dma_start(so, state_ctx[64 * r:64 * r + 64, :].rearrange("p (h v) -> p h v", h=R_HEADS)
                                       ).then_inc(S["cache_out"], 16)
                    for n in range(2):
                        pool.wait_ge(*filled(("mgT", 0) if n == 0 else ("gu", "s", 0)))
                        for v in range(2):
                            pool.dma_start(gp[:, v, :], spread(a["gate_rows"][n, v])).then_inc(S["gates_in"], 16)
                        pool.dma_start(gpost, spread(rows(a["g_post1" if n == 0 else "g_post2"], l))).then_inc(S["gates_in"], 16)
                    pool.wait_ge(S["cache_out"], l * POOL_COUNTS["cache_out"] + 16 * 8)

                @block.scalar
                def _(act):
                    link = linker(act, S["act_link"])

                    def dma(dst, src, sem="params_in", scattered=False):
                        act.dma_start(dst, src, allow_slow_non_contiguous=scattered).then_inc(S[sem], 16)

                    dma(modrow, rows(a["b_mod"], l).partition_broadcast(2), "bmod_in")
                    for n, name in enumerate(("g_pre1", "g_pre2")):
                        dma(gpre[:, n * KD:(n + 1) * KD], rows(a[name], l).rearrange("(k p) -> p k", p=P), scattered=True)
                    for g, name in (("q", "g_mla_q"), ("kv", "g_mla_kv"), ("gq", "g_gqa_q"), ("gk", "g_gqa_k"),
                                    ("ret", "g_ret"), ("diff", "g_diff")):
                        dma(gains[:, GAIN[g]], spread(rows(a[name], l)))
                    dma(lamp[:, :], spread(rows(a["diff_lambda"], l).rearrange("a b -> (a b)")))
                    dma(lamv[:, 6:8], rows(a["lam_init"], l))
                    dma(rdec[:, :], spread(rows(a["ret_decay"], l).rearrange("a b -> (a b)")))
                    dma(brt[:, :], spread(rows(a["b_router"], l)))
                    dma(wr[:, :].rearrange("p (k n) -> p k n", k=KD), rows(a["w_router"], l).rearrange("(k p) n -> p k n", p=P))
                    for buf, name in ((c_ckv, "cache_mla_ckv"), (c_kpe, "cache_mla_kpe"), (c_gk, "cache_gqa_k"),
                                      (c_gv, "cache_gqa_v"), (c_dk, "cache_diff_k"), (c_dv, "cache_diff_v")):
                        src = a[name][0][bass.ds(l, 1)]
                        src = src.rearrange({3: "o s n -> (o s) n", 4: "o s k d -> (o s) (k d)",
                                             5: "o s h c d -> (o s) (h c d)"}[len(a[name].shape) - 1])
                        dma(buf[:, :], src)
                    for r in range(2):
                        src = a["state_ret"][0][bass.ds(l, 1)].rearrange("o r h k v -> (o r) k h v")[r]
                        dma(state0v[64 * r:64 * r + 64], src)

                    def square_rows(v, junk_rows, sem):
                        for t in range(T):
                            nc.scalar.activation(junk_rows[:, t], v[:, t], ACT.Square,
                                                 accum_out=stat[:, t:t + 1]).then_inc(S[sem], 1)

                    def root(n, site):
                        act.wait_ge(S["var_ready"], site + 1)
                        nc.scalar.activation(rs[:, 0:n], stat[:, 0:n], ACT.Sqrt).then_inc(S["root_ready"], 1)

                    square_rows(xv, junk, "x_squared")
                    root(T, 0)

                    def modulated(name, n):
                        for k in range(KD):
                            act.wait_ge(*filled((name, k)))
                            for v, cols in ((0, slice(0, P)), (1, slice(P, T * P))):
                                ins = nc.scalar.activation(hTv[:, k, cols], psum[:, J.bank((name, k)), cols], ACT.Identity,
                                                           scale=modTv[:, 2 * n + 1, k, v:v + 1], bias=modTv[:, 2 * n, k, v:v + 1])
                            ins.then_inc(S["act_emptied"], 1)

                    act.wait_ge(S["modT_ready"], 1)
                    modulated("h1", 0)

                    act.wait_ge(S["gates_out"], l * POOL_COUNTS["gates_out"] + 32)
                    for s in SEGS:
                        at, n = SEG[s]
                        for t in range(T):
                            act.wait_ge(*filled(("z", s, t)))
                            nc.scalar.activation(z[:, t, at:at + n], bank(("z", s, t), n),
                                                 ACT.Silu if s == "rg" else ACT.Copy).then_inc(S["act_emptied"], 1)
                    act.wait_ge(S["absx_ready"], 1)
                    nc.scalar.activation(small[:, 8:16], small[:, 0:8], ACT.Exp, scale=-1.0).then_inc(S["expx_ready"], 1)
                    act.wait_ge(S["u_ready"], 1)
                    nc.scalar.activation(small[:, 24:32], small[:, 16:24], ACT.Ln).then_inc(S["ln_ready"], 1)
                    act.wait_ge(S["lg_ready"], 1)
                    for q in range(4):
                        f = q % 2
                        nc.scalar.activation(dec[:, 4 * q:4 * q + 4], small[:, 32 + 4 * f:36 + 4 * f], ACT.Exp,
                                             scale=const[:, K_POS + q:K_POS + q + 1])
                    for f in range(2):
                        ins = nc.scalar.activation(dec[64 * f:64 * f + 64, 16:20], small[64 * f:64 * f + 64, 32 + 4 * f:36 + 4 * f],
                                                   ACT.Exp, scale=float(P))
                    ins.then_inc(S["dec_ready"], 1)
                    act.wait_ge(S["lam_dots"], 1)
                    nc.scalar.activation(lamv[:, 2:4], lamv[:, 0:2], ACT.Exp).then_inc(S["lam_exps"], 1)
                    root(36, 1)

                    def softmax_maps(g):
                        m = MAPS[g]
                        for i in range(len(m) + 3):
                            if i < len(m):
                                key = m[i]
                                n = P * len(keys_of(key[2]))
                                act.wait_ge(S["max_ready"], MAX_AT[key])
                                if i >= 3:
                                    act.wait_ge(*filled(("PT",) + m[i - 3]))
                                if i >= 4:
                                    act.wait_ge(*emptied(("O",) + m[i - 4]))
                                nc.scalar.activation(Pb[:, (i % 3) * 384:(i % 3) * 384 + n], bank(("S",) + key, n), ACT.Exp,
                                                     bias=nmax[:, i % 4:i % 4 + 1], scale=1.0,
                                                     accum_out=rsum[:, i % 4:i % 4 + 1]).then_inc(S["act_emptied"], 1)
                            if 2 <= i < len(m) + 2 and J.taker[("PT",) + m[i - 2]] == "act":
                                empty_turned(i - 2, m)

                    def empty_turned(i, m):
                        key = ("PT",) + m[i]
                        n = P * len(keys_of(m[i][2]))
                        act.wait_ge(*filled(key))
                        if i >= 2:
                            act.wait_ge(*filled(("O",) + m[i - 2]))
                        nc.scalar.activation(PTb[:, (i % 2) * 384:(i % 2) * 384 + n], bank(key, n),
                                             ACT.Copy).then_inc(S["act_emptied"], 1)

                    for c, g in enumerate(("ma", "mb")):
                        for t in range(T):
                            act.wait_ge(*filled(("qm", c, t)))
                            if c == 1:
                                act.wait_ge(*filled(("mqT", 0, HALF - 1)))
                            nc.scalar.activation(qmv[:, t], bank(("qm", c, t), 384).rearrange("p (h d) -> p h d", h=HALF),
                                                 ACT.Copy).then_inc(S["act_emptied"], 1)
                        for h in range(HALF):
                            act.wait_ge(*filled(("mqT", c, h)))
                            if c == 1:
                                act.wait_ge(*filled(("kv", 1, 3)))
                            nc.scalar.activation(qTv[0:M_HD, c, h, :], bank(("mqT", c, h), 384, slice(0, M_HD)), ACT.Copy,
                                                 scale=M_HD ** -0.5).then_inc(S["act_emptied"], 1)
                        softmax_maps(g)
                    for b in range(4):
                        act.wait_ge(*filled(("gqT", b)))
                        nc.scalar.activation(qTv[:, 0, b, :], bank(("gqT", b), 384), ACT.Copy,
                                             scale=HD ** -0.5).then_inc(S["act_emptied"], 1)
                    softmax_maps("g")
                    act.wait_ge(*filled(("gkT", 1)))
                    for h in range(R_HEADS):
                        nc.scalar.activation(mask[:, h], cview(K_DF, P), ACT.Exp, scale=small[:, 32 + h:33 + h])
                        ins = nc.scalar.activation(maskb[:, h], cview(K_DB, P), ACT.Exp, scale=small[:, 36 + h:37 + h])
                    ins.then_inc(S["masks_raw"], 1)
                    for b in range(4):
                        act.wait_ge(*filled(("dqT", b)))
                        nc.scalar.activation(qTv[:, 1, b, :], bank(("dqT", b), 384), ACT.Copy,
                                             scale=HD ** -0.5).then_inc(S["act_emptied"], 1)
                    m = MAPS["d"]
                    for i in range(len(m) + 2):
                        if i < len(m):
                            n = P * len(keys_of(m[i][2]))
                            for w in range(2):
                                s = (i % 2, 2)[w]
                                r = 2 * (i % 2) + w
                                act.wait_ge(S["max_ready"], MAX_AT[("S1", "S2")[w], *m[i]])
                                if w == 0 and i >= 2:
                                    act.wait_ge(*filled(("PT",) + m[i - 2]))
                                if w == 1 and i >= 1:
                                    act.wait_ge(S["pd_ready"], i)
                                nc.scalar.activation(Pb[:, s * 384:s * 384 + n], bank((("S1", "S2")[w],) + m[i], n), ACT.Exp,
                                                     bias=nmax[:, r:r + 1], scale=1.0,
                                                     accum_out=rsum[:, r:r + 1]).then_inc(S["act_emptied"], 1)
                        if 1 <= i < len(m) + 1:
                            empty_turned(i - 1, m)
                        if i >= 2:
                            key = m[i - 2]
                            act.wait_ge(*filled(("O",) + key))
                            nc.scalar.activation(out_cols(*key), bank(("O",) + key, F_DV), ACT.Copy).then_inc(S["act_emptied"], 1)
                    for b in range(2):
                        act.wait_ge(*filled(("rqT", b)))
                        nc.scalar.activation(qTv[:, 0, b, :], bank(("rqT", b), 384), ACT.Copy).then_inc(S["act_emptied"], 1)
                    for b in range(2):
                        act.wait_ge(*filled(("rkT", b)))
                        nc.scalar.activation(qTv[:, 0, 2 + b, :], bank(("rkT", b), 384), ACT.Copy).then_inc(S["act_emptied"], 1)
                    for h in range(R_HEADS):
                        act.wait_ge(*filled(("qfbT", h)))
                        nc.scalar.activation(qfbT[:, h, :], bank(("qfbT", h), 384), ACT.Copy).then_inc(S["act_emptied"], 1)
                    for t in range(T):
                        act.wait_ge(*filled(("R", t)))
                        nc.scalar.activation(z[:, t, Z_RQ:Z_RQ + 512], bank(("R", t)), ACT.Copy).then_inc(S["act_emptied"], 1)
                    dma(earlier, a["earlier"], "earlier_in")
                    root(24, 2)
                    for n in range(NBR):
                        for c in range(2):
                            for t in range(T):
                                i = (n * 2 + c) * T + t
                                act.wait_ge(*filled(("gl", n, c, t)))
                                if i >= 2:
                                    act.wait_ge(S["dve_emptied"], J.rank[("br", *GATES[i - 2])])
                                if i < 2:
                                    act.wait_ge(S["head_normed"], 1)
                                nc.scalar.activation(gs[i % 2], bank(("gl", n, c, t)), ACT.Sigmoid).then_inc(S["act_emptied"], 1)
                    for k in range(1, KD, 2):
                        act.wait_ge(*filled(("mgT", k)))
                        nc.scalar.activation(hTv[:, k, :], bank(("mgT", k), 384), ACT.Copy).then_inc(S["act_emptied"], 1)
                    for c in range(2):
                        for t in range(T):
                            act.wait_ge(*filled(("out", c, t)))
                            nc.scalar.activation(m_row[:, t, c * C:(c + 1) * C], bank(("out", c, t)), ACT.Copy).then_inc(S["act_emptied"], 1)
                    act.wait_ge(*emptied(("out", 1, T - 1)))
                    square_rows(m_row, merged, "x_squared")
                    root(T, 3)
                    act.wait_ge(S["x_ready"], 1)
                    square_rows(xv, cmpj, "x_squared")
                    root(T, 4)
                    modulated("h2", 1)
                    act.wait_ge(*filled(("route",)))
                    nc.scalar.activation(rt[:, R_EXP], bank(("route",), T * NE).rearrange("p (t e) -> p t e", t=T), ACT.Exp,
                                         scale=-1.0).then_inc(S["act_emptied"], 1)

                    def silu_of(key, u, more=0):
                        act.wait_ge(S["psum_filled"], more + J.filled(key))
                        nc.scalar.activation(silu[:, u % 2, :], bank(key, FF), ACT.Silu).then_inc(S["silu_ready"], 1)

                    def turned_of(key, u, more=0):
                        act.wait_ge(S["psum_filled"], more + J.filled(key))
                        nc.scalar.activation(aT[:, u % 2].rearrange("p f n -> p (f n)"), bank(key, FF), ACT.Copy).then_inc(S["act_emptied"], 1)

                    silu_of(("gu", "s", 0), 0)
                    for t in range(T):
                        silu_of(("gu", "s", t + 1) if t + 1 < T else ("gu", 0, 0), t + 1)
                        turned_of(("aT", "s", t), t)

                    def two_experts(more, last=False):
                        for e in range(2):
                            for t in range(T):
                                u = T + e * T + t
                                no_next = last and u == 3 * T - 1
                                if not no_next:
                                    silu_of(("gu", e, t + 1) if t + 1 < T else ("gu", e + 1, 0), u + 1, more)
                                turned_of(("aT", e, t), u, more - 1 if no_next else more)

                    with act.Fori(0, TURNS - 1) as turn:
                        two_experts(turn * TURN_JOBS)
                    two_experts((TURNS - 1) * TURN_JOBS, last=True)
                    act.wait_ge(S["dve_emptied"], LAST_DVE)
                    square_rows(acc, cmpj, "x_squared")
                    root(T, 5)

                @block.vector
                def _(dve):
                    V = nc.vector
                    link = linker(dve, S["dve_link"])

                    def variance(at, n, count, site):
                        V.tensor_scalar(stat[:, at:at + n], stat[:, at:at + n], 1.0 / count, EPS, ALU.mult,
                                        ALU.add).then_inc(S["var_ready"], 1)
                        one_over_root(n, site)

                    def one_over_root(n, site):
                        dve.wait_ge(S["root_ready"], site + 1)
                        link(V.reciprocal(rs[:, 0:n], rs[:, 0:n]))

                    def empty(key, dst, src):
                        dve.wait_ge(*filled(key))
                        V.tensor_copy(dst, src).then_inc(S["dve_emptied"], 1)

                    dve.wait_ge(S["x_squared"], T)
                    variance(0, T, D, 0)
                    for t in range(T):
                        ins = V.tensor_scalar(xn[:, t], xv[:, t], rs[:, t:t + 1], None, ALU.mult)
                    ins.then_inc(S["xn_ready"], 1)
                    dve.wait_ge(S["bmod_in"], 16)
                    for m in range(12):
                        dve.wait_ge(*filled(("mod", m)))
                        cols = modrow[:, m * C:(m + 1) * C]
                        V.tensor_tensor(cols, cols, bank(("mod", m), C, slice(0, 2)), ALU.add).then_inc(S["dve_emptied"], 1)
                    empty(("modT",), modT[:, :], bank(("modT",), 4 * KD * 2))
                    dve.wait_ge(*emptied(("modT",)))
                    dve.wait_ge(S["params_in"], 16 * N_PARAMS)
                    for n in range(2):
                        g = gpre[:, n * KD:(n + 1) * KD, None].to_broadcast([P, KD, 2])
                        ins = V.scalar_tensor_tensor(modTv[:, 2 * n + 1], modTv[:, 2 * n + 1], 1.0, g, ALU.add, ALU.mult)
                    ins.then_inc(S["modT_ready"], 1)
                    V.scalar_tensor_tensor(small[:, 0:8], rdec[:, :], -1.0, rdec[:, :], ALU.mult, ALU.max).then_inc(S["absx_ready"], 1)
                    dve.wait_ge(S["expx_ready"], 1)
                    V.tensor_scalar(small[:, 16:24], small[:, 8:16], 1.0, None, ALU.add).then_inc(S["u_ready"], 1)
                    dve.wait_ge(S["u_ready"], 1)
                    link(V.scalar_tensor_tensor(small[:, 40:48], small[:, 16:24], -1.0, small[:, 8:16], ALU.add, ALU.subtract))
                    link(V.reciprocal(small[:, 48:56], small[:, 16:24]))
                    link(V.scalar_tensor_tensor(small[:, 40:48], small[:, 40:48], -1.0, small[:, 48:56], ALU.mult, ALU.mult))
                    dve.wait_ge(S["ln_ready"], 1)
                    link(V.tensor_tensor(small[:, 40:48], small[:, 40:48], small[:, 24:32], ALU.add))
                    V.scalar_tensor_tensor(small[:, 32:40], rdec[:, :], 0.0, small[:, 40:48], ALU.min, ALU.subtract).then_inc(S["lg_ready"], 1)
                    lp = lamp[:, :].rearrange("p (q c d) -> p q c d", q=2, c=2)
                    link(V.tensor_tensor(lp[:, :, 0], lp[:, :, 0], lp[:, :, 1], ALU.mult))
                    V.tensor_reduce(lamv[:, 0:2], lp[:, :, 0], AX, ALU.add).then_inc(S["lam_dots"], 1)
                    dve.wait_ge(S["lam_exps"], 1)
                    link(V.tensor_tensor(lamv[:, 4:5], lamv[:, 2:3], lamv[:, 3:4], ALU.subtract))
                    link(V.tensor_tensor(lamv[:, 4:5], lamv[:, 4:5], lamv[:, 6:7], ALU.add))
                    link(V.tensor_scalar(lamv[:, 5:6], lamv[:, 4:5], -1.0, None, ALU.mult))
                    link(V.tensor_scalar(gains[:, GAIN["diff"]], gains[:, GAIN["diff"]], lamv[:, 7:8], None, ALU.mult))
                    dve.wait_ge(S["dec_ready"], 1)
                    link(V.tensor_scalar(dec[:, 8:16], dec[:, 8:16], R_DK ** -0.5, None, ALU.mult))

                    dve.wait_ge(*emptied(("z", "gkv", T - 1)))
                    for t in range(T):
                        for c, (at, n) in enumerate(((Z_CQ, Q_LORA), (Z_CKV, KV_LORA))):
                            j = (t * Q_LORA, T * Q_LORA + t * KV_LORA)[c]
                            v = z[:, t, at:at + n]
                            ins = V.tensor_tensor_reduce(out=kT[:, j:j + n], in0=v, in1=v, scale=1.0, scalar=0.0, op0=ALU.mult,
                                                         op1=ALU.add, accum_out=statv[:, t, c:c + 1])
                    link(ins)
                    heads = G_HEADS + G_KV
                    qk = z[:, :, Z_GQ:Z_GQ + heads * HD]
                    sq = kT[:, 0:T * heads * HD]
                    link(V.tensor_tensor(sq.rearrange("p (t n) -> p t n", t=T), qk, qk, ALU.mult))
                    link(V.tensor_reduce(statv[:, :, 2:12], sq.rearrange("p (t h d) -> p t h d", t=T, d=HD), AX, ALU.add))
                    for a0, a1, count in ((0, 1, Q_LORA), (1, 2, KV_LORA), (2, 12, HD)):
                        ins = V.tensor_scalar(statv[:, :, a0:a1], statv[:, :, a0:a1], 1.0 / count, EPS, ALU.mult, ALU.add)
                    ins.then_inc(S["var_ready"], 1)
                    dve.wait_ge(S["root_ready"], 2)
                    V.reciprocal(rs[:, 0:36], rs[:, 0:36]).then_inc(S["head_rs"], 1)
                    dve.wait_ge(S["head_rs"], 1)
                    for c, (at, n, g, done) in enumerate(((Z_CQ, Q_LORA, "q", "cq_ready"), (Z_CKV, KV_LORA, "kv", "ckv_ready"))):
                        for t in range(T):
                            v = z[:, t, at:at + n]
                            ins = V.scalar_tensor_tensor(v, v, rsv[:, t, c:c + 1], gains[:, GAIN[g]], ALU.mult, ALU.mult)
                        ins.then_inc(S[done], 1)

                    for k in range(3):
                        empty(("cqT", k), cqT[:, k, :], bank(("cqT", k), 384))
                    for k in range(2):
                        empty(("ckvT", k), ckvT[:, k, :], bank(("ckvT", k)))
                    tmp = kT[:, 0:M_ROPE], kT[:, M_ROPE:2 * M_ROPE]
                    for t in (1, 2):
                        v = z[:, t, Z_KPE:Z_KPE + M_ROPE].rearrange("p (h d) -> p h d", h=1)
                        link(rope(V, link, t, v, tmp[t - 1], 1, M_ROPE, K_C32, K_S32))
                    for kt in range(4):
                        src = c_kpe[:, :] if kt == 1 else z[:, (0, None, 1, 2)[kt], Z_KPE:Z_KPE + M_ROPE]
                        ins = V.tensor_copy(kmv[:, kt, :, M_NOPE:], src[:, None, :].to_broadcast([P, HALF, M_ROPE]))
                    ins.then_inc(S["km_ready"], 1)

                    def largest(key):
                        g, h, t = key[1:]
                        i = MAPS[g].index((g, h, t))
                        col = i % 4 if key[0] == "S" else 2 * (i % 2) + (key[0] == "S2")
                        dve.wait_ge(*filled(key))
                        V.tensor_reduce(nmax[:, col:col + 1], bank(key, P * len(keys_of(t))), AX, ALU.max,
                                        negate=True).then_inc(S["max_ready"], 1)

                    def softmax_maps(g):
                        m = MAPS[g]
                        for i in range(len(m) + 3):
                            if i < len(m):
                                largest(("S",) + m[i])
                            if 2 <= i < len(m) + 2 and J.taker[("PT",) + m[i - 2]] == "dve":
                                n = P * len(keys_of(m[i - 2][2]))
                                if i >= 4:
                                    dve.wait_ge(*filled(("O",) + m[i - 4]))
                                s = (i - 2) % 2
                                empty(("PT",) + m[i - 2], PTb[:, s * 384:s * 384 + n], bank(("PT",) + m[i - 2], n))
                            if i >= 3:
                                key, s = m[i - 3], (i - 3) % 4
                                dve.wait_ge(*emptied(("S",) + key))
                                link(V.reciprocal(rrec[:, s:s + 1], rsum[:, s:s + 1]))
                                dve.wait_ge(*filled(("O",) + key))
                                V.tensor_scalar(out_cols(*key), bank(("O",) + key, HD), rrec[:, s:s + 1], None,
                                                ALU.mult).then_inc(S["dve_emptied"], 1)

                    for c, g in enumerate(("ma", "mb")):
                        for kt in range(4):
                            key = ("kv", c, kt)
                            both = bank(key).rearrange("p (h d) -> p h d", h=HALF)
                            dve.wait_ge(*filled(key))
                            V.tensor_copy(kmv[:, kt, :, 0:M_NOPE], both[:, :, 0:M_NOPE])
                            V.tensor_copy(vmv[:, kt, c * HALF:(c + 1) * HALF, :], both[:, :, M_NOPE:]).then_inc(S["dve_emptied"], 1)
                        for t in (1, 2):
                            dve.wait_ge(*emptied(("qm", c, t)))
                            tmp = c_ckv[:, (t - 1) * 128:t * 128]
                            ins = rope(V, link, t, qmv[:, t, :, M_NOPE:], tmp, HALF, M_ROPE, K_C32, K_S32)
                            if t == 1:
                                link(ins)
                        ins.then_inc(S["qm_roped"], 1)
                        for h in range(HALF):
                            empty(("mkT", c, h), kTv[0:M_HD, c, h, :], bank(("mkT", c, h), C, slice(0, M_HD)))
                        if c == 1:
                            dve.wait_ge(S["cache_out"], l * POOL_COUNTS["cache_out"] + 16 * 6)
                        softmax_maps(g)

                    for b in range(2):
                        empty(("gkT", b), kTv[:, 0, b, :], bank(("gkT", b)))
                    softmax_maps("g")
                    for dst, at, q in ((qfb, Z_RQ, 0), (kfb, Z_RK, 2)):
                        src = z[:, :, at:at + R_HEADS * R_DK].rearrange("p t (h d) -> p t h d", h=R_HEADS)
                        for f in range(2):
                            decay = dec[:, None, 4 * (q + f):4 * (q + f) + 4, None].to_broadcast([P, T, R_HEADS, R_DK])
                            ins = V.tensor_tensor(dst[:, :, :, f, :], src, decay, ALU.mult)
                    ins.then_inc(S["qkfb_ready"], 1)
                    chunk = dec[:, 16:20, None].to_broadcast([P, R_HEADS, R_DV])
                    dve.wait_ge(S["masks_raw"], 1)
                    link(V.tensor_tensor(mask, mask, const[:, None, K_MF:K_MF + P].to_broadcast([P, R_HEADS, P]), ALU.mult))
                    link(V.tensor_tensor(maskb, maskb, const[:, None, K_MB:K_MB + P].to_broadcast([P, R_HEADS, P]), ALU.mult))
                    link(V.tensor_tensor(mask, mask, maskb, ALU.add))
                    link(V.tensor_scalar(kdup[:, 0:512], kdup[:, 0:512], R_DK ** -0.5, None, ALU.mult))
                    for b in range(4):
                        empty(("dkT", b), kTv[:, 1, b, :], bank(("dkT", b)))
                    m = MAPS["d"]

                    def difference(i):
                        n = P * len(keys_of(m[i][2]))
                        r = 2 * (i % 2)
                        p1, p2 = Pb[:, (i % 2) * 384:(i % 2) * 384 + n], Pb[:, 768:768 + n]
                        dve.wait_ge(*emptied(("S2",) + m[i]))
                        link(V.reciprocal(rrec[:, r:r + 2], rsum[:, r:r + 2]))
                        link(V.tensor_scalar(rrec[:, r + 1:r + 2], rrec[:, r + 1:r + 2], lamv[:, 5:6], None, ALU.mult))
                        link(V.tensor_scalar(p2, p2, rrec[:, r + 1:r + 2], None, ALU.mult))
                        V.scalar_tensor_tensor(p1, p1, rrec[:, r:r + 1], p2, ALU.mult, ALU.add).then_inc(S["pd_ready"], 1)

                    for i in range(len(m) + 1):
                        if i < len(m):
                            largest(("S1",) + m[i])
                            largest(("S2",) + m[i])
                        if i >= 1:
                            difference(i - 1)
                    link(V.tensor_tensor(state1, state0v, chunk, ALU.mult))
                    link(V.tensor_copy(state2, state0v))
                    empty(("KV", 0), state_ctx[:, :], bank(("KV", 0)))
                    dve.wait_ge(*filled(("KV", 1)))
                    V.tensor_tensor(state2[0:64], state1[0:64], psum[0:64, J.bank(("KV", 1)), :].rearrange("p (h v) -> p h v", h=R_HEADS),
                                    ALU.add).then_inc(S["dve_emptied"], 1)
                    dve.wait_ge(*filled(("KV", 2)))
                    V.tensor_tensor(state1[64:128], state1[64:128], psum[64:128, J.bank(("KV", 2)), :].rearrange("p (h v) -> p h v", h=R_HEADS),
                                    ALU.add).then_inc(S["dve_emptied"], 1)
                    dve.wait_ge(*emptied(("KV", 2)))
                    V.tensor_copy(state1[0:64], state0v[0:64]).then_inc(S["state_ready"], 1)
                    for t in range(T):
                        for odd in range(2):
                            key = ("A", t, odd)
                            dve.wait_ge(*filled(key))
                            V.tensor_tensor(AT[t][:, odd::2], bank(key, 2 * P).rearrange("p (h n) -> p h n", h=2), mask[:, odd::2],
                                            ALU.mult).then_inc(S["dve_emptied"], 1)

                    def heads_of(at):
                        return z[:, :, at:at + 512].rearrange("p t (h d) -> p t h d", d=128)

                    def per_head(v):
                        return v.rearrange("p (t h) -> p t h", t=T)

                    ro, do = heads_of(Z_RQ), heads_of(Z_DQ)
                    dve.wait_ge(*emptied(("R", T - 1)))
                    link(V.tensor_reduce(per_head(mu[:, :]), ro, AX, ALU.add))
                    link(V.tensor_scalar(mu[:, :], mu[:, :], 1.0 / R_DV, None, ALU.mult))
                    link(V.tensor_tensor(ro, ro, per_head(mu[:, :])[:, :, :, None].to_broadcast([P, T, 4, 128]), ALU.subtract))
                    for n, v in enumerate((ro, do)):
                        s4 = kT[:, n * 1536:(n + 1) * 1536].rearrange("p (t h d) -> p t h d", t=T, h=4)
                        link(V.tensor_tensor(s4, v, v, ALU.mult))
                        link(V.tensor_reduce(per_head(stat[:, 12 * n:12 * n + 12]), s4, AX, ALU.add))
                    variance(0, 24, 128, 2)
                    for n, v in enumerate((ro, do)):
                        link(V.tensor_tensor(v, v, per_head(rs[:, 12 * n:12 * n + 12])[:, :, :, None].to_broadcast([P, T, 4, 128]), ALU.mult))
                    rr = z[:, :, Z_RQ:Z_RQ + 512]
                    link(V.tensor_tensor(rr, rr, gains[:, None, GAIN["ret"]].to_broadcast([P, T, 512]), ALU.mult))
                    link(V.tensor_tensor(rr, rr, z[:, :, Z_RG:Z_RG + 512], ALU.mult))
                    V.tensor_tensor(do, do, gains[:, None, None, GAIN["diff"]].to_broadcast([P, T, 4, 128]), ALU.mult).then_inc(S["head_normed"], 1)
                    dve.wait_ge(S["head_normed"], 1)

                    for n in range(NBR):
                        for k in range(4):
                            empty(("oT", n, k), oT[:, k, :], bank(("oT", n, k), 384))
                        for c in range(2):
                            for t in range(T):
                                i = GATES.index((n, c, t))
                                dst = merged[:, t, c * C:(c + 1) * C]
                                dve.wait_ge(*emptied(("gl", n, c, t)))
                                dve.wait_ge(*filled(("br", n, c, t)))
                                V.tensor_tensor(dst if n == 0 else gtmp, bank(("br", n, c, t)), gs[i % 2],
                                                ALU.mult).then_inc(S["dve_emptied"], 1)
                                dve.wait_ge(*emptied(("br", n, c, t)))
                                if n:
                                    link(V.tensor_tensor(dst, dst, gtmp, ALU.add))
                    V.tensor_copy(mu[:, 0:1], merged[:, 0, 0:1]).then_inc(S["merged_ready"], 1)
                    for k in range(0, KD, 2):
                        empty(("mgT", k), hTv[:, k, :], bank(("mgT", k), 384))

                    def residual(rows_m, n, site):
                        dve.wait_ge(S["gates_in"], l * POOL_COUNTS["gates_in"] + 48 * (n + 1))
                        for v in range(2):
                            ins = V.tensor_tensor(gp[:, v], gp[:, v], gpost, ALU.mult)
                        link(ins)
                        dve.wait_ge(S["x_squared"], T * (2 if n == 0 else 4))
                        variance(0, T, D, site)
                        for t in range(T):
                            ins = V.scalar_tensor_tensor(rows_m[:, t], rows_m[:, t], rs[:, t:t + 1], gp[:, min(t, 1)], ALU.mult, ALU.mult)
                        link(ins)
                        V.tensor_tensor(xv, xv, rows_m, ALU.add).then_inc(S["x_ready"], 1)
                        dve.wait_ge(S["x_ready"], n + 1)

                    residual(m_row, 0, 3)
                    dve.wait_ge(S["x_squared"], 3 * T)
                    variance(0, T, D, 4)
                    for t in range(T):
                        ins = V.tensor_scalar(xn2[:, t], xv[:, t], rs[:, t:t + 1], None, ALU.mult)
                    ins.then_inc(S["xn_ready"], 1)
                    dve.wait_ge(*emptied(("route",)))
                    link(V.tensor_scalar(rt[:, R_SC], rt[:, R_EXP], 1.0, None, ALU.add))
                    link(V.reciprocal(rt[:, R_SC], rt[:, R_SC]))
                    link(V.tensor_tensor(rt[:, R_SEL], rt[:, R_SC], brt[:, None, :].to_broadcast([P, T, NE]), ALU.add))
                    for t in range(T):
                        for g in range(NG):
                            ins = V.max(rt[:, R_TOP, t, g * EG:(g + 1) * EG], rt[:, R_SEL, t, g * EG:(g + 1) * EG])
                    link(ins)
                    top = rt[:, R_TOP].rearrange("p t (g e) -> p t g e", g=NG)
                    grp = rt[:, R_GRP, :, 0:NG]
                    link(V.tensor_tensor(grp, top[:, :, :, 0], top[:, :, :, 1], ALU.add))
                    dve.wait_ge(S["earlier_in"], 16)

                    def rank(v, dst, n):
                        c1, c2 = cmp1[:, :, 0:n, 0:n], cmp2[:, :, 0:n, 0:n]
                        vj, vi = v[:, :, None, :].to_broadcast([P, T, n, n]), v[:, :, :, None].to_broadcast([P, T, n, n])
                        link(V.tensor_tensor(c2, vj, vi, ALU.is_equal))
                        link(V.tensor_tensor(c2, c2, before[:, None, 0:n, 0:n].to_broadcast([P, T, n, n]), ALU.mult))
                        link(V.tensor_tensor(c1, vj, vi, ALU.is_gt))
                        link(V.tensor_tensor(c1, c1, c2, ALU.add))
                        link(V.tensor_reduce(dst, c1, AX, ALU.add))

                    gr = rt[:, R_GRP, :, NG:2 * NG]
                    gm = rt[:, R_GRP, :, 2 * NG:3 * NG]
                    go = rt[:, R_GRP, :, 3 * NG:4 * NG]
                    rank(grp, gr, NG)
                    link(V.tensor_scalar(gm, gr, float(TOPG), None, ALU.is_lt))
                    link(V.tensor_scalar(go, gm, -1.0, 1e30, ALU.add, ALU.mult))
                    sel4 = rt[:, R_SEL].rearrange("p t (g e) -> p t g e", g=NG)
                    ms4 = rt[:, R_MSEL].rearrange("p t (g e) -> p t g e", g=NG)
                    link(V.tensor_tensor(ms4, sel4, gm[:, :, :, None].to_broadcast([P, T, NG, EG]), ALU.mult))
                    link(V.tensor_tensor(ms4, ms4, go[:, :, :, None].to_broadcast([P, T, NG, EG]), ALU.add))
                    rank(rt[:, R_MSEL], rt[:, R_RANK], NE)
                    link(V.tensor_scalar(rt[:, R_RANK], rt[:, R_RANK], float(TOPK), None, ALU.is_lt))
                    link(V.tensor_tensor(rt[:, R_COMB], rt[:, R_SC], rt[:, R_RANK], ALU.mult))
                    link(V.tensor_reduce(mu[:, 0:3], rt[:, R_COMB], AX, ALU.add))
                    link(V.reciprocal(mu[:, 0:3], mu[:, 0:3]))
                    link(V.scalar_tensor_tensor(rt[:, R_COMB], rt[:, R_COMB], ROUTE_SCALE,
                                                mu[:, 0:3, None].to_broadcast([P, T, NE]), ALU.mult, ALU.mult))

                    def product(key, u, turns=0):
                        dve.wait_ge(S["silu_ready"], turns * 2 * T + u + 1)
                        V.tensor_tensor(av[:, u % 2], psum[:, J.bank(key), FF:2 * FF], silu[:, u % 2], ALU.mult).then_inc(S["dve_emptied"], 1)

                    product(("gu", "s", 0), 0)
                    for t in range(T):
                        product(("gu", "s", t + 1) if t + 1 < T else ("gu", 0, 0), t + 1)
                        for c in range(2):
                            empty(("y", "s", t, c), acc[:, t, c * C:(c + 1) * C], bank(("y", "s", t, c)))

                    def two_experts(turns, last=False):
                        for e in range(2):
                            for t in range(T):
                                u = T + e * T + t
                                less = 1 if last and u == 3 * T - 1 else 0
                                if not less:
                                    product(("gu", e, t + 1) if t + 1 < T else ("gu", e + 1, 0), u + 1, turns)
                                for c in range(2):
                                    key = ("y", e, t, c)
                                    dst = acc[:, t, c * C:(c + 1) * C]
                                    at = turns * 2 + e
                                    col = R_COMB * T * NE + t * NE + at
                                    w = Pb[:, col:col + 1] if isinstance(col, int) else Pb[:, bass.ds(col, 1)]
                                    dve.wait_ge(S["psum_filled"], turns * TURN_JOBS + J.filled(key) - less)
                                    before_key = ("y", "s" if e == 0 else 0, t, c)
                                    dve.wait_ge(S["dve_emptied"], turns * TURN_DVE + J.rank[before_key])
                                    V.scalar_tensor_tensor(dst, bank(key), w, dst, ALU.mult, ALU.add).then_inc(S["dve_emptied"], 1)

                    with dve.Fori(0, TURNS - 1) as turn:
                        two_experts(turn)
                    two_experts(TURNS - 1, last=True)
                    dve.wait_ge(S["dve_emptied"], LAST_DVE)
                    residual(acc, 1, 5)

                @block.tensor
                def _(pe):
                    def bank_free(key, turns=0):
                        j = J.number[key] - 8
                        if j < 0:
                            return
                        old = J.order[j]
                        name, per = ("act_emptied", TURN_ACT) if J.taker[old] == "act" else ("dve_emptied", TURN_DVE)
                        pe.wait_ge(S[name], turns * per + J.rank[old])

                    def multiply(key, dst, pairs):
                        for i, (lhsT, rhs) in enumerate(pairs):
                            ins = nc.tensor.matmul(dst, lhsT, rhs, start=(i == 0), stop=(i == len(pairs) - 1))
                        return ins

                    def turn_rows(key, sources, n=P):
                        bank_free(key)
                        for i, src in enumerate(sources):
                            ins = nc.tensor.transpose(psum[0:n, J.bank(key), i * P:(i + 1) * P], src, ident)
                        ins.then_inc(S["psum_filled"], 1)

                    def project(key, t, w, at, n, k_tiles, src=hTv):
                        bank_free(key)
                        multiply(key, bank(key, n), [(src[:, k, t * P:(t + 1) * P], w[:, k, at:at + n])
                                                     for k in range(k_tiles)]).then_inc(S["psum_filled"], 1)

                    for m in range(12):
                        pe.wait_ge(*landed(("mod", m)))
                        w = weights(("mod", m), KD, C)
                        bank_free(("mod", m))
                        multiply(("mod", m), bank(("mod", m), C, slice(0, 2)),
                                 [(silTv[:, k, :], w[:, k, :]) for k in range(KD)]).then_inc(S["psum_filled"], 1)
                    pe.wait_ge(*emptied(("mod", 11)))
                    for q, at in enumerate((0, D, 3 * D, 4 * D)):
                        for k in range(KD):
                            col = (q * KD + k) * 2
                            ins = nc.tensor.transpose(psum[:, J.bank(("modT",)), col:col + 2], modrow[:, at + k * P:at + (k + 1) * P],
                                                      const[0:2, K_ID:K_ID + 2])
                    ins.then_inc(S["psum_filled"], 1)
                    pe.wait_ge(S["xn_ready"], 1)
                    for k in range(KD):
                        turn_rows(("h1", k), [xn[:, t, k * P:(k + 1) * P] for t in range(T)])
                    pe.wait_ge(*emptied(("h1", KD - 1)))
                    for s in SEGS:
                        pe.wait_ge(*landed(("z", s)))
                        n = SEG[s][1]
                        for t in range(T):
                            project(("z", s, t), t, weights(("z", s), KD, n), 0, n, KD)
                    pe.wait_ge(S["cq_ready"], 1)
                    for k in range(3):
                        turn_rows(("cqT", k), [z[:, t, Z_CQ + k * P:Z_CQ + (k + 1) * P] for t in range(T)])
                    pe.wait_ge(S["ckv_ready"], 1)
                    pe.wait_ge(S["params_in"], 16 * N_PARAMS)
                    for k in range(2):
                        turn_rows(("ckvT", k), [tile_rows(c_ckv, Z_CKV, KV_LORA, kt)[:, k * P:(k + 1) * P] for kt in range(4)])
                    pe.wait_ge(*landed(("uq",)))
                    pe.wait_ge(*landed(("ukv",)))

                    def softmax_maps(g):
                        m = MAPS[g]
                        for i in range(len(m) + 3):
                            if i < len(m):
                                key = ("S",) + m[i]
                                bank_free(key)
                                multiply(key, bank(key, P * len(keys_of(m[i][2]))), [(queries(*m[i]), keys(*m[i]))]).then_inc(S["psum_filled"], 1)
                            if 2 <= i < len(m) + 2:
                                j = i - 2
                                pe.wait_ge(*emptied(("S",) + m[j]))
                                base = (j % 3) * 384
                                turn_rows(("PT",) + m[j], [Pb[:, base + b * P:base + (b + 1) * P] for b in range(len(keys_of(m[j][2])))])
                            if i >= 3:
                                weigh_values(m[i - 3], (i - 3) % 2)

                    def weigh_values(mp, s):
                        key = ("O",) + mp
                        g, h, t = mp
                        bank_free(key)
                        pe.wait_ge(*emptied(("PT",) + mp))
                        multiply(key, bank(key, F_DV if g == "d" else HD),
                                 [(PTb[:, s * 384 + b * P:s * 384 + (b + 1) * P], values(g, h, kt))
                                  for b, kt in enumerate(keys_of(t))]).then_inc(S["psum_filled"], 1)

                    for c, g in enumerate(("ma", "mb")):
                        if c == 0:
                            pe.wait_ge(*emptied(("cqT", 2)))
                        uq = weights(("uq",), 3, M_HEADS * M_HD)
                        ukv = weights(("ukv",), 2, D)
                        for t in range(T):
                            project(("qm", c, t), t, uq, c * 384, 384, 3, cqT)
                        if c == 0:
                            pe.wait_ge(*emptied(("ckvT", 1)))
                        for kt in range(4):
                            project(("kv", c, kt), kt, ukv, c * C, C, 2, ckvT)
                        pe.wait_ge(S["km_ready"], 1)
                        pe.wait_ge(*emptied(("kv", c, 3)))
                        for h in range(HALF):
                            turn_rows(("mkT", c, h), [kmv[:, kt, h, :] for kt in range(4)], M_HD)
                        pe.wait_ge(S["qm_roped"], c + 1)
                        pe.wait_ge(*emptied(("qm", c, 2)))
                        for h in range(HALF):
                            turn_rows(("mqT", c, h), [qmv[:, t, h, :] for t in range(T)], M_HD)
                        pe.wait_ge(*emptied(("mkT", c, HALF - 1)))
                        pe.wait_ge(*emptied(("mqT", c, HALF - 1)))
                        softmax_maps(g)
                    pe.wait_ge(S["kdup_ready"], 1)
                    for b in range(4):
                        turn_rows(("gqT", b), [z[:, t, Z_GQ + b * P:Z_GQ + (b + 1) * P] for t in range(T)])
                    for b in range(2):
                        turn_rows(("gkT", b), [kdv[:, kt, b].rearrange("p c d -> p (c d)") for kt in range(4)])
                    pe.wait_ge(*emptied(("gqT", 3)))
                    pe.wait_ge(*emptied(("gkT", 1)))
                    softmax_maps("g")
                    pe.wait_ge(S["diff_roped"], 1)
                    for b in range(4):
                        turn_rows(("dqT", b), [z[:, t, Z_DQ + b * P:Z_DQ + (b + 1) * P] for t in range(T)])
                    for b in range(4):
                        turn_rows(("dkT", b), [tile_rows(c_dk, Z_DK, 512, kt)[:, b * P:(b + 1) * P] for kt in range(4)])
                    pe.wait_ge(*emptied(("dqT", 3)))
                    pe.wait_ge(*emptied(("dkT", 3)))
                    m = MAPS["d"]
                    for i in range(len(m) + 2):
                        if i < len(m):
                            _, h, t = m[i]
                            cols = slice(0, P) if t == 0 else slice(P, 4 * P)
                            for s in range(2):
                                half = slice(64 * s, 64 * s + 64)
                                key = (("S1", "S2")[s],) + m[i]
                                bank_free(key)
                                multiply(key, bank(key, P * len(keys_of(t))), [(qTv[half, 1, h, t * P:(t + 1) * P], kTv[half, 1, h, cols])]
                                         ).then_inc(S["psum_filled"], 1)
                        if 1 <= i < len(m) + 1:
                            j = i - 1
                            pe.wait_ge(S["pd_ready"], j + 1)
                            base = (j % 2) * 384
                            turn_rows(("PT",) + m[j], [Pb[:, base + b * P:base + (b + 1) * P] for b in range(len(keys_of(m[j][2])))])
                        if i >= 2:
                            weigh_values(m[i - 2], (i - 2) % 2)
                    for b in range(2):
                        turn_rows(("rqT", b), [z[:, t, Z_RQ + b * P:Z_RQ + (b + 1) * P] for t in range(T)])
                    for b in range(2):
                        turn_rows(("rkT", b), [z[:, t, Z_RK + b * P:Z_RK + (b + 1) * P] for t in range(T)])
                    pe.wait_ge(S["qkfb_ready"], 1)
                    for h in range(R_HEADS):
                        turn_rows(("qfbT", h), [qfb[:, t, h].rearrange("p f d -> p (f d)") for t in range(T)])

                    def retained(t, h):
                        return z[:, t, Z_RV + h * R_DV:Z_RV + (h + 1) * R_DV]

                    def part(key, h):
                        return psum[:, J.bank(key), h * P:(h + 1) * P]

                    for t in range(T):
                        bank_free(("KV", t))
                        for h in range(R_HEADS):
                            ins = multiply(("KV", t), part(("KV", t), h), [(kfb[:, t, h].rearrange("p f d -> p (f d)"), retained(t, h))])
                        ins.then_inc(S["psum_filled"], 1)
                    pe.wait_ge(*emptied(("rkT", 1)))
                    for t in range(T):
                        for odd in range(2):
                            key = ("A", t, odd)
                            bank_free(key)
                            for pair in range(2):
                                half, cols = slice(64 * odd, 64 * odd + 64), slice(t * P, (t + 1) * P)
                                ins = multiply(key, part(key, pair), [(qTv[half, 0, 2 + pair, cols], qTv[half, 0, pair, cols])])
                            ins.then_inc(S["psum_filled"], 1)
                    pe.wait_ge(*emptied(("qfbT", R_HEADS - 1)))
                    pe.wait_ge(S["state_ready"], 1)
                    for t in range(T):
                        bank_free(("R", t))
                        pe.wait_ge(*emptied(("A", t, 1)))
                        for h in range(R_HEADS):
                            pairs = [(AT[t][:, h, :], retained(t, h))]
                            if t:
                                pairs.append((qfbT[:, h, t * P:(t + 1) * P], (state1, state2)[t - 1][:, h, :]))
                            ins = multiply(("R", t), part(("R", t), h), pairs)
                        ins.then_inc(S["psum_filled"], 1)
                    for n in range(NBR):
                        pe.wait_ge(S["head_normed"], 1)
                        for k in range(4):
                            turn_rows(("oT", n, k), [z[:, t, OUT_COLS[n] + k * P:OUT_COLS[n] + (k + 1) * P] for t in range(T)])
                        for c in range(2):
                            pe.wait_ge(*landed(("gl", n, c)))
                            pe.wait_ge(*landed(("br", n, c)))
                            for t in range(T):
                                project(("gl", n, c, t), t, weights(("gl", n, c), KD, C), 0, C, KD)
                                if c == 0 and t == 0:
                                    pe.wait_ge(*emptied(("oT", n, 3)))
                                project(("br", n, c, t), t, weights(("br", n, c), 4, C), 0, C, 4, oT)
                    pe.wait_ge(S["merged_ready"], 1)
                    for k in range(KD):
                        turn_rows(("mgT", k), [merged[:, t, k * P:(k + 1) * P] for t in range(T)])
                    pe.wait_ge(*emptied(("mgT", KD - 2)))
                    pe.wait_ge(*emptied(("mgT", KD - 1)))
                    for c in range(2):
                        pe.wait_ge(*landed(("out", c)))
                        for t in range(T):
                            project(("out", c, t), t, weights(("out", c), KD, C), 0, C, KD)
                    pe.wait_ge(S["xn_ready"], 2)
                    for k in range(KD):
                        turn_rows(("h2", k), [xn2[:, t, k * P:(k + 1) * P] for t in range(T)])
                    pe.wait_ge(*emptied(("h2", KD - 1)))
                    bank_free(("route",))
                    for t in range(T):
                        ins = multiply(("route",), psum[:, J.bank(("route",)), t * NE:(t + 1) * NE],
                                       [(hTv[:, k, t * P:(t + 1) * P], wr[:, k * NE:(k + 1) * NE]) for k in range(KD)])
                    ins.then_inc(S["psum_filled"], 1)

                    def gate_up(key, t, s, turns=0):
                        bank_free(key, turns)
                        multiply(key, bank(key), [(hTv[:, k, t * P:(t + 1) * P], expert_gu(s)[:, k, :]) for k in range(KD)]
                                 ).then_inc(S["psum_filled"], 1)

                    def down(e, t, u, s, turns=0, less=0):
                        gu = ("gu", e, t)
                        own = 0 if (gu in J.rank) else None
                        pe.wait_ge(S["dve_emptied"], turns * TURN_DVE + J.rank[gu])
                        bank_free(("aT", e, t), turns)
                        for f in range(2):
                            ins = nc.tensor.transpose(psum[:, J.bank(("aT", e, t)), f * P:(f + 1) * P], av[:, u % 2, f * P:(f + 1) * P], ident)
                        ins.then_inc(S["psum_filled"], 1)
                        pe.wait_ge(S["act_emptied"], turns * TURN_ACT + J.rank[("aT", e, t)])
                        for c in range(2):
                            key = ("y", e, t, c)
                            bank_free(key, turns)
                            multiply(key, bank(key), [(aT[:, u % 2, f, :], expert_dn(s)[:, f, c * C:(c + 1) * C]) for f in range(2)]
                                     ).then_inc(S["psum_filled"], 1)

                    pe.wait_ge(S["e_landed1"], 32)
                    gate_up(("gu", "s", 0), 0, 1)
                    for t in range(T):
                        if t + 1 < T:
                            gate_up(("gu", "s", t + 1), t + 1, 1)
                        else:
                            pe.wait_ge(S["e_landed0"], 32)
                            gate_up(("gu", 0, 0), 0, 0)
                        down("s", t, t, 1)

                    def two_experts(turns, last=False):
                        for e in range(2):
                            for t in range(T):
                                u = T + e * T + t
                                if t + 1 < T:
                                    gate_up(("gu", e, t + 1), t + 1, e, turns)
                                elif not (last and e == 1):
                                    if e == 0:
                                        pe.wait_ge(S["e_landed1"], turns * 32 + 64)
                                    else:
                                        pe.wait_ge(S["e_landed0"], turns * 32 + 64)
                                    gate_up(("gu", e + 1, 0), 0, 1 - e, turns)
                                down(e, t, u, e, turns)

                    with pe.Fori(0, TURNS - 1) as turn:
                        two_experts(turn)
                    two_experts(TURNS - 1, last=True)

            nc.gpsimd.sem_clear(range(sems[0].num, sems[-1].num + 1))
            nc.all_engine_barrier()

        with nc.Block() as block:
            @block.sync
            def _(sp):
                sp.dma_start(a["outs"]["y_prompt"][0], xv[:, 0, :]).then_inc(y_out, 16)
                sp.dma_start(a["outs"]["y_sample"][0].rearrange("(t p) n -> p t n", p=P), xv[:, 1:3, :]).then_inc(y_out, 16)
                sp.wait_ge(y_out, 32)


INPUTS = ["x_prompt", "x_sample", "cache_mla_ckv", "cache_mla_kpe", "cache_gqa_k", "cache_gqa_v", "cache_diff_k",
          "cache_diff_v", "state_ret", "c", "c_ctx", "w_mod", "b_mod", "g_pre1", "g_post1", "g_pre2", "g_post2", "w_in",
          "g_mla_q", "w_mla_uq", "g_mla_kv", "w_mla_ukv", "g_gqa_q", "g_gqa_k", "ret_decay", "g_ret", "diff_lambda",
          "g_diff", "w_br", "w_out", "w_router", "b_router", "w_exp_gu", "w_exp_down", "w_sh_gu", "w_sh_down"]
OUTPUTS = [("y_prompt", (1, P, D)), ("y_sample", (1, 2 * P, D)), ("mla_ckv", (1, DEPTH, P, KV_LORA)),
           ("mla_kpe", (1, DEPTH, P, M_ROPE)), ("gqa_k", (1, DEPTH, P, G_KV, HD)), ("gqa_v", (1, DEPTH, P, G_KV, HD)),
           ("diff_k", (1, DEPTH, P, F_HEADS, 2, HD)), ("diff_v", (1, DEPTH, P, F_HEADS, F_DV)),
           ("state_ret", (1, DEPTH, 2, R_HEADS, R_DK, R_DV))]


def kernel(**inputs):
    import concourse.bacc as bacc
    from concourse.bass_utils import run_bass_kernel_spmd

    nc = bacc.Bacc("TRN2", target_bir_lowering=False, num_devices=1)
    consts, earlier, lam_init = constants()
    arrays = {name: np.ascontiguousarray(inputs[name]) for name in INPUTS}
    arrays.update(consts=consts, earlier=earlier, lam_init=lam_init)
    a = {name: nc.dram_tensor(f"in_{name}", v.shape, F32, kind="ExternalInput").ap() for name, v in arrays.items()}
    a["gate_rows"] = nc.dram_tensor("gate_rows", (2, 2, D), F32, kind="Internal").ap()
    a["outs"] = {name: nc.dram_tensor(f"out_{name}", shape, F32, kind="ExternalOutput").ap() for name, shape in OUTPUTS}
    trunk(nc, a)
    r = run_bass_kernel_spmd(nc, [{f"in_{name}": v for name, v in arrays.items()}], core_ids=[0])
    return tuple(r.results[0][f"out_{name}"] for name, _ in OUTPUTS)
```

```python
import math
from contextlib import ExitStack

import numpy as np

import concourse.bass as bass
from concourse import mybir

P = 128
D = 1024
KD = D // P
T = 3
DEPTH = 2
F32 = mybir.dt.float32
U32 = mybir.dt.uint32
ALU = mybir.AluOpType
ACT = mybir.ActivationFunctionType
AX = mybir.AxisListType.X
EPS = 1e-6
C = 512

Q_LORA, KV_LORA, M_ROPE, M_NOPE, M_V, M_HEADS = 384, 256, 32, 64, 64, 8
M_HD = M_NOPE + M_ROPE
HALF = M_HEADS // 2
HD, G_HEADS, G_KV = 64, 8, 2
R_HEADS, R_DK, R_DV = 4, 64, 128
F_HEADS, F_DV = 4, 128
NE, TOPK, NG, TOPG, FF = 32, 4, 4, 2, 256
EG = NE // NG
ROUTE_SCALE = 2.5
NBR = 4
BW = 512

SEG = {}
_at = 0
for _name, _n in (("cq", Q_LORA), ("ckv", KV_LORA + M_ROPE), ("gq", G_HEADS * HD), ("gkv", 2 * G_KV * HD),
                  ("rqk", 2 * R_HEADS * R_DK), ("rv", R_HEADS * R_DV), ("rg", R_HEADS * R_DV),
                  ("dq", F_HEADS * 2 * HD), ("dk", F_HEADS * 2 * HD), ("dv", F_HEADS * F_DV)):
    SEG[_name] = (_at, _n)
    _at += _n
ZC = _at
SEGS = list(SEG)
Z_CQ, Z_CKV, Z_KPE = 0, Q_LORA, Q_LORA + KV_LORA
Z_GQ, Z_GK = SEG["gq"][0], SEG["gkv"][0]
Z_GV = Z_GK + G_KV * HD
Z_RQ = SEG["rqk"][0]
Z_RK = Z_RQ + R_HEADS * R_DK
Z_RV, Z_RG = SEG["rv"][0], SEG["rg"][0]
Z_DQ, Z_DK, Z_DV = SEG["dq"][0], SEG["dk"][0], SEG["dv"][0]
OUT_COLS = [Z_CQ, Z_GQ, Z_RQ, Z_DQ]
Z_MERGED = Z_RV
Z_M = Z_DQ

GAIN = {}
_at = 0
for _name, _n in (("q", Q_LORA), ("kv", KV_LORA), ("gq", HD), ("gk", HD), ("ret", R_HEADS * R_DV), ("diff", F_DV)):
    GAIN[_name] = slice(_at, _at + _n)
    _at += _n
GAINS = _at

K_ID, K_DF, K_DB, K_MF, K_MB, K_C64 = 0, 128, 256, 384, 512, 640
K_S64, K_C32, K_S32, K_POS, K_IOTA, K_N = 768, 896, 960, 1024, 1028, 1060
RANK_COLS = NE * NE


def constants():
    k = np.zeros((P, K_N), np.float32)
    k[:, K_ID:K_ID + P] = np.eye(P)
    j, i = np.meshgrid(np.arange(P), np.arange(P), indexing="ij")
    k[:, K_DF:K_DF + P] = np.maximum(i - j, 0)
    k[:, K_DB:K_DB + P] = np.maximum(j - i, 0)
    k[:, K_MF:K_MF + P] = i >= j
    k[:, K_MB:K_MB + P] = j >= i
    n = np.arange(2 * P)
    for d, at_c, at_s in ((64, K_C64, K_S64), (32, K_C32, K_S32)):
        quarter = d // 4
        freq = np.float32(10000.0) ** (-np.arange(quarter, dtype=np.float32) / np.float32(quarter))
        cos = np.zeros((2 * P, 2, 2, quarter), np.float32)
        sin = np.zeros_like(cos)
        for a, pos in enumerate((n // 64, n % 64)):
            ang = pos.astype(np.float32)[:, None] * freq[None]
            cos[:, a] = np.cos(ang)[:, None]
            sin[:, a, 0], sin[:, a, 1] = -np.sin(ang), np.sin(ang)
        for t in range(2):
            k[:, at_c + t * d:at_c + (t + 1) * d] = cos[t * P:(t + 1) * P].reshape(P, d)
            k[:, at_s + t * d:at_s + (t + 1) * d] = sin[t * P:(t + 1) * P].reshape(P, d)
    p = np.arange(P)
    k[:, K_POS:K_POS + 4] = np.stack([p + 1, P - p, P - 1 - p, p], 1)
    k[:, K_IOTA:K_IOTA + NE] = np.arange(NE)
    earlier = np.broadcast_to((np.arange(NE)[None, :] < np.arange(NE)[:, None]).reshape(1, -1), (P, NE * NE))
    lam = np.zeros((DEPTH, P, 2), np.float32)
    for layer in range(DEPTH):
        init = 0.8 - 0.6 * math.exp(-0.3 * layer)
        lam[layer] = [init, 1.0 - init]
    return k, np.ascontiguousarray(earlier.astype(np.float32)), lam


class PsumJobs:

    def __init__(self):
        self.number, self.taker, self.rank, self.banks, self.before = {}, {}, {}, {}, {}
        self.taken = {"act": 0, "dve": 0}
        self.last = {}

    def add(self, key, taker, bank=None):
        assert key not in self.number
        self.number[key] = len(self.number)
        self.taker[key] = taker
        self.taken[taker] += 1
        self.rank[key] = self.taken[taker]
        self.banks[key] = self.number[key] % 8 if bank is None else bank
        self.before[key] = self.last.get(self.banks[key])
        self.last[self.banks[key]] = key

    def filled(self, key):
        return self.number[key] + 1

    def bank(self, key):
        return self.banks[key]


def attention_maps():
    maps = {}
    for g, heads in (("ma", HALF), ("mb", HALF), ("g", G_HEADS), ("d", F_HEADS)):
        maps[g] = [(g, h, t) for h in range(heads) for t in range(T)]
    return maps


MAPS = attention_maps()


def plan_jobs():
    jobs = PsumJobs()
    for m in range(12):
        jobs.add(("mod", m), "dve")
    jobs.add(("modT",), "dve")
    for k in range(KD):
        jobs.add(("h1", k), "act")
    for s in SEGS:
        for t in range(T):
            jobs.add(("z", s, t), "act")
    for k in range(3):
        jobs.add(("cqT", k), "dve")
    for k in range(2):
        jobs.add(("ckvT", k), "dve")

    def softmax_maps(g):
        m = MAPS[g]
        for i in range(len(m) + 3):
            if i < len(m):
                jobs.add(("S",) + m[i], "act")
            if 2 <= i < len(m) + 2:
                jobs.add(("PT",) + m[i - 2], "act" if i % 2 else "dve")
            if i >= 3:
                jobs.add(("O",) + m[i - 3], "dve")

    for c, g in enumerate(("ma", "mb")):
        for t in range(T):
            jobs.add(("qm", c, t), "act")
        for kt in range(4):
            jobs.add(("kv", c, kt), "dve")
        for h in range(HALF):
            jobs.add(("mkT", c, h), "dve")
        for h in range(HALF):
            jobs.add(("mqT", c, h), "act")
        softmax_maps(g)
    for b in range(4):
        jobs.add(("gqT", b), "act")
    for b in range(2):
        jobs.add(("gkT", b), "dve")
    softmax_maps("g")
    for b in range(4):
        jobs.add(("dqT", b), "act")
    for b in range(4):
        jobs.add(("dkT", b), "dve")
    m = MAPS["d"]
    for i in range(len(m) + 2):
        if i < len(m):
            jobs.add(("S1",) + m[i], "act")
            jobs.add(("S2",) + m[i], "act")
        if 1 <= i < len(m) + 1:
            jobs.add(("PT",) + m[i - 1], "act")
        if i >= 2:
            jobs.add(("O",) + m[i - 2], "act")
    for b in range(2):
        jobs.add(("rqT", b), "act")
    for b in range(2):
        jobs.add(("rkT", b), "act")
    for h in range(R_HEADS):
        jobs.add(("qfbT", h), "act")
    for t in range(T):
        jobs.add(("KV", t), "dve")
    for t in range(T):
        for odd in range(2):
            jobs.add(("A", t, odd), "dve")
    for t in range(T):
        jobs.add(("R", t), "act")
    for n in range(NBR):
        for k in range(4):
            jobs.add(("oT", n, k), "dve")
        for c in range(2):
            for t in range(T):
                jobs.add(("gl", n, c, t), "act")
                jobs.add(("br", n, c, t), "dve")
    for k in range(KD):
        jobs.add(("mgT", k), "act" if k % 2 else "dve")
    for c in range(2):
        for t in range(T):
            jobs.add(("out", c, t), "act")
    for k in range(KD):
        jobs.add(("h2", k), "act")
    for t in range(T):
        for c in range(2):
            jobs.add(("hrow", t, c), "act" if c else "dve")
    jobs.add(("route",), "act")
    jobs.add(("gu", "s", 0), "dve")
    for t in range(T):
        if t == T - 1:
            jobs.add(("place",), "dve")
        if t + 1 < T:
            jobs.add(("gu", "s", t + 1), "dve")
        jobs.add(("aT", "s", t), "act")
        jobs.add(("y", "s", t, 0), "dve")
        jobs.add(("y", "s", t, 1), "dve")
    for i in range(2):
        for h in range(2):
            jobs.add(("xt", i, h), ("act", "dve")[h], BANK_XT + h)
    jobs.add(("gu", 0), "dve", BANK_GU)
    return jobs


CHOICES = T * P * TOPK
MORE = (CHOICES - 1) // (P + 1)
assert T == 3 and MORE == 11
NT = NE + MORE + 1
BANK_XT, BANK_GU, BANK_AT, BANK_Y = 0, 2, 4, 5
STEP = (("xt0", "act"), ("xt1", "dve"), ("gu", "dve"), ("aT", "act"), ("y0", "act"), ("y1", "dve"))
TURN_JOBS, TURN_TAKEN = 2 * len(STEP), 6
JOBS = plan_jobs()

FILLS = ([("mod", m) for m in range(12)] + [("z", s) for s in SEGS] + [("uq",), ("ukv",)]
         + [f for n in range(NBR) for c in range(2) for f in (("gl", n, c), ("br", n, c))] + [("out", 0), ("out", 1)])
SLOTS = 3
SLOT = KD * C
FILL = {key: i for i, key in enumerate(FILLS)}


def last_user(key):
    if key[0] == "mod":
        return key
    return {"uq": ("qm", 1, T - 1), "ukv": ("kv", 1, 3)}.get(key[0], (*key, T - 1))


MAX_AT = {}
for _g in ("ma", "mb", "g", "d"):
    for _m in MAPS[_g]:
        for _key in ((("S1", *_m), ("S2", *_m)) if _g == "d" else (_m,)):
            MAX_AT[_key] = len(MAX_AT) + 1
GATES = [(n, c, t) for n in range(NBR) for c in range(2) for t in range(T)]
N_PARAMS = 21



def trunk(nc, a):
    J = JOBS
    with ExitStack() as ctx:
        def sb(name, n, parts=P):
            return ctx.enter_context(nc.sbuf_tensor(name, [parts, n], F32))

        const = sb("const", K_N)
        x = sb("x", T * D)
        hT = sb("hT", KD * T * P)
        zf = sb("zf", 13824)
        W = sb("W", SLOTS * SLOT)
        silT = sb("silT", KD * 2)
        gains = sb("gains", GAINS)
        wr = sb("wr", KD * NE)
        brt = sb("brt", NE)
        gpre = sb("gpre", 2 * KD)
        modT = sb("modT", 4 * KD * 2)
        lamp = sb("lamp", 4 * HD)
        lamv = sb("lamv", 8)
        rdec = sb("rdec", 8)
        small = sb("small", 64)
        mu = sb("mu", 12)
        rrec = sb("rrec", 8)

        stat = sb("stat", 36)
        rs = sb("rs", 36)
        dec = sb("dec", 32)
        km = sb("km", 4 * HALF * M_HD)
        qm = sb("qm", T * HALF * M_HD)
        vm = sb("vm", 4 * M_HEADS * M_V)
        qT = sb("qT", 2 * 4 * T * P)
        kT = sb("kT", 2 * 4 * 4 * P)
        Pb = sb("Pb", 3 * T * P)
        PTb = sb("PTb", 2 * T * P)
        nmax = sb("nmax", 4)
        rsum = sb("rsum", 8)
        c_ckv = sb("c_ckv", KV_LORA)
        c_kpe = sb("c_kpe", M_ROPE)
        c_gk = sb("c_gk", G_KV * HD)
        c_gv = sb("c_gv", G_KV * HD)
        c_dk = sb("c_dk", 2 * F_HEADS * HD)
        c_dv = sb("c_dv", F_HEADS * F_DV)
        state0 = sb("state0", R_HEADS * R_DV)
        kdup = sb("kdup", 4 * G_KV * 2 * HD)
        rtmp = sb("rtmp", (G_HEADS + G_KV) * HD)
        psum = ctx.enter_context(nc.psum_tensor("psum", [P, 8, C], F32))

        names = ["psum_filled", "act_emptied", "dve_emptied", "params_in", "bmod_in", 
                 "x_squared", "var_ready", "head_rs", "earlier_in", "root_ready", "xn_ready", "modT_ready", 
                 "gp_ready", "dve_link", "act_link", "pool_link", "cq_ready", "ckv_ready",
                 "gqa_ready", "kdup_ready", "diff_roped", "qm_roped", "km_ready", "max_ready",
                 "pd_ready", "lam_ready", "absx_ready", "expx_ready", "u_ready", "ln_ready", "lg_ready",
                 "dec_ready", "qkfb_ready", "masks_raw", "mask_ready", "state_ready", "state_out", "ro_ready",
                 "do_ready", "gate_ready", "merged_ready", "m_squared", "x_ready", "chosen_ready", "slots_ready", "ones_ready", "gathers", "sp_steps", "table_reset", "slots_out", "table_in", "rows_out", "tables_ready", "summed", "silu_ready",
                 "lam_dots", "lam_exps", "head_normed"]
        names += ["gates_out", "gates_in", "cache_out"] + [f"{n}{i}" for n in ("x_landed", "y_written", "index_copied") for i in range(2)]
        names += [f"y_landed{i}" for i in range(6)]
        landed_names = [f"w_landed{i}" for i in range(SLOTS)] + ["gu_landed0", "gu_landed1", "dn_landed0", "dn_landed1"]
        sems = [nc.alloc_semaphore(n) for n in names + landed_names]
        S = dict(zip(names + landed_names, sems))
        const_in = nc.alloc_semaphore("const_in")
        silc_in = nc.alloc_semaphore("silc_in")
        silc_ready = nc.alloc_semaphore("silc_ready")
        y_out = nc.alloc_semaphore("y_out")
        zeros_ready = nc.alloc_semaphore("zeros_ready")
        zeros_out = nc.alloc_semaphore("zeros_out")

        def cview(at, n):
            return const[:, at:at + n]

        ident = cview(K_ID, P)
        xv = x[:, :].rearrange("p (t n) -> p t n", t=T)
        hTv = hT[:, :].rearrange("p (k n) -> p k n", k=KD)
        z = zf[:, 0:T * ZC].rearrange("p (t n) -> p t n", t=T)
        modrow = zf[0:2, 0:6 * D]
        xn = zf[:, 6 * D:9 * D].rearrange("p (t n) -> p t n", t=T)
        junk = zf[:, 9 * D:12 * D].rearrange("p (t n) -> p t n", t=T)
        silTv = silT[:, :].rearrange("p (k v) -> p k v", v=2)
        modTv = modT[:, :].rearrange("p (q k v) -> p q k v", q=4, v=2)
        qmv = qm[:, :].rearrange("p (t h d) -> p t h d", t=T, h=HALF)
        kmv = km[:, :].rearrange("p (t h d) -> p t h d", t=4, h=HALF)
        vmv = vm[:, :].rearrange("p (t h d) -> p t h d", t=4, h=M_HEADS)
        qTv = qT[:, :].rearrange("p (s b n) -> p s b n", s=2, b=4)
        kTv = kT[:, :].rearrange("p (s b n) -> p s b n", s=2, b=4)
        rsv = rs[:, :].rearrange("p (t n) -> p t n", t=T)
        statv = stat[:, :].rearrange("p (t n) -> p t n", t=T)
        kdv = kdup[:, :].rearrange("p (t k c d) -> p t k c d", t=4, k=G_KV, c=2)
        cqT = kT[:, 2048:2048 + 3 * T * P].rearrange("p (k n) -> p k n", k=3)
        ckvT = qT[:, 1536:1536 + 2 * 4 * P].rearrange("p (k n) -> p k n", k=2)
        qfb = vm[:, 0:T * R_HEADS * 2 * R_DK].rearrange("p (t h f d) -> p t h f d", t=T, h=R_HEADS, f=2)
        kfb = km[:, :].rearrange("p (t h f d) -> p t h f d", t=T, h=R_HEADS, f=2)
        qfbT = kTv[:, 0].rearrange("p b n -> p (b n)")[:, 0:4 * T * P].rearrange("p (h n) -> p h n", h=4)
        state1 = kTv[:, 0].rearrange("p b n -> p (b n)")[:, 1536:2048].rearrange("p (h v) -> p h v", h=R_HEADS)
        state2 = vm[:, 1536:2048].rearrange("p (h v) -> p h v", h=R_HEADS)
        state0v = state0[:, :].rearrange("p (h v) -> p h v", h=R_HEADS)
        state_ctx = c_dk
        mask = kdup[:, 0:512].rearrange("p (h n) -> p h n", h=R_HEADS)
        AT = [r.rearrange("p (h n) -> p h n", h=R_HEADS) for r in (PTb[:, 0:512], Pb[:, 0:512], Pb[:, 512:1024])]
        maskb = kdup[:, 512:1024].rearrange("p (h n) -> p h n", h=R_HEADS)
        oT = qTv[:, 0]
        gs = [kTv[:, 0, 0], kTv[:, 0, 1]]
        gtmp = kTv[:, 0, 2]
        gp = kT[:, 0:2 * D].rearrange("p (v n) -> p v n", v=2)
        gpost = kT[:, 2 * D:3 * D]
        merged = z[:, :, Z_MERGED:Z_MERGED + D]
        m_row = z[:, :, Z_M:Z_M + D]
        acc = zf[:, 0:3 * D].rearrange("p (t n) -> p t n", t=T)
        xn2 = zf[:, 3 * D:6 * D].rearrange("p (t n) -> p t n", t=T)
        av = zf[:, 6144:6656].rearrange("p (s n) -> p s n", s=2)
        silu = zf[:, 6656:7168].rearrange("p (s n) -> p s n", s=2)
        aT = zf[:, 7168:7680].rearrange("p (s f n) -> p s f n", s=2, f=2)
        cmp1 = zf[:, 7680:10752].rearrange("p (t i j) -> p t i j", t=T, i=NE)
        cmp2 = zf[:, 10752:13824].rearrange("p (t i j) -> p t i j", t=T, i=NE)
        cmpj = zf[:, 7680:10752].rearrange("p (t n) -> p t n", t=T)
        xg = zf[:, 7680:9728].rearrange("p (s n) -> p s n", s=2)
        xT = zf[:, 9728:11776].rearrange("p (s k n) -> p s k n", s=2, k=KD)
        yrow = zf[:, 11776:13824].rearrange("p (s n) -> p s n", s=2)
        ybuf = zf[:, 7680:13824].rearrange("p (s n) -> p s n", s=6)
        slot_f, weight, slot_u = vm[:, 1024:1036], vm[:, 1036:1048], vm[:, 1048:1060].bitcast(U32)
        token_f, token_u = vm[:, 1060:1063], vm[:, 1063:1066].bitcast(U32)
        tokens = vm[:, 1068:1068 + NT].bitcast(U32)
        index = vm[:, 1120:1122].bitcast(U32)
        expert_f, expert_u = vm[:, 1124:1124 + NT], vm[:, 1172:1172 + NT].bitcast(U32)
        turns_f, turns_u = vm[:, 1220:1221], vm[:, 1221:1222].bitcast(U32)
        ones = vm[:, 1232:1360]
        iota = const[:, K_IOTA:K_IOTA + NE]
        earlier = vm[:, 0:RANK_COLS]
        before = earlier.rearrange("p (i j) -> p i j", i=NE)
        rt = Pb[:, :].rearrange("p (s t e) -> p s t e", s=12, t=T)
        R_EXP, R_SC, R_SEL, R_RANK, R_COMB, R_MSEL, R_TOP, R_GRP, R_POS, R_SLOT, R_TMP, R_ROW = range(12)

        def slot(i):
            return W[:, (i % SLOTS) * SLOT:(i % SLOTS + 1) * SLOT]

        def weights(key, k, n):
            return slot(FILL[key])[:, 0:k * n].rearrange("p (k n) -> p k n", k=k)

        def expert_gu(s):
            return W[:, s * SLOT:(s + 1) * SLOT].rearrange("p (k n) -> p k n", k=KD)

        def expert_dn(s):
            return W[:, 2 * SLOT + s * SLOT // 2:2 * SLOT + (s + 1) * SLOT // 2].rearrange("p (k n) -> p k n", k=2)

        def landed(key):
            i = FILL[key]
            return S[f"w_landed{i % SLOTS}"], 16 * (i // SLOTS + 1)

        def filled(key):
            return S["psum_filled"], J.filled(key)

        def emptied(key):
            return S["act_emptied" if J.taker[key] == "act" else "dve_emptied"], J.rank[key]

        def bank(key, n=C, parts=slice(0, P)):
            return psum[parts, J.bank(key), 0:n]

        def rows(ap, l):
            r = ap[bass.ds(l, 1)]
            n = len(ap.shape)
            if n == 2:
                return r.rearrange("o n -> (o n)")
            return r.rearrange("o a b -> (o a) b") if n == 3 else r.rearrange("o a b c -> (o a) b c")

        def spread(ap1):
            return ap1.partition_broadcast(P)

        def in_turn(turn, e, name):
            order = [(i, n) for i in range(2) for n, _ in STEP]
            at = order.index((e, name))
            taker = dict(STEP)[name]
            rank = sum(dict(STEP)[n] == taker for _, n in order[:at + 1])
            return (len(J.number) + at + 1 + turn * TURN_JOBS,
                    S["act_emptied" if taker == "act" else "dve_emptied"], J.taken[taker] + rank + turn * TURN_TAKEN)

        def job_filled(turn, e, name, less=0):
            return S["psum_filled"], in_turn(turn, e, name)[0] - less

        def job_emptied(turn, e, name, less=0):
            _, sem, n = in_turn(turn, e, name)
            return sem, n - less

        def previous(turn, e):
            return (turn, 0) if e == 1 else (turn - 1, 1)

        LESS = {"filled": (2, 5), "act": (1, 2), "dve": (1, 3)}

        def turns_of(eng):
            eng.wait_ge(S["tables_ready"], 1)
            return eng.value_load(turns_u[0:1, 0:1], min_val=NE // 2, max_val=NT // 2)

        def linker(eng, sem):
            n = [0]

            def link(ins):
                n[0] += 1
                ins.then_inc(sem, 1)
                eng.wait_ge(sem, n[0])
            return link

        def rope(eng, link, t, v, tmp, heads, d, at_c, at_s):
            q = d // 4
            cos = cview(at_c + (t - 1) * d, d)
            sin = cview(at_s + (t - 1) * d, d).rearrange("p (a j i) -> p a j i", a=2, j=2)
            v4 = v.rearrange("p h (a j i) -> p h a j i", a=2, j=2)
            tm = tmp[:, 0:heads * d].rearrange("p (h d) -> p h d", d=d)
            t4 = tm.rearrange("p h (a j i) -> p h a j i", a=2, j=2)
            for j in range(2):
                ins = eng.tensor_tensor(t4[:, :, :, j, :], v4[:, :, :, 1 - j, :],
                                        sin[:, None, :, j, :].to_broadcast([P, heads, 2, q]), ALU.mult)
            link(ins)
            link(eng.tensor_tensor(v, v, cos[:, None, :].to_broadcast([P, heads, d]), ALU.mult))
            return eng.tensor_tensor(v, v, tm, ALU.add)

        def tile_rows(cache, col, n, kt):
            return cache[:, 0:n] if kt == 1 else z[:, (0, None, 1, 2)[kt], col:col + n]

        def keys_of(t):
            return (0,) if t == 0 else (1, 2, 3)

        def queries(g, h, t):
            if g in ("ma", "mb"):
                return qTv[0:M_HD, 0 if g == "ma" else 1, h, t * P:(t + 1) * P]
            return qTv[64 * (h % 2):64 * (h % 2) + 64, 0, h // 2, t * P:(t + 1) * P]

        def keys(g, h, t):
            cols = slice(0, P) if t == 0 else slice(P, 4 * P)
            if g in ("ma", "mb"):
                return kTv[0:M_HD, 0 if g == "ma" else 1, h, cols]
            return kTv[64 * (h % 2):64 * (h % 2) + 64, 0, h // (G_HEADS // G_KV), cols]

        def values(g, h, kt):
            if g in ("ma", "mb"):
                return vmv[:, kt, h + (HALF if g == "mb" else 0), :]
            if g == "g":
                return tile_rows(c_gv, Z_GV, P, kt)[:, HD * (h // 4):HD * (h // 4) + HD]
            return tile_rows(c_dv, Z_DV, 4 * P, kt)[:, F_DV * h:F_DV * (h + 1)]

        def out_cols(g, h, t):
            if g in ("ma", "mb"):
                h = h + (HALF if g == "mb" else 0)
                return z[:, t, Z_CQ + M_V * h:Z_CQ + M_V * (h + 1)]
            if g == "g":
                return z[:, t, Z_GQ + HD * h:Z_GQ + HD * (h + 1)]
            return z[:, t, Z_DQ + F_DV * h:Z_DQ + F_DV * (h + 1)]

        with nc.Block() as block:
            @block.sync
            def _(sp):
                sp.dma_start(const[:, :], a["consts"]).then_inc(const_in, 16)
                sp.dma_start(xv[:, 0, :], a["x_prompt"][0]).then_inc(const_in, 16)
                sp.dma_start(xv[:, 1:3, :], a["x_sample"][0].rearrange("(t p) n -> p t n", p=P)).then_inc(const_in, 16)
                sp.dma_start(silTv[:, :, 0], a["c_ctx"].rearrange("(k p) -> p k", p=P), allow_slow_non_contiguous=True).then_inc(silc_in, 16)
                sp.dma_start(silTv[:, :, 1], a["c"][0].rearrange("(k p) -> p k", p=P), allow_slow_non_contiguous=True).then_inc(silc_in, 16)
                sp.wait_ge(const_in, 48)

            @block.scalar
            def _(act):
                act.wait_ge(silc_in, 32)
                nc.scalar.activation(silT[:, :], silT[:, :], ACT.Silu).then_inc(silc_ready, 1)
                act.wait_ge(silc_ready, 1)
                act.wait_ge(zeros_ready, 1)
                act.dma_start(a["y_slots"].rearrange("(p i) n -> p i n", i=NT)[:, NE:, :],
                              vm[:, None, 0:D].to_broadcast([P, NT - NE, D])).then_inc(zeros_out, 16)

            @block.vector
            def _(dve):
                nc.vector.memset(vm[:, 0:D], 0.0).then_inc(zeros_ready, 1)

        with nc.Fori(0, DEPTH) as l:
            with nc.Block() as block:
                @block.sync
                def _(sp):
                    def source(key):
                        kind = key[0]
                        if kind == "mod":
                            return rows(a["w_mod"], l)[:, key[1] * C:(key[1] + 1) * C], KD, C
                        if kind == "z":
                            at, n = SEG[key[1]]
                            return rows(a["w_in"], l)[:, at:at + n], KD, n
                        if kind == "gl":
                            at = ZC + key[1] * D + key[2] * C
                            return rows(a["w_in"], l)[:, at:at + C], KD, C
                        if kind == "uq":
                            return rows(a["w_mla_uq"], l), 3, M_HEADS * M_HD
                        if kind == "ukv":
                            return rows(a["w_mla_ukv"], l), 2, D
                        if kind == "br":
                            return rows(a["w_br"], l)[key[1]][:, key[2] * C:(key[2] + 1) * C], 4, C
                        return rows(a["w_out"], l)[:, key[1] * C:(key[1] + 1) * C], KD, C

                    for i, key in enumerate(FILLS):
                        src, k, n = source(key)
                        if i >= SLOTS:
                            sp.wait_ge(*filled(last_user(FILLS[i - SLOTS])))
                        sp.dma_start(weights(key, k, n), src.rearrange("(k p) n -> p k n", p=P)).then_inc(landed(key)[0], 16)

                    def load_gate_up(s, src):
                        sp.dma_start(expert_gu(s), src.rearrange("(k p) n -> p k n", p=P)).then_inc(S[f"gu_landed{s}"], 16)

                    def load_down(s, src):
                        sp.dma_start(expert_dn(s), src.rearrange("(k p) n -> p k n", p=P)).then_inc(S[f"dn_landed{s}"], 16)

                    def expert(name, e):
                        return a[name].rearrange("l e d n -> (l e) d n")[bass.ds(l * NE + e, 1)].rearrange("o d n -> (o d) n")

                    sp.wait_ge(*filled(("out", 1, T - 1)))
                    load_gate_up(1, rows(a["w_sh_gu"], l))
                    load_down(1, rows(a["w_sh_down"], l))
                    load_gate_up(0, expert("w_exp_gu", 0))
                    load_down(0, expert("w_exp_down", 0))
                    sp.wait_ge(*filled(("gu", "s", T - 1)))
                    load_gate_up(1, expert("w_exp_gu", 1))
                    sp.wait_ge(*filled(("y", "s", T - 1, 1)))
                    load_down(1, expert("w_exp_down", 1))
                    sp.wait_ge(*filled(("gu", 0)))
                    load_gate_up(0, expert("w_exp_gu", 2))
                    for e in range(2):
                        sp.sem_inc(S[f"y_written{e}"], 16)
                    turns = turns_of(sp)

                    def write_rows(turn, e, less=(0, 0)):
                        sp.wait_ge(*job_emptied(turn, e, "y0", less[0]))
                        sp.sem_inc(S["sp_steps"], 1)
                        sp.wait_ge(*job_emptied(turn, e, "y1", less[1]))
                        sp.sem_inc(S["sp_steps"], 1)
                        dst = a["y_slots"].rearrange("(p i) n -> p i n", i=NT)[:, bass.ds(turn * 2 + e, 1), :].rearrange("p o n -> p (o n)")
                        sp.dma_start(dst, yrow[:, e, :]).then_inc(S[f"y_written{e}"], 16)

                    def expert_of(tile):
                        sp.sem_inc(S["sp_steps"], 1)
                        return sp.value_load(expert_u[0:1, bass.ds(tile, 1)], min_val=0, max_val=NE - 1)

                    def steps(turn, last=False):
                        for e in range(2):
                            tile = turn * 2 + e
                            if not (last and e == 1):
                                sp.wait_ge(*job_filled(turn, e, "gu"))
                                load_gate_up(1 - e, expert("w_exp_gu", expert_of(tile + 3)))
                            sp.wait_ge(*job_filled(turn, e, "y1"))
                            load_down(e, expert("w_exp_down", expert_of(tile + 2)))
                            write_rows(turn, e)

                    with sp.Fori(0, turns - 2) as turn:
                        steps(turn)
                    steps(turns - 2, last=True)
                    for e in range(2):
                        write_rows(turns - 1, e, (LESS["act"][e], LESS["dve"][e]))

                @block.gpsimd
                def _(pool):
                    link = linker(pool, S["pool_link"])
                    out = a["outs"]

                    def row(name):
                        r = out[name][0][bass.ds(l, 1)]
                        return r.rearrange({3: "o s n -> (o s) n", 4: "o s k d -> (o s) (k d)",
                                            5: "o s h c d -> (o s) (h c d)"}[len(r.shape)])

                    pool.wait_ge(*emptied(("mod", 11)))
                    for n, at in enumerate((2 * D, 5 * D)):
                        pool.dma_start(a["gate_rows"][n], modrow[:, at:at + D]).then_inc(S["gates_out"], 16)
                    pool.wait_ge(*emptied(("z", "gkv", 0)))
                    pool.dma_start(row("mla_kpe"), z[:, 0, Z_KPE:Z_KPE + M_ROPE]).then_inc(S["cache_out"], 16)
                    pool.dma_start(row("gqa_v"), z[:, 0, Z_GV:Z_GV + P]).then_inc(S["cache_out"], 16)
                    pool.wait_ge(*emptied(("z", "dv", T - 1)))
                    pool.dma_start(row("diff_k"), z[:, 0, Z_DK:Z_DK + 512]).then_inc(S["cache_out"], 16)
                    pool.dma_start(row("diff_v"), z[:, 0, Z_DV:Z_DV + 512]).then_inc(S["cache_out"], 16)
                    heads = G_HEADS + G_KV
                    pool.wait_ge(S["head_rs"], 1)
                    qk = z[:, :, Z_GQ:Z_GQ + heads * HD].rearrange("p t (h d) -> p t h d", d=HD)
                    link(nc.gpsimd.tensor_tensor(qk, qk, rsv[:, :, 2:2 + heads, None].to_broadcast([P, T, heads, HD]), ALU.mult))
                    for g, h0, h1 in (("gq", 0, G_HEADS), ("gk", G_HEADS, heads)):
                        gain = gains[:, None, None, GAIN[g]].to_broadcast([P, T, h1 - h0, HD])
                        link(nc.gpsimd.tensor_tensor(qk[:, :, h0:h1], qk[:, :, h0:h1], gain, ALU.mult))
                    pool.wait_ge(S["ckv_ready"], 1)
                    pool.dma_start(row("mla_ckv"), z[:, 0, Z_CKV:Z_CKV + KV_LORA]).then_inc(S["cache_out"], 16)
                    pool.dma_start(row("gqa_k"), z[:, 0, Z_GK:Z_GK + P]).then_inc(S["cache_out"], 16)
                    for t in (1, 2):
                        link(rope(nc.gpsimd, link, t, qk[:, t], rtmp[:, :], heads, HD, K_C64, K_S64))
                    for kt in range(4):
                        src = tile_rows(c_gk, Z_GK, G_KV * HD, kt).rearrange("p (k d) -> p k d", d=HD)
                        if kt == 1:
                            pool.wait_ge(S["params_in"], 16 * N_PARAMS)
                        for c in range(2):
                            ins = nc.gpsimd.tensor_copy(kdv[:, kt, :, c, :], src)
                    ins.then_inc(S["kdup_ready"], 1)
                    for t in (1, 2):
                        for at in (Z_DQ, Z_DK):
                            ins = rope(nc.gpsimd, link, t, z[:, t, at:at + 512].rearrange("p (h d) -> p h d", d=HD), rtmp[:, :],
                                       2 * F_HEADS, HD, K_C64, K_S64)
                            if (t, at) != (2, Z_DK):
                                link(ins)
                    ins.then_inc(S["diff_roped"], 1)
                    pool.wait_ge(*emptied(("KV", 0)))
                    for r in range(2):
                        so = out["state_ret"][0][bass.ds(l, 1)].rearrange("o r h k v -> (o r) k h v")[r]
                        pool.dma_start(so, state_ctx[64 * r:64 * r + 64, :].rearrange("p (h v) -> p h v", h=R_HEADS)
                                       ).then_inc(S["cache_out"], 16)
                    def fetch_gates(n):
                        for v in range(2):
                            pool.dma_start(gp[:, v, :], spread(a["gate_rows"][n, v])).then_inc(S["gates_in"], 16)
                        pool.dma_start(gpost, spread(rows(a["g_post1" if n == 0 else "g_post2"], l))).then_inc(S["gates_in"], 16)

                    pool.wait_ge(*filled(("R", T - 1)))
                    nc.gpsimd.memset(ones, 1.0).then_inc(S["ones_ready"], 1)
                    pool.wait_ge(*filled(("mgT", 0)))
                    fetch_gates(0)
                    pool.wait_ge(*filled(("gu", "s", 0)))
                    fetch_gates(1)
                    pool.wait_ge(S["table_reset"], 16)
                    pool.wait_ge(S["slots_ready"], 1)
                    for i in range(T * TOPK):
                        pool.indirect_dma_start(a["slot_tokens"], bass.IndirectOffsetOnAxis(ap=slot_u[:, i:i + 1], axis=0),
                                                token_u[:, i // TOPK:i // TOPK + 1], None).then_inc(S["slots_out"], 16)
                    pool.wait_ge(S["slots_out"], 16 * T * TOPK)
                    pool.dma_start(tokens, a["slot_tokens"].rearrange("(p i) o -> p (i o)", i=NT)).then_inc(S["table_in"], 16)
                    pool.wait_ge(S["table_in"], 16)
                    pool.wait_ge(S["rows_out"], 16 * T)

                    def gather(tile, e, n):
                        col = tokens[:, tile:tile + 1] if isinstance(tile, int) else tokens[:, bass.ds(tile, 1)]
                        nc.gpsimd.tensor_copy(index[:, e:e + 1], col).then_inc(S[f"index_copied{e}"], 1)
                        pool.wait_ge(S[f"index_copied{e}"], n)
                        pool.sem_inc(S["gathers"], 1)
                        pool.indirect_dma_start(xg[:, e, :], None, a["token_rows"],
                                                bass.IndirectOffsetOnAxis(ap=index[:, e:e + 1], axis=0)).then_inc(S[f"x_landed{e}"], 16)

                    for e in range(2):
                        gather(e, e, 1)
                    for e in range(2):
                        pool.wait_ge(*filled(("xt", e, 1)))
                        gather(2 + e, e, 2)
                    turns = turns_of(pool)
                    with pool.Fori(0, turns - 2) as turn:
                        for e in range(2):
                            pool.wait_ge(*job_filled(turn, e, "xt1"))
                            gather(turn * 2 + e + 4, e, turn + 3)
                    for e in range(2):
                        pool.wait_ge(S[f"y_written{e}"], turns * 16 + 16)
                        pool.sem_inc(S["gathers"], 1)
                    for i in range(T * TOPK):
                        if i >= 6:
                            pool.wait_ge(S["summed"], i - 5)
                        pool.indirect_dma_start(ybuf[:, i % 6, :], None, a["y_slots"],
                                                bass.IndirectOffsetOnAxis(ap=slot_u[:, i:i + 1], axis=0)).then_inc(S[f"y_landed{i % 6}"], 16)
                    pool.wait_ge(S["cache_out"], 16 * 8)
                    pool.wait_ge(S["summed"], T * TOPK)

                @block.scalar
                def _(act):
                    link = linker(act, S["act_link"])

                    def dma(dst, src, sem="params_in", scattered=False):
                        act.dma_start(dst, src, allow_slow_non_contiguous=scattered).then_inc(S[sem], 16)

                    dma(modrow, rows(a["b_mod"], l).partition_broadcast(2), "bmod_in")
                    for n, name in enumerate(("g_pre1", "g_pre2")):
                        dma(gpre[:, n * KD:(n + 1) * KD], rows(a[name], l).rearrange("(k p) -> p k", p=P), scattered=True)
                    for g, name in (("q", "g_mla_q"), ("kv", "g_mla_kv"), ("gq", "g_gqa_q"), ("gk", "g_gqa_k"),
                                    ("ret", "g_ret"), ("diff", "g_diff")):
                        dma(gains[:, GAIN[g]], spread(rows(a[name], l)))
                    dma(lamp[:, :], spread(rows(a["diff_lambda"], l).rearrange("a b -> (a b)")))
                    dma(lamv[:, 6:8], rows(a["lam_init"], l))
                    dma(rdec[:, :], spread(rows(a["ret_decay"], l).rearrange("a b -> (a b)")))
                    dma(brt[:, :], spread(rows(a["b_router"], l)))
                    dma(wr[:, :].rearrange("p (k n) -> p k n", k=KD), rows(a["w_router"], l).rearrange("(k p) n -> p k n", p=P))
                    for buf, name in ((c_ckv, "cache_mla_ckv"), (c_kpe, "cache_mla_kpe"), (c_gk, "cache_gqa_k"),
                                      (c_gv, "cache_gqa_v"), (c_dk, "cache_diff_k"), (c_dv, "cache_diff_v")):
                        src = a[name][0][bass.ds(l, 1)]
                        src = src.rearrange({3: "o s n -> (o s) n", 4: "o s k d -> (o s) (k d)",
                                             5: "o s h c d -> (o s) (h c d)"}[len(a[name].shape) - 1])
                        dma(buf[:, :], src)
                    for r in range(2):
                        src = a["state_ret"][0][bass.ds(l, 1)].rearrange("o r h k v -> (o r) k h v")[r]
                        dma(state0v[64 * r:64 * r + 64], src)

                    def square_rows(v, junk_rows, sem):
                        for t in range(T):
                            nc.scalar.activation(junk_rows[:, t], v[:, t], ACT.Square,
                                                 accum_out=stat[:, t:t + 1]).then_inc(S[sem], 1)

                    def root(n, site):
                        act.wait_ge(S["var_ready"], site + 1)
                        nc.scalar.activation(rs[:, 0:n], stat[:, 0:n], ACT.Sqrt).then_inc(S["root_ready"], 1)

                    square_rows(xv, junk, "x_squared")
                    root(T, 0)

                    def modulated(name, n):
                        for k in range(KD):
                            act.wait_ge(*filled((name, k)))
                            for v, cols in ((0, slice(0, P)), (1, slice(P, T * P))):
                                ins = nc.scalar.activation(hTv[:, k, cols], psum[:, J.bank((name, k)), cols], ACT.Identity,
                                                           scale=modTv[:, 2 * n + 1, k, v:v + 1], bias=modTv[:, 2 * n, k, v:v + 1])
                            ins.then_inc(S["act_emptied"], 1)

                    act.wait_ge(S["modT_ready"], 1)
                    modulated("h1", 0)

                    act.wait_ge(S["gates_out"], 32)
                    for s in SEGS:
                        at, n = SEG[s]
                        for t in range(T):
                            act.wait_ge(*filled(("z", s, t)))
                            nc.scalar.activation(z[:, t, at:at + n], bank(("z", s, t), n),
                                                 ACT.Silu if s == "rg" else ACT.Copy).then_inc(S["act_emptied"], 1)
                    act.wait_ge(S["absx_ready"], 1)
                    nc.scalar.activation(small[:, 8:16], small[:, 0:8], ACT.Exp, scale=-1.0).then_inc(S["expx_ready"], 1)
                    act.wait_ge(S["u_ready"], 1)
                    nc.scalar.activation(small[:, 24:32], small[:, 16:24], ACT.Ln).then_inc(S["ln_ready"], 1)
                    act.wait_ge(S["lg_ready"], 1)
                    for q in range(4):
                        f = q % 2
                        nc.scalar.activation(dec[:, 4 * q:4 * q + 4], small[:, 32 + 4 * f:36 + 4 * f], ACT.Exp,
                                             scale=const[:, K_POS + q:K_POS + q + 1])
                    for f in range(2):
                        ins = nc.scalar.activation(dec[64 * f:64 * f + 64, 16:20], small[64 * f:64 * f + 64, 32 + 4 * f:36 + 4 * f],
                                                   ACT.Exp, scale=float(P))
                    ins.then_inc(S["dec_ready"], 1)
                    act.wait_ge(S["lam_dots"], 1)
                    nc.scalar.activation(lamv[:, 2:4], lamv[:, 0:2], ACT.Exp).then_inc(S["lam_exps"], 1)
                    root(36, 1)

                    def softmax_maps(g):
                        m = MAPS[g]
                        for i in range(len(m) + 3):
                            if i < len(m):
                                key = m[i]
                                n = P * len(keys_of(key[2]))
                                act.wait_ge(S["max_ready"], MAX_AT[key])
                                if i >= 3:
                                    act.wait_ge(*filled(("PT",) + m[i - 3]))
                                if i >= 4:
                                    act.wait_ge(*emptied(("O",) + m[i - 4]))
                                nc.scalar.activation(Pb[:, (i % 3) * 384:(i % 3) * 384 + n], bank(("S",) + key, n), ACT.Exp,
                                                     bias=nmax[:, i % 4:i % 4 + 1], scale=1.0,
                                                     accum_out=rsum[:, i % 4:i % 4 + 1]).then_inc(S["act_emptied"], 1)
                            if 2 <= i < len(m) + 2 and J.taker[("PT",) + m[i - 2]] == "act":
                                empty_turned(i - 2, m)

                    def empty_turned(i, m):
                        key = ("PT",) + m[i]
                        n = P * len(keys_of(m[i][2]))
                        act.wait_ge(*filled(key))
                        if i >= 2:
                            act.wait_ge(*filled(("O",) + m[i - 2]))
                        nc.scalar.activation(PTb[:, (i % 2) * 384:(i % 2) * 384 + n], bank(key, n),
                                             ACT.Copy).then_inc(S["act_emptied"], 1)

                    for c, g in enumerate(("ma", "mb")):
                        for t in range(T):
                            act.wait_ge(*filled(("qm", c, t)))
                            if c == 1:
                                act.wait_ge(*filled(("mqT", 0, HALF - 1)))
                            nc.scalar.activation(qmv[:, t], bank(("qm", c, t), 384).rearrange("p (h d) -> p h d", h=HALF),
                                                 ACT.Copy).then_inc(S["act_emptied"], 1)
                        for h in range(HALF):
                            act.wait_ge(*filled(("mqT", c, h)))
                            if c == 1:
                                act.wait_ge(*filled(("kv", 1, 3)))
                            nc.scalar.activation(qTv[0:M_HD, c, h, :], bank(("mqT", c, h), 384, slice(0, M_HD)), ACT.Copy,
                                                 scale=M_HD ** -0.5).then_inc(S["act_emptied"], 1)
                        softmax_maps(g)
                    for b in range(4):
                        act.wait_ge(*filled(("gqT", b)))
                        nc.scalar.activation(qTv[:, 0, b, :], bank(("gqT", b), 384), ACT.Copy,
                                             scale=HD ** -0.5).then_inc(S["act_emptied"], 1)
                    softmax_maps("g")
                    act.wait_ge(*filled(("gkT", 1)))
                    for h in range(R_HEADS):
                        nc.scalar.activation(mask[:, h], cview(K_DF, P), ACT.Exp, scale=small[:, 32 + h:33 + h])
                        ins = nc.scalar.activation(maskb[:, h], cview(K_DB, P), ACT.Exp, scale=small[:, 36 + h:37 + h])
                    ins.then_inc(S["masks_raw"], 1)
                    for b in range(4):
                        act.wait_ge(*filled(("dqT", b)))
                        nc.scalar.activation(qTv[:, 1, b, :], bank(("dqT", b), 384), ACT.Copy,
                                             scale=HD ** -0.5).then_inc(S["act_emptied"], 1)
                    m = MAPS["d"]
                    for i in range(len(m) + 2):
                        if i < len(m):
                            n = P * len(keys_of(m[i][2]))
                            for w in range(2):
                                s = (i % 2, 2)[w]
                                r = 2 * (i % 2) + w
                                act.wait_ge(S["max_ready"], MAX_AT[("S1", "S2")[w], *m[i]])
                                if w == 0 and i >= 2:
                                    act.wait_ge(*filled(("PT",) + m[i - 2]))
                                if w == 1 and i >= 1:
                                    act.wait_ge(S["pd_ready"], i)
                                nc.scalar.activation(Pb[:, s * 384:s * 384 + n], bank((("S1", "S2")[w],) + m[i], n), ACT.Exp,
                                                     bias=nmax[:, r:r + 1], scale=1.0,
                                                     accum_out=rsum[:, r:r + 1]).then_inc(S["act_emptied"], 1)
                        if 1 <= i < len(m) + 1:
                            empty_turned(i - 1, m)
                        if i >= 2:
                            key = m[i - 2]
                            act.wait_ge(*filled(("O",) + key))
                            nc.scalar.activation(out_cols(*key), bank(("O",) + key, F_DV), ACT.Copy).then_inc(S["act_emptied"], 1)
                    for b in range(2):
                        act.wait_ge(*filled(("rqT", b)))
                        nc.scalar.activation(qTv[:, 0, b, :], bank(("rqT", b), 384), ACT.Copy).then_inc(S["act_emptied"], 1)
                    for b in range(2):
                        act.wait_ge(*filled(("rkT", b)))
                        nc.scalar.activation(qTv[:, 0, 2 + b, :], bank(("rkT", b), 384), ACT.Copy).then_inc(S["act_emptied"], 1)
                    for h in range(R_HEADS):
                        act.wait_ge(*filled(("qfbT", h)))
                        nc.scalar.activation(qfbT[:, h, :], bank(("qfbT", h), 384), ACT.Copy).then_inc(S["act_emptied"], 1)
                    for t in range(T):
                        act.wait_ge(*filled(("R", t)))
                        nc.scalar.activation(z[:, t, Z_RQ:Z_RQ + 512], bank(("R", t)), ACT.Copy).then_inc(S["act_emptied"], 1)
                    dma(earlier, a["earlier"], "earlier_in")
                    root(24, 2)
                    for n in range(NBR):
                        for c in range(2):
                            for t in range(T):
                                i = (n * 2 + c) * T + t
                                act.wait_ge(*filled(("gl", n, c, t)))
                                if i >= 2:
                                    act.wait_ge(S["dve_emptied"], J.rank[("br", *GATES[i - 2])])
                                if i < 2:
                                    act.wait_ge(S["head_normed"], 1)
                                nc.scalar.activation(gs[i % 2], bank(("gl", n, c, t)), ACT.Sigmoid).then_inc(S["act_emptied"], 1)
                    for k in range(1, KD, 2):
                        act.wait_ge(*filled(("mgT", k)))
                        nc.scalar.activation(hTv[:, k, :], bank(("mgT", k), 384), ACT.Copy).then_inc(S["act_emptied"], 1)
                    for c in range(2):
                        for t in range(T):
                            act.wait_ge(*filled(("out", c, t)))
                            nc.scalar.activation(m_row[:, t, c * C:(c + 1) * C], bank(("out", c, t)), ACT.Copy).then_inc(S["act_emptied"], 1)
                    act.wait_ge(*emptied(("out", 1, T - 1)))
                    square_rows(m_row, merged, "x_squared")
                    root(T, 3)
                    act.wait_ge(S["x_ready"], 1)
                    square_rows(xv, cmpj, "x_squared")
                    root(T, 4)
                    modulated("h2", 1)
                    for t in range(T):
                        act.wait_ge(*filled(("hrow", t, 1)))
                        nc.scalar.activation(xn2[:, t, C:], bank(("hrow", t, 1)), ACT.Copy).then_inc(S["act_emptied"], 1)
                    act.wait_ge(*filled(("route",)))
                    nc.scalar.activation(rt[:, R_EXP], bank(("route",), T * NE).rearrange("p (t e) -> p t e", t=T), ACT.Exp,
                                         scale=-1.0).then_inc(S["act_emptied"], 1)

                    act.dma_start(a["slot_tokens"].rearrange("(p i) o -> p (i o)", i=NT), a["no_tokens"]).then_inc(S["table_reset"], 16)
                    for t in range(T):
                        act.wait_ge(*emptied(("hrow", t, 0)))
                        act.wait_ge(*emptied(("hrow", t, 1)))
                        act.dma_start(a["token_rows"][t * P:(t + 1) * P, :], xn2[:, t, :]).then_inc(S["rows_out"], 16)
                    for t in range(T + 1):
                        if t < T:
                            act.wait_ge(*filled(("gu", "s", t)))
                            nc.scalar.activation(silu[:, t % 2, :], bank(("gu", "s", t), FF), ACT.Silu).then_inc(S["silu_ready"], 1)
                        if t:
                            act.wait_ge(*filled(("aT", "s", t - 1)))
                            nc.scalar.activation(aT[:, (t - 1) % 2].rearrange("p f n -> p (f n)"), bank(("aT", "s", t - 1), FF),
                                                 ACT.Copy).then_inc(S["act_emptied"], 1)
                    for i in range(2):
                        act.wait_ge(*filled(("xt", i, 0)))
                        nc.scalar.activation(xT[:, i, 0:4].rearrange("p k n -> p (k n)"), psum[:, BANK_XT, :], ACT.Copy).then_inc(S["act_emptied"], 1)
                    act.wait_ge(*filled(("gu", 0)))
                    nc.scalar.activation(silu[:, 0, :], psum[:, BANK_GU, 0:FF], ACT.Silu).then_inc(S["silu_ready"], 1)
                    turns = turns_of(act)

                    def steps(turn, last=False):
                        for e in range(2):
                            less = LESS["filled"][e] if last else 0
                            if not last:
                                act.wait_ge(*job_filled(turn, e, "xt0"))
                                nc.scalar.activation(xT[:, e, 0:4].rearrange("p k n -> p (k n)"), psum[:, BANK_XT, :],
                                                     ACT.Copy).then_inc(S["act_emptied"], 1)
                            if not (last and e == 1):
                                act.wait_ge(*job_filled(turn, e, "gu", 2 if last else 0))
                                nc.scalar.activation(silu[:, 1 - e, :], psum[:, BANK_GU + 1 - e, 0:FF], ACT.Silu).then_inc(S["silu_ready"], 1)
                            act.wait_ge(*job_filled(turn, e, "aT", less))
                            nc.scalar.activation(aT[:, e].rearrange("p f n -> p (f n)"), psum[:, BANK_AT, 0:FF],
                                                 ACT.Copy).then_inc(S["act_emptied"], 1)
                            act.wait_ge(*job_filled(turn, e, "y0", less))
                            act.wait_ge(S[f"y_written{e}"], turn * 16 + 16)
                            nc.scalar.activation(yrow[:, e, 0:C], psum[:, BANK_Y, :], ACT.Copy).then_inc(S["act_emptied"], 1)

                    with act.Fori(0, turns - 1) as turn:
                        steps(turn)
                    steps(turns - 1, last=True)
                    act.wait_ge(S["summed"], T * TOPK)
                    square_rows(acc, cmpj, "x_squared")
                    root(T, 5)

                @block.vector
                def _(dve):
                    V = nc.vector
                    link = linker(dve, S["dve_link"])

                    def variance(at, n, count, site):
                        V.tensor_scalar(stat[:, at:at + n], stat[:, at:at + n], 1.0 / count, EPS, ALU.mult,
                                        ALU.add).then_inc(S["var_ready"], 1)
                        one_over_root(n, site)

                    def one_over_root(n, site):
                        dve.wait_ge(S["root_ready"], site + 1)
                        link(V.reciprocal(rs[:, 0:n], rs[:, 0:n]))

                    def empty(key, dst, src):
                        dve.wait_ge(*filled(key))
                        V.tensor_copy(dst, src).then_inc(S["dve_emptied"], 1)

                    dve.wait_ge(S["x_squared"], T)
                    variance(0, T, D, 0)
                    for t in range(T):
                        ins = V.tensor_scalar(xn[:, t], xv[:, t], rs[:, t:t + 1], None, ALU.mult)
                    ins.then_inc(S["xn_ready"], 1)
                    dve.wait_ge(S["bmod_in"], 16)
                    for m in range(12):
                        dve.wait_ge(*filled(("mod", m)))
                        cols = modrow[:, m * C:(m + 1) * C]
                        V.tensor_tensor(cols, cols, bank(("mod", m), C, slice(0, 2)), ALU.add).then_inc(S["dve_emptied"], 1)
                    empty(("modT",), modT[:, :], bank(("modT",), 4 * KD * 2))
                    dve.wait_ge(*emptied(("modT",)))
                    dve.wait_ge(S["params_in"], 16 * N_PARAMS)
                    for n in range(2):
                        g = gpre[:, n * KD:(n + 1) * KD, None].to_broadcast([P, KD, 2])
                        ins = V.scalar_tensor_tensor(modTv[:, 2 * n + 1], modTv[:, 2 * n + 1], 1.0, g, ALU.add, ALU.mult)
                    ins.then_inc(S["modT_ready"], 1)
                    V.scalar_tensor_tensor(small[:, 0:8], rdec[:, :], -1.0, rdec[:, :], ALU.mult, ALU.max).then_inc(S["absx_ready"], 1)
                    dve.wait_ge(S["expx_ready"], 1)
                    V.tensor_scalar(small[:, 16:24], small[:, 8:16], 1.0, None, ALU.add).then_inc(S["u_ready"], 1)
                    dve.wait_ge(S["u_ready"], 1)
                    link(V.scalar_tensor_tensor(small[:, 40:48], small[:, 16:24], -1.0, small[:, 8:16], ALU.add, ALU.subtract))
                    link(V.reciprocal(small[:, 48:56], small[:, 16:24]))
                    link(V.scalar_tensor_tensor(small[:, 40:48], small[:, 40:48], -1.0, small[:, 48:56], ALU.mult, ALU.mult))
                    dve.wait_ge(S["ln_ready"], 1)
                    link(V.tensor_tensor(small[:, 40:48], small[:, 40:48], small[:, 24:32], ALU.add))
                    V.scalar_tensor_tensor(small[:, 32:40], rdec[:, :], 0.0, small[:, 40:48], ALU.min, ALU.subtract).then_inc(S["lg_ready"], 1)
                    lp = lamp[:, :].rearrange("p (q c d) -> p q c d", q=2, c=2)
                    link(V.tensor_tensor(lp[:, :, 0], lp[:, :, 0], lp[:, :, 1], ALU.mult))
                    V.tensor_reduce(lamv[:, 0:2], lp[:, :, 0], AX, ALU.add).then_inc(S["lam_dots"], 1)
                    dve.wait_ge(S["lam_exps"], 1)
                    link(V.tensor_tensor(lamv[:, 4:5], lamv[:, 2:3], lamv[:, 3:4], ALU.subtract))
                    link(V.tensor_tensor(lamv[:, 4:5], lamv[:, 4:5], lamv[:, 6:7], ALU.add))
                    link(V.tensor_scalar(lamv[:, 5:6], lamv[:, 4:5], -1.0, None, ALU.mult))
                    link(V.tensor_scalar(gains[:, GAIN["diff"]], gains[:, GAIN["diff"]], lamv[:, 7:8], None, ALU.mult))
                    dve.wait_ge(S["dec_ready"], 1)
                    link(V.tensor_scalar(dec[:, 8:16], dec[:, 8:16], R_DK ** -0.5, None, ALU.mult))

                    dve.wait_ge(*emptied(("z", "gkv", T - 1)))
                    for t in range(T):
                        for c, (at, n) in enumerate(((Z_CQ, Q_LORA), (Z_CKV, KV_LORA))):
                            j = (t * Q_LORA, T * Q_LORA + t * KV_LORA)[c]
                            v = z[:, t, at:at + n]
                            ins = V.tensor_tensor_reduce(out=kT[:, j:j + n], in0=v, in1=v, scale=1.0, scalar=0.0, op0=ALU.mult,
                                                         op1=ALU.add, accum_out=statv[:, t, c:c + 1])
                    link(ins)
                    heads = G_HEADS + G_KV
                    qk = z[:, :, Z_GQ:Z_GQ + heads * HD]
                    sq = kT[:, 0:T * heads * HD]
                    link(V.tensor_tensor(sq.rearrange("p (t n) -> p t n", t=T), qk, qk, ALU.mult))
                    link(V.tensor_reduce(statv[:, :, 2:12], sq.rearrange("p (t h d) -> p t h d", t=T, d=HD), AX, ALU.add))
                    for a0, a1, count in ((0, 1, Q_LORA), (1, 2, KV_LORA), (2, 12, HD)):
                        ins = V.tensor_scalar(statv[:, :, a0:a1], statv[:, :, a0:a1], 1.0 / count, EPS, ALU.mult, ALU.add)
                    ins.then_inc(S["var_ready"], 1)
                    dve.wait_ge(S["root_ready"], 2)
                    V.reciprocal(rs[:, 0:36], rs[:, 0:36]).then_inc(S["head_rs"], 1)
                    dve.wait_ge(S["head_rs"], 1)
                    for c, (at, n, g, done) in enumerate(((Z_CQ, Q_LORA, "q", "cq_ready"), (Z_CKV, KV_LORA, "kv", "ckv_ready"))):
                        for t in range(T):
                            v = z[:, t, at:at + n]
                            ins = V.scalar_tensor_tensor(v, v, rsv[:, t, c:c + 1], gains[:, GAIN[g]], ALU.mult, ALU.mult)
                        ins.then_inc(S[done], 1)

                    for k in range(3):
                        empty(("cqT", k), cqT[:, k, :], bank(("cqT", k), 384))
                    for k in range(2):
                        empty(("ckvT", k), ckvT[:, k, :], bank(("ckvT", k)))
                    tmp = kT[:, 0:M_ROPE], kT[:, M_ROPE:2 * M_ROPE]
                    for t in (1, 2):
                        v = z[:, t, Z_KPE:Z_KPE + M_ROPE].rearrange("p (h d) -> p h d", h=1)
                        link(rope(V, link, t, v, tmp[t - 1], 1, M_ROPE, K_C32, K_S32))
                    for kt in range(4):
                        src = c_kpe[:, :] if kt == 1 else z[:, (0, None, 1, 2)[kt], Z_KPE:Z_KPE + M_ROPE]
                        ins = V.tensor_copy(kmv[:, kt, :, M_NOPE:], src[:, None, :].to_broadcast([P, HALF, M_ROPE]))
                    ins.then_inc(S["km_ready"], 1)

                    def largest(key):
                        g, h, t = key[1:]
                        i = MAPS[g].index((g, h, t))
                        col = i % 4 if key[0] == "S" else 2 * (i % 2) + (key[0] == "S2")
                        dve.wait_ge(*filled(key))
                        V.tensor_reduce(nmax[:, col:col + 1], bank(key, P * len(keys_of(t))), AX, ALU.max,
                                        negate=True).then_inc(S["max_ready"], 1)

                    def softmax_maps(g):
                        m = MAPS[g]
                        for i in range(len(m) + 3):
                            if i < len(m):
                                largest(("S",) + m[i])
                            if 2 <= i < len(m) + 2 and J.taker[("PT",) + m[i - 2]] == "dve":
                                n = P * len(keys_of(m[i - 2][2]))
                                if i >= 4:
                                    dve.wait_ge(*filled(("O",) + m[i - 4]))
                                s = (i - 2) % 2
                                empty(("PT",) + m[i - 2], PTb[:, s * 384:s * 384 + n], bank(("PT",) + m[i - 2], n))
                            if i >= 3:
                                key, s = m[i - 3], (i - 3) % 4
                                dve.wait_ge(*emptied(("S",) + key))
                                link(V.reciprocal(rrec[:, s:s + 1], rsum[:, s:s + 1]))
                                dve.wait_ge(*filled(("O",) + key))
                                V.tensor_scalar(out_cols(*key), bank(("O",) + key, HD), rrec[:, s:s + 1], None,
                                                ALU.mult).then_inc(S["dve_emptied"], 1)

                    dve.wait_ge(zeros_out, 16)
                    for c, g in enumerate(("ma", "mb")):
                        for kt in range(4):
                            key = ("kv", c, kt)
                            both = bank(key).rearrange("p (h d) -> p h d", h=HALF)
                            dve.wait_ge(*filled(key))
                            V.tensor_copy(kmv[:, kt, :, 0:M_NOPE], both[:, :, 0:M_NOPE])
                            V.tensor_copy(vmv[:, kt, c * HALF:(c + 1) * HALF, :], both[:, :, M_NOPE:]).then_inc(S["dve_emptied"], 1)
                        for t in (1, 2):
                            dve.wait_ge(*emptied(("qm", c, t)))
                            tmp = c_ckv[:, (t - 1) * 128:t * 128]
                            ins = rope(V, link, t, qmv[:, t, :, M_NOPE:], tmp, HALF, M_ROPE, K_C32, K_S32)
                            if t == 1:
                                link(ins)
                        ins.then_inc(S["qm_roped"], 1)
                        for h in range(HALF):
                            empty(("mkT", c, h), kTv[0:M_HD, c, h, :], bank(("mkT", c, h), C, slice(0, M_HD)))
                        if c == 1:
                            dve.wait_ge(S["cache_out"], 16 * 6)
                        softmax_maps(g)

                    for b in range(2):
                        empty(("gkT", b), kTv[:, 0, b, :], bank(("gkT", b)))
                    softmax_maps("g")
                    for dst, at, q in ((qfb, Z_RQ, 0), (kfb, Z_RK, 2)):
                        src = z[:, :, at:at + R_HEADS * R_DK].rearrange("p t (h d) -> p t h d", h=R_HEADS)
                        for f in range(2):
                            decay = dec[:, None, 4 * (q + f):4 * (q + f) + 4, None].to_broadcast([P, T, R_HEADS, R_DK])
                            ins = V.tensor_tensor(dst[:, :, :, f, :], src, decay, ALU.mult)
                    ins.then_inc(S["qkfb_ready"], 1)
                    chunk = dec[:, 16:20, None].to_broadcast([P, R_HEADS, R_DV])
                    dve.wait_ge(S["masks_raw"], 1)
                    link(V.tensor_tensor(mask, mask, const[:, None, K_MF:K_MF + P].to_broadcast([P, R_HEADS, P]), ALU.mult))
                    link(V.tensor_tensor(maskb, maskb, const[:, None, K_MB:K_MB + P].to_broadcast([P, R_HEADS, P]), ALU.mult))
                    link(V.tensor_tensor(mask, mask, maskb, ALU.add))
                    link(V.tensor_scalar(kdup[:, 0:512], kdup[:, 0:512], R_DK ** -0.5, None, ALU.mult))
                    for b in range(4):
                        empty(("dkT", b), kTv[:, 1, b, :], bank(("dkT", b)))
                    m = MAPS["d"]

                    def difference(i):
                        n = P * len(keys_of(m[i][2]))
                        r = 2 * (i % 2)
                        p1, p2 = Pb[:, (i % 2) * 384:(i % 2) * 384 + n], Pb[:, 768:768 + n]
                        dve.wait_ge(*emptied(("S2",) + m[i]))
                        link(V.reciprocal(rrec[:, r:r + 2], rsum[:, r:r + 2]))
                        link(V.tensor_scalar(rrec[:, r + 1:r + 2], rrec[:, r + 1:r + 2], lamv[:, 5:6], None, ALU.mult))
                        link(V.tensor_scalar(p2, p2, rrec[:, r + 1:r + 2], None, ALU.mult))
                        V.scalar_tensor_tensor(p1, p1, rrec[:, r:r + 1], p2, ALU.mult, ALU.add).then_inc(S["pd_ready"], 1)

                    for i in range(len(m) + 1):
                        if i < len(m):
                            largest(("S1",) + m[i])
                            largest(("S2",) + m[i])
                        if i >= 1:
                            difference(i - 1)
                    link(V.tensor_tensor(state1, state0v, chunk, ALU.mult))
                    link(V.tensor_copy(state2, state0v))
                    empty(("KV", 0), state_ctx[:, :], bank(("KV", 0)))
                    dve.wait_ge(*filled(("KV", 1)))
                    V.tensor_tensor(state2[0:64], state1[0:64], psum[0:64, J.bank(("KV", 1)), :].rearrange("p (h v) -> p h v", h=R_HEADS),
                                    ALU.add).then_inc(S["dve_emptied"], 1)
                    dve.wait_ge(*filled(("KV", 2)))
                    V.tensor_tensor(state1[64:128], state1[64:128], psum[64:128, J.bank(("KV", 2)), :].rearrange("p (h v) -> p h v", h=R_HEADS),
                                    ALU.add).then_inc(S["dve_emptied"], 1)
                    dve.wait_ge(*emptied(("KV", 2)))
                    V.tensor_copy(state1[0:64], state0v[0:64]).then_inc(S["state_ready"], 1)
                    for t in range(T):
                        for odd in range(2):
                            key = ("A", t, odd)
                            dve.wait_ge(*filled(key))
                            V.tensor_tensor(AT[t][:, odd::2], bank(key, 2 * P).rearrange("p (h n) -> p h n", h=2), mask[:, odd::2],
                                            ALU.mult).then_inc(S["dve_emptied"], 1)

                    def heads_of(at):
                        return z[:, :, at:at + 512].rearrange("p t (h d) -> p t h d", d=128)

                    def per_head(v):
                        return v.rearrange("p (t h) -> p t h", t=T)

                    ro, do = heads_of(Z_RQ), heads_of(Z_DQ)
                    dve.wait_ge(*emptied(("R", T - 1)))
                    link(V.tensor_reduce(per_head(mu[:, :]), ro, AX, ALU.add))
                    link(V.tensor_scalar(mu[:, :], mu[:, :], 1.0 / R_DV, None, ALU.mult))
                    link(V.tensor_tensor(ro, ro, per_head(mu[:, :])[:, :, :, None].to_broadcast([P, T, 4, 128]), ALU.subtract))
                    for n, v in enumerate((ro, do)):
                        s4 = kT[:, n * 1536:(n + 1) * 1536].rearrange("p (t h d) -> p t h d", t=T, h=4)
                        link(V.tensor_tensor(s4, v, v, ALU.mult))
                        link(V.tensor_reduce(per_head(stat[:, 12 * n:12 * n + 12]), s4, AX, ALU.add))
                    variance(0, 24, 128, 2)
                    for n, v in enumerate((ro, do)):
                        link(V.tensor_tensor(v, v, per_head(rs[:, 12 * n:12 * n + 12])[:, :, :, None].to_broadcast([P, T, 4, 128]), ALU.mult))
                    rr = z[:, :, Z_RQ:Z_RQ + 512]
                    link(V.tensor_tensor(rr, rr, gains[:, None, GAIN["ret"]].to_broadcast([P, T, 512]), ALU.mult))
                    link(V.tensor_tensor(rr, rr, z[:, :, Z_RG:Z_RG + 512], ALU.mult))
                    V.tensor_tensor(do, do, gains[:, None, None, GAIN["diff"]].to_broadcast([P, T, 4, 128]), ALU.mult).then_inc(S["head_normed"], 1)
                    dve.wait_ge(S["head_normed"], 1)

                    for n in range(NBR):
                        for k in range(4):
                            empty(("oT", n, k), oT[:, k, :], bank(("oT", n, k), 384))
                        for c in range(2):
                            for t in range(T):
                                i = GATES.index((n, c, t))
                                dst = merged[:, t, c * C:(c + 1) * C]
                                dve.wait_ge(*emptied(("gl", n, c, t)))
                                dve.wait_ge(*filled(("br", n, c, t)))
                                V.tensor_tensor(dst if n == 0 else gtmp, bank(("br", n, c, t)), gs[i % 2],
                                                ALU.mult).then_inc(S["dve_emptied"], 1)
                                dve.wait_ge(*emptied(("br", n, c, t)))
                                if n:
                                    link(V.tensor_tensor(dst, dst, gtmp, ALU.add))
                    V.tensor_copy(mu[:, 0:1], merged[:, 0, 0:1]).then_inc(S["merged_ready"], 1)
                    for k in range(0, KD, 2):
                        empty(("mgT", k), hTv[:, k, :], bank(("mgT", k), 384))

                    def residual(rows_m, n, site):
                        dve.wait_ge(S["gates_in"], 48 * (n + 1))
                        for v in range(2):
                            ins = V.tensor_tensor(gp[:, v], gp[:, v], gpost, ALU.mult)
                        link(ins)
                        dve.wait_ge(S["x_squared"], T * (2 if n == 0 else 4))
                        variance(0, T, D, site)
                        for t in range(T):
                            ins = V.scalar_tensor_tensor(rows_m[:, t], rows_m[:, t], rs[:, t:t + 1], gp[:, min(t, 1)], ALU.mult, ALU.mult)
                        link(ins)
                        V.tensor_tensor(xv, xv, rows_m, ALU.add).then_inc(S["x_ready"], 1)
                        dve.wait_ge(S["x_ready"], n + 1)

                    residual(m_row, 0, 3)
                    dve.wait_ge(S["x_squared"], 3 * T)
                    variance(0, T, D, 4)
                    for t in range(T):
                        ins = V.tensor_scalar(xn2[:, t], xv[:, t], rs[:, t:t + 1], None, ALU.mult)
                    ins.then_inc(S["xn_ready"], 1)
                    for t in range(T):
                        empty(("hrow", t, 0), xn2[:, t, 0:C], bank(("hrow", t, 0)))
                    dve.wait_ge(*emptied(("route",)))
                    link(V.tensor_scalar(rt[:, R_SC], rt[:, R_EXP], 1.0, None, ALU.add))
                    link(V.reciprocal(rt[:, R_SC], rt[:, R_SC]))
                    link(V.tensor_tensor(rt[:, R_SEL], rt[:, R_SC], brt[:, None, :].to_broadcast([P, T, NE]), ALU.add))
                    for t in range(T):
                        for g in range(NG):
                            ins = V.max(rt[:, R_TOP, t, g * EG:(g + 1) * EG], rt[:, R_SEL, t, g * EG:(g + 1) * EG])
                    link(ins)
                    top = rt[:, R_TOP].rearrange("p t (g e) -> p t g e", g=NG)
                    grp = rt[:, R_GRP, :, 0:NG]
                    link(V.tensor_tensor(grp, top[:, :, :, 0], top[:, :, :, 1], ALU.add))
                    dve.wait_ge(S["earlier_in"], 16)

                    def rank(v, dst, n):
                        c1, c2 = cmp1[:, :, 0:n, 0:n], cmp2[:, :, 0:n, 0:n]
                        vj, vi = v[:, :, None, :].to_broadcast([P, T, n, n]), v[:, :, :, None].to_broadcast([P, T, n, n])
                        link(V.tensor_tensor(c2, vj, vi, ALU.is_equal))
                        link(V.tensor_tensor(c2, c2, before[:, None, 0:n, 0:n].to_broadcast([P, T, n, n]), ALU.mult))
                        link(V.tensor_tensor(c1, vj, vi, ALU.is_gt))
                        link(V.tensor_tensor(c1, c1, c2, ALU.add))
                        link(V.tensor_reduce(dst, c1, AX, ALU.add))

                    gr = rt[:, R_GRP, :, NG:2 * NG]
                    gm = rt[:, R_GRP, :, 2 * NG:3 * NG]
                    go = rt[:, R_GRP, :, 3 * NG:4 * NG]
                    rank(grp, gr, NG)
                    link(V.tensor_scalar(gm, gr, float(TOPG), None, ALU.is_lt))
                    link(V.tensor_scalar(go, gm, -1.0, 1e30, ALU.add, ALU.mult))
                    sel4 = rt[:, R_SEL].rearrange("p t (g e) -> p t g e", g=NG)
                    ms4 = rt[:, R_MSEL].rearrange("p t (g e) -> p t g e", g=NG)
                    link(V.tensor_tensor(ms4, sel4, gm[:, :, :, None].to_broadcast([P, T, NG, EG]), ALU.mult))
                    link(V.tensor_tensor(ms4, ms4, go[:, :, :, None].to_broadcast([P, T, NG, EG]), ALU.add))
                    rank(rt[:, R_MSEL], rt[:, R_RANK], NE)
                    chosen = rt[:, R_TOP]
                    V.tensor_scalar(chosen, rt[:, R_RANK], float(TOPK), None, ALU.is_lt).then_inc(S["chosen_ready"], 1)
                    dve.wait_ge(S["chosen_ready"], 1)
                    link(V.tensor_tensor(rt[:, R_COMB], rt[:, R_SC], chosen, ALU.mult))
                    link(V.tensor_reduce(mu[:, 0:3], rt[:, R_COMB], AX, ALU.add))
                    link(V.reciprocal(mu[:, 0:3], mu[:, 0:3]))
                    link(V.scalar_tensor_tensor(rt[:, R_COMB], rt[:, R_COMB], ROUTE_SCALE,
                                                mu[:, 0:3, None].to_broadcast([P, T, NE]), ALU.mult, ALU.mult))

                    def product(gu, s, n):
                        dve.wait_ge(S["silu_ready"], n)
                        V.tensor_tensor(av[:, s], psum[:, gu, FF:2 * FF], silu[:, s], ALU.mult).then_inc(S["dve_emptied"], 1)

                    product(J.bank(("gu", "s", 0)), 0, 1)
                    product(J.bank(("gu", "s", 1)), 1, 2)
                    for c in range(2):
                        empty(("y", "s", 0, c), acc[:, 0, c * C:(c + 1) * C], bank(("y", "s", 0, c)))
                    product(J.bank(("gu", "s", 2)), 0, 3)
                    for c in range(2):
                        empty(("y", "s", 1, c), acc[:, 1, c * C:(c + 1) * C], bank(("y", "s", 1, c)))
                    counts = bank(("place",), (T + 1) * NE).rearrange("p (t e) -> p t e", t=T + 1)
                    row_more, row_base, row_end = (rt[:, R_ROW, i] for i in range(3))
                    pos, slot, tmp = rt[:, R_POS], rt[:, R_SLOT], rt[:, R_TMP]
                    dve.wait_ge(*filled(("place",)))
                    link(V.tensor_scalar(pos, counts[:, 0:T], -1.0, None, ALU.add))
                    link(V.tensor_scalar(row_base, counts[:, T], float(2 * P), None, ALU.is_gt))
                    V.scalar_tensor_tensor(row_more, counts[:, T], float(P), row_base, ALU.is_gt, ALU.add).then_inc(S["dve_emptied"], 1)
                    dve.wait_ge(*emptied(("place",)))
                    link(V.tensor_tensor_scan(row_end, row_more, row_more, 0.0, ALU.add, ALU.max))
                    link(V.tensor_tensor(row_base, row_end, row_more, ALU.subtract))
                    q1, q2 = rt[:, R_GRP], rt[:, R_EXP]
                    link(V.tensor_scalar(q1, pos, float(P), None, ALU.is_ge))
                    link(V.tensor_scalar(q2, pos, float(2 * P), None, ALU.is_ge))
                    link(V.scalar_tensor_tensor(slot, pos, float(NT), iota[:, None, :].to_broadcast([P, T, NE]), ALU.mult, ALU.add))
                    link(V.scalar_tensor_tensor(rt[:, R_SEL, 0], row_base, float(NE - P * NT), iota, ALU.add, ALU.subtract))
                    link(V.tensor_tensor(tmp, q1, rt[:, R_SEL, 0:1].to_broadcast([P, T, NE]), ALU.mult))
                    link(V.tensor_tensor(slot, slot, tmp, ALU.add))
                    link(V.scalar_tensor_tensor(slot, q2, float(1 - P * NT), slot, ALU.mult, ALU.add))
                    hot = zf[:, 11776:11776 + T * TOPK * NE].rearrange("p (t k e) -> p t k e", t=T, k=TOPK)
                    val = zf[:, 12288:12288 + T * TOPK * NE].rearrange("p (t k e) -> p t k e", t=T, k=TOPK)
                    for k in range(TOPK):
                        ins = V.tensor_scalar(hot[:, :, k], rt[:, R_RANK], float(k), None, ALU.is_equal)
                    link(ins)
                    for src, dst in ((slot, slot_f), (rt[:, R_COMB], weight)):
                        link(V.tensor_tensor(val, hot, src[:, :, None, :].to_broadcast([P, T, TOPK, NE]), ALU.mult))
                        link(V.tensor_reduce(dst.rearrange("p (t k) -> p t k", t=T), val, AX, ALU.add))
                    for t in range(T):
                        ins = V.tensor_scalar(token_f[:, t:t + 1], const[:, K_POS + 3:K_POS + 4], float(t * P), None, ALU.add)
                    link(ins)
                    V.tensor_copy(token_u, token_f)
                    V.tensor_copy(slot_u, slot_f).then_inc(S["slots_ready"], 1)
                    within = zf[:, 12800:12800 + NE * (MORE + 1)].rearrange("p (j e) -> p j e", e=NE)
                    below = zf[:, 13312:13312 + NE * (MORE + 1)].rearrange("p (j e) -> p j e", e=NE)
                    shape = [P, MORE + 1, NE]
                    j = iota[:, 0:MORE + 1, None].to_broadcast(shape)
                    link(V.tensor_tensor(within, row_base[:, None, :].to_broadcast(shape), j, ALU.is_le))
                    link(V.tensor_tensor(below, row_end[:, None, :].to_broadcast(shape), j, ALU.is_gt))
                    link(V.tensor_tensor(within, within, below, ALU.mult))
                    link(V.tensor_tensor(within, within, iota[:, None, :].to_broadcast(shape), ALU.mult))
                    link(V.tensor_copy(expert_f[:, 0:NE], iota))
                    link(V.tensor_reduce(expert_f[:, NE:NT], within, AX, ALU.add))
                    link(V.tensor_scalar(tmp[:, 0, 0:6], iota[:, 0:12:2], row_end[:, NE - 1:NE], None, ALU.is_lt))
                    link(V.tensor_reduce(turns_f, tmp[:, 0, 0:6], AX, ALU.add))
                    link(V.tensor_scalar(turns_f, turns_f, float(NE // 2), None, ALU.add))
                    V.tensor_copy(expert_u, expert_f)
                    V.tensor_copy(turns_u, turns_f).then_inc(S["tables_ready"], 1)
                    for c in range(2):
                        empty(("y", "s", 2, c), acc[:, 2, c * C:(c + 1) * C], bank(("y", "s", 2, c)))
                    dve.wait_ge(S["tables_ready"], 1)
                    for i in range(2):
                        empty(("xt", i, 1), xT[:, i, 4:8].rearrange("p k n -> p (k n)"), psum[:, BANK_XT + 1, :])
                    product(BANK_GU, 0, T + 1)
                    turns = turns_of(dve)

                    def steps(turn, last=False):
                        for e in range(2):
                            less = LESS["filled"][e] if last else 0
                            if not last:
                                dve.wait_ge(*job_filled(turn, e, "xt1"))
                                V.tensor_copy(xT[:, e, 4:8].rearrange("p k n -> p (k n)"), psum[:, BANK_XT + 1, :]).then_inc(S["dve_emptied"], 1)
                            if not (last and e == 1):
                                product(BANK_GU + 1 - e, 1 - e, turn * 2 + e + T + 2)
                            dve.wait_ge(*job_filled(turn, e, "y1", less))
                            dve.wait_ge(S[f"y_written{e}"], turn * 16 + 16)
                            V.tensor_copy(yrow[:, e, C:], psum[:, BANK_Y + 1, :]).then_inc(S["dve_emptied"], 1)

                    with dve.Fori(0, turns - 1) as turn:
                        steps(turn)
                    steps(turns - 1, last=True)
                    for i in range(T * TOPK):
                        dve.wait_ge(S[f"y_landed{i % 6}"], 16 * (i // 6 + 1))
                        V.scalar_tensor_tensor(acc[:, i // TOPK], ybuf[:, i % 6], weight[:, i:i + 1], acc[:, i // TOPK], ALU.mult,
                                               ALU.add).then_inc(S["summed"], 1)
                        dve.wait_ge(S["summed"], i + 1)
                    residual(acc, 1, 5)

                @block.tensor
                def _(pe):
                    def bank_free(key):
                        if J.before[key] is not None:
                            pe.wait_ge(*emptied(J.before[key]))

                    def multiply(key, dst, pairs):
                        for i, (lhsT, rhs) in enumerate(pairs):
                            ins = nc.tensor.matmul(dst, lhsT, rhs, start=(i == 0), stop=(i == len(pairs) - 1))
                        return ins

                    def turn_rows(key, sources, n=P):
                        bank_free(key)
                        for i, src in enumerate(sources):
                            ins = nc.tensor.transpose(psum[0:n, J.bank(key), i * P:(i + 1) * P], src, ident)
                        ins.then_inc(S["psum_filled"], 1)

                    def project(key, t, w, at, n, k_tiles, src=hTv):
                        bank_free(key)
                        multiply(key, bank(key, n), [(src[:, k, t * P:(t + 1) * P], w[:, k, at:at + n])
                                                     for k in range(k_tiles)]).then_inc(S["psum_filled"], 1)

                    for m in range(12):
                        pe.wait_ge(*landed(("mod", m)))
                        w = weights(("mod", m), KD, C)
                        bank_free(("mod", m))
                        multiply(("mod", m), bank(("mod", m), C, slice(0, 2)),
                                 [(silTv[:, k, :], w[:, k, :]) for k in range(KD)]).then_inc(S["psum_filled"], 1)
                    pe.wait_ge(*emptied(("mod", 11)))
                    for q, at in enumerate((0, D, 3 * D, 4 * D)):
                        for k in range(KD):
                            col = (q * KD + k) * 2
                            ins = nc.tensor.transpose(psum[:, J.bank(("modT",)), col:col + 2], modrow[:, at + k * P:at + (k + 1) * P],
                                                      const[0:2, K_ID:K_ID + 2])
                    ins.then_inc(S["psum_filled"], 1)
                    pe.wait_ge(S["xn_ready"], 1)
                    for k in range(KD):
                        turn_rows(("h1", k), [xn[:, t, k * P:(k + 1) * P] for t in range(T)])
                    pe.wait_ge(*emptied(("h1", KD - 1)))
                    for s in SEGS:
                        pe.wait_ge(*landed(("z", s)))
                        n = SEG[s][1]
                        for t in range(T):
                            project(("z", s, t), t, weights(("z", s), KD, n), 0, n, KD)
                    pe.wait_ge(S["cq_ready"], 1)
                    for k in range(3):
                        turn_rows(("cqT", k), [z[:, t, Z_CQ + k * P:Z_CQ + (k + 1) * P] for t in range(T)])
                    pe.wait_ge(S["ckv_ready"], 1)
                    pe.wait_ge(S["params_in"], 16 * N_PARAMS)
                    for k in range(2):
                        turn_rows(("ckvT", k), [tile_rows(c_ckv, Z_CKV, KV_LORA, kt)[:, k * P:(k + 1) * P] for kt in range(4)])
                    pe.wait_ge(*landed(("uq",)))
                    pe.wait_ge(*landed(("ukv",)))

                    def softmax_maps(g):
                        m = MAPS[g]
                        for i in range(len(m) + 3):
                            if i < len(m):
                                key = ("S",) + m[i]
                                bank_free(key)
                                multiply(key, bank(key, P * len(keys_of(m[i][2]))), [(queries(*m[i]), keys(*m[i]))]).then_inc(S["psum_filled"], 1)
                            if 2 <= i < len(m) + 2:
                                j = i - 2
                                pe.wait_ge(*emptied(("S",) + m[j]))
                                base = (j % 3) * 384
                                turn_rows(("PT",) + m[j], [Pb[:, base + b * P:base + (b + 1) * P] for b in range(len(keys_of(m[j][2])))])
                            if i >= 3:
                                weigh_values(m[i - 3], (i - 3) % 2)

                    def weigh_values(mp, s):
                        key = ("O",) + mp
                        g, h, t = mp
                        bank_free(key)
                        pe.wait_ge(*emptied(("PT",) + mp))
                        multiply(key, bank(key, F_DV if g == "d" else HD),
                                 [(PTb[:, s * 384 + b * P:s * 384 + (b + 1) * P], values(g, h, kt))
                                  for b, kt in enumerate(keys_of(t))]).then_inc(S["psum_filled"], 1)

                    for c, g in enumerate(("ma", "mb")):
                        if c == 0:
                            pe.wait_ge(*emptied(("cqT", 2)))
                        uq = weights(("uq",), 3, M_HEADS * M_HD)
                        ukv = weights(("ukv",), 2, D)
                        for t in range(T):
                            project(("qm", c, t), t, uq, c * 384, 384, 3, cqT)
                        if c == 0:
                            pe.wait_ge(*emptied(("ckvT", 1)))
                        for kt in range(4):
                            project(("kv", c, kt), kt, ukv, c * C, C, 2, ckvT)
                        pe.wait_ge(S["km_ready"], 1)
                        pe.wait_ge(*emptied(("kv", c, 3)))
                        for h in range(HALF):
                            turn_rows(("mkT", c, h), [kmv[:, kt, h, :] for kt in range(4)], M_HD)
                        pe.wait_ge(S["qm_roped"], c + 1)
                        pe.wait_ge(*emptied(("qm", c, 2)))
                        for h in range(HALF):
                            turn_rows(("mqT", c, h), [qmv[:, t, h, :] for t in range(T)], M_HD)
                        pe.wait_ge(*emptied(("mkT", c, HALF - 1)))
                        pe.wait_ge(*emptied(("mqT", c, HALF - 1)))
                        softmax_maps(g)
                    pe.wait_ge(S["kdup_ready"], 1)
                    for b in range(4):
                        turn_rows(("gqT", b), [z[:, t, Z_GQ + b * P:Z_GQ + (b + 1) * P] for t in range(T)])
                    for b in range(2):
                        turn_rows(("gkT", b), [kdv[:, kt, b].rearrange("p c d -> p (c d)") for kt in range(4)])
                    pe.wait_ge(*emptied(("gqT", 3)))
                    pe.wait_ge(*emptied(("gkT", 1)))
                    softmax_maps("g")
                    pe.wait_ge(S["diff_roped"], 1)
                    for b in range(4):
                        turn_rows(("dqT", b), [z[:, t, Z_DQ + b * P:Z_DQ + (b + 1) * P] for t in range(T)])
                    for b in range(4):
                        turn_rows(("dkT", b), [tile_rows(c_dk, Z_DK, 512, kt)[:, b * P:(b + 1) * P] for kt in range(4)])
                    pe.wait_ge(*emptied(("dqT", 3)))
                    pe.wait_ge(*emptied(("dkT", 3)))
                    m = MAPS["d"]
                    for i in range(len(m) + 2):
                        if i < len(m):
                            _, h, t = m[i]
                            cols = slice(0, P) if t == 0 else slice(P, 4 * P)
                            for s in range(2):
                                half = slice(64 * s, 64 * s + 64)
                                key = (("S1", "S2")[s],) + m[i]
                                bank_free(key)
                                multiply(key, bank(key, P * len(keys_of(t))), [(qTv[half, 1, h, t * P:(t + 1) * P], kTv[half, 1, h, cols])]
                                         ).then_inc(S["psum_filled"], 1)
                        if 1 <= i < len(m) + 1:
                            j = i - 1
                            pe.wait_ge(S["pd_ready"], j + 1)
                            base = (j % 2) * 384
                            turn_rows(("PT",) + m[j], [Pb[:, base + b * P:base + (b + 1) * P] for b in range(len(keys_of(m[j][2])))])
                        if i >= 2:
                            weigh_values(m[i - 2], (i - 2) % 2)
                    for b in range(2):
                        turn_rows(("rqT", b), [z[:, t, Z_RQ + b * P:Z_RQ + (b + 1) * P] for t in range(T)])
                    for b in range(2):
                        turn_rows(("rkT", b), [z[:, t, Z_RK + b * P:Z_RK + (b + 1) * P] for t in range(T)])
                    pe.wait_ge(S["qkfb_ready"], 1)
                    for h in range(R_HEADS):
                        turn_rows(("qfbT", h), [qfb[:, t, h].rearrange("p f d -> p (f d)") for t in range(T)])

                    def retained(t, h):
                        return z[:, t, Z_RV + h * R_DV:Z_RV + (h + 1) * R_DV]

                    def part(key, h):
                        return psum[:, J.bank(key), h * P:(h + 1) * P]

                    for t in range(T):
                        bank_free(("KV", t))
                        for h in range(R_HEADS):
                            ins = multiply(("KV", t), part(("KV", t), h), [(kfb[:, t, h].rearrange("p f d -> p (f d)"), retained(t, h))])
                        ins.then_inc(S["psum_filled"], 1)
                    pe.wait_ge(*emptied(("rkT", 1)))
                    for t in range(T):
                        for odd in range(2):
                            key = ("A", t, odd)
                            bank_free(key)
                            for pair in range(2):
                                half, cols = slice(64 * odd, 64 * odd + 64), slice(t * P, (t + 1) * P)
                                ins = multiply(key, part(key, pair), [(qTv[half, 0, 2 + pair, cols], qTv[half, 0, pair, cols])])
                            ins.then_inc(S["psum_filled"], 1)
                    pe.wait_ge(*emptied(("qfbT", R_HEADS - 1)))
                    pe.wait_ge(S["state_ready"], 1)
                    for t in range(T):
                        bank_free(("R", t))
                        pe.wait_ge(*emptied(("A", t, 1)))
                        for h in range(R_HEADS):
                            pairs = [(AT[t][:, h, :], retained(t, h))]
                            if t:
                                pairs.append((qfbT[:, h, t * P:(t + 1) * P], (state1, state2)[t - 1][:, h, :]))
                            ins = multiply(("R", t), part(("R", t), h), pairs)
                        ins.then_inc(S["psum_filled"], 1)
                    for n in range(NBR):
                        pe.wait_ge(S["head_normed"], 1)
                        for k in range(4):
                            turn_rows(("oT", n, k), [z[:, t, OUT_COLS[n] + k * P:OUT_COLS[n] + (k + 1) * P] for t in range(T)])
                        for c in range(2):
                            pe.wait_ge(*landed(("gl", n, c)))
                            pe.wait_ge(*landed(("br", n, c)))
                            for t in range(T):
                                project(("gl", n, c, t), t, weights(("gl", n, c), KD, C), 0, C, KD)
                                if c == 0 and t == 0:
                                    pe.wait_ge(*emptied(("oT", n, 3)))
                                project(("br", n, c, t), t, weights(("br", n, c), 4, C), 0, C, 4, oT)
                    pe.wait_ge(S["merged_ready"], 1)
                    for k in range(KD):
                        turn_rows(("mgT", k), [merged[:, t, k * P:(k + 1) * P] for t in range(T)])
                    pe.wait_ge(*emptied(("mgT", KD - 2)))
                    pe.wait_ge(*emptied(("mgT", KD - 1)))
                    for c in range(2):
                        pe.wait_ge(*landed(("out", c)))
                        for t in range(T):
                            project(("out", c, t), t, weights(("out", c), KD, C), 0, C, KD)
                    pe.wait_ge(S["xn_ready"], 2)
                    for k in range(KD):
                        turn_rows(("h2", k), [xn2[:, t, k * P:(k + 1) * P] for t in range(T)])
                    pe.wait_ge(*emptied(("h2", KD - 1)))
                    for t in range(T):
                        for c in range(2):
                            turn_rows(("hrow", t, c), [hTv[:, 4 * c + k, t * P:(t + 1) * P] for k in range(4)])
                    bank_free(("route",))
                    for t in range(T):
                        ins = multiply(("route",), psum[:, J.bank(("route",)), t * NE:(t + 1) * NE],
                                       [(hTv[:, k, t * P:(t + 1) * P], wr[:, k * NE:(k + 1) * NE]) for k in range(KD)])
                    ins.then_inc(S["psum_filled"], 1)

                    def turn_product(dst, s):
                        for f in range(2):
                            ins = nc.tensor.transpose(psum[:, dst, f * P:(f + 1) * P], av[:, s, f * P:(f + 1) * P], ident)
                        ins.then_inc(S["psum_filled"], 1)

                    def down(dst, s, w, c):
                        multiply(None, psum[:, dst, :], [(aT[:, s, f, :], expert_dn(w)[:, f, c * C:(c + 1) * C]) for f in range(2)]
                                 ).then_inc(S["psum_filled"], 1)

                    def shared_gate_up(t):
                        bank_free(("gu", "s", t))
                        multiply(None, bank(("gu", "s", t)), [(hTv[:, k, t * P:(t + 1) * P], expert_gu(1)[:, k, :]) for k in range(KD)]
                                 ).then_inc(S["psum_filled"], 1)

                    pe.wait_ge(S["gu_landed1"], 16)
                    shared_gate_up(0)
                    pe.wait_ge(S["dn_landed1"], 16)
                    for t in range(T):
                        if t == T - 1:
                            pe.wait_ge(S["chosen_ready"], 1)
                            pe.wait_ge(S["ones_ready"], 1)
                            bank_free(("place",))
                            chosen = rt[:, R_TOP]
                            for q in range(T + 1):
                                pairs = [(ones, chosen[:, b, :]) for b in range(min(q, T))]
                                if q < T:
                                    pairs.append((cview(K_MF, P), chosen[:, q, :]))
                                ins = multiply(None, psum[:, J.bank(("place",)), q * NE:(q + 1) * NE], pairs)
                            ins.then_inc(S["psum_filled"], 1)
                        if t + 1 < T:
                            shared_gate_up(t + 1)
                        pe.wait_ge(*emptied(("gu", "s", t)))
                        bank_free(("aT", "s", t))
                        turn_product(J.bank(("aT", "s", t)), t % 2)
                        pe.wait_ge(*emptied(("aT", "s", t)))
                        for c in range(2):
                            bank_free(("y", "s", t, c))
                            down(J.bank(("y", "s", t, c)), t % 2, 1, c)

                    def turn_gathered(s):
                        for h in range(2):
                            for k in range(4):
                                ins = nc.tensor.transpose(psum[:, BANK_XT + h, k * P:(k + 1) * P], xg[:, s, (4 * h + k) * P:(4 * h + k + 1) * P], ident)
                            ins.then_inc(S["psum_filled"], 1)

                    def gate_up(s):
                        multiply(None, psum[:, BANK_GU + s, :], [(xT[:, s, k, :], expert_gu(s)[:, k, :]) for k in range(KD)]
                                 ).then_inc(S["psum_filled"], 1)

                    for i in range(2):
                        pe.wait_ge(S[f"x_landed{i}"], 16)
                        for h in range(2):
                            bank_free(("xt", i, h))
                        turn_gathered(i)
                    pe.wait_ge(*emptied(("xt", 0, 0)))
                    pe.wait_ge(*emptied(("xt", 0, 1)))
                    pe.wait_ge(S["gu_landed0"], 16)
                    bank_free(("gu", 0))
                    gate_up(0)
                    pe.wait_ge(S["act_emptied"], J.taken["act"])
                    pe.wait_ge(S["dve_emptied"], J.taken["dve"])
                    turns = turns_of(pe)

                    def steps(turn, last=False):
                        for e in range(2):
                            less = {"act": LESS["act"][e], "dve": LESS["dve"][e]} if last else {"act": 0, "dve": 0}
                            before = previous(turn, e)
                            gone = (1 if last and e == 1 else 0)
                            if not last:
                                pe.wait_ge(S[f"x_landed{e}"], turn * 16 + 32)
                                pe.wait_ge(*job_emptied(*before, "xt0"))
                                pe.wait_ge(*job_emptied(*before, "xt1"))
                                turn_gathered(e)
                            if not (last and e == 1):
                                if last:
                                    pe.wait_ge(*job_emptied(*before, "xt0"))
                                    pe.wait_ge(*job_emptied(*before, "xt1"))
                                pe.wait_ge(S[f"gu_landed{1 - e}"], turn * 16 + 32)
                                gate_up(1 - e)
                            pe.wait_ge(*job_emptied(*before, "gu", gone))
                            pe.wait_ge(*job_emptied(*before, "aT", gone))
                            turn_product(BANK_AT, e)
                            pe.wait_ge(*job_emptied(turn, e, "aT", less["act"]))
                            pe.wait_ge(S[f"dn_landed{e}"], turn * 16 + 16 * (e + 1))
                            pe.wait_ge(*job_emptied(*before, "y0", gone))
                            down(BANK_Y, e, e, 0)
                            pe.wait_ge(*job_emptied(*before, "y1", gone))
                            down(BANK_Y + 1, e, e, 1)

                    with pe.Fori(0, turns - 1) as turn:
                        steps(turn)
                    steps(turns - 1, last=True)

            nc.gpsimd.dma_reset(range(sems[0].num, sems[-1].num + 1))
            nc.gpsimd.sem_clear(range(sems[0].num, sems[-1].num + 1))
            nc.all_engine_barrier()

        with nc.Block() as block:
            @block.sync
            def _(sp):
                sp.dma_start(a["outs"]["y_prompt"][0], xv[:, 0, :]).then_inc(y_out, 16)
                sp.dma_start(a["outs"]["y_sample"][0].rearrange("(t p) n -> p t n", p=P), xv[:, 1:3, :]).then_inc(y_out, 16)
                sp.wait_ge(y_out, 32)


INPUTS = ["x_prompt", "x_sample", "cache_mla_ckv", "cache_mla_kpe", "cache_gqa_k", "cache_gqa_v", "cache_diff_k",
          "cache_diff_v", "state_ret", "c", "c_ctx", "w_mod", "b_mod", "g_pre1", "g_post1", "g_pre2", "g_post2", "w_in",
          "g_mla_q", "w_mla_uq", "g_mla_kv", "w_mla_ukv", "g_gqa_q", "g_gqa_k", "ret_decay", "g_ret", "diff_lambda",
          "g_diff", "w_br", "w_out", "w_router", "b_router", "w_exp_gu", "w_exp_down", "w_sh_gu", "w_sh_down"]
OUTPUTS = [("y_prompt", (1, P, D)), ("y_sample", (1, 2 * P, D)), ("mla_ckv", (1, DEPTH, P, KV_LORA)),
           ("mla_kpe", (1, DEPTH, P, M_ROPE)), ("gqa_k", (1, DEPTH, P, G_KV, HD)), ("gqa_v", (1, DEPTH, P, G_KV, HD)),
           ("diff_k", (1, DEPTH, P, F_HEADS, 2, HD)), ("diff_v", (1, DEPTH, P, F_HEADS, F_DV)),
           ("state_ret", (1, DEPTH, 2, R_HEADS, R_DK, R_DV))]


def kernel(**inputs):
    import concourse.bacc as bacc
    from concourse.bass_utils import run_bass_kernel_spmd

    nc = bacc.Bacc("TRN2", target_bir_lowering=False, num_devices=1)
    consts, earlier, lam_init = constants()
    no_tokens = np.ascontiguousarray(np.broadcast_to(np.arange(P, dtype=np.uint32)[:, None], (P, NT)))
    arrays = {name: np.ascontiguousarray(inputs[name]) for name in INPUTS}
    arrays.update(consts=consts, earlier=earlier, lam_init=lam_init, no_tokens=no_tokens)
    a = {name: nc.dram_tensor(f"in_{name}", v.shape, U32 if name == "no_tokens" else F32, kind="ExternalInput").ap() for name, v in arrays.items()}
    a["gate_rows"] = nc.dram_tensor("gate_rows", (2, 2, D), F32, kind="Internal").ap()
    a["token_rows"] = nc.dram_tensor("token_rows", (T * P, D), F32, kind="Internal").ap()
    a["y_slots"] = nc.dram_tensor("y_slots", (P * NT, D), F32, kind="Internal").ap()
    a["slot_tokens"] = nc.dram_tensor("slot_tokens", (P * NT, 1), U32, kind="Internal").ap()
    a["outs"] = {name: nc.dram_tensor(f"out_{name}", shape, F32, kind="ExternalOutput").ap() for name, shape in OUTPUTS}
    trunk(nc, a)
    r = run_bass_kernel_spmd(nc, [{f"in_{name}": v for name, v in arrays.items()}], core_ids=[0])
    return tuple(r.results[0][f"out_{name}"] for name, _ in OUTPUTS)
```

```python
import math
from contextlib import ExitStack

import numpy as np

import concourse.bass as bass
from concourse import mybir

P = 128
D = 1024
KD = D // P
T = 3
DEPTH = 2
F32 = mybir.dt.float32
U32 = mybir.dt.uint32
F32R = mybir.dt.float32r
ALU = mybir.AluOpType
ACT = mybir.ActivationFunctionType
AX = mybir.AxisListType.X
EPS = 1e-6
C = 512

Q_LORA, KV_LORA, M_ROPE, M_NOPE, M_V, M_HEADS = 384, 256, 32, 64, 64, 8
M_HD = M_NOPE + M_ROPE
HALF = M_HEADS // 2
HD, G_HEADS, G_KV = 64, 8, 2
R_HEADS, R_DK, R_DV = 4, 64, 128
F_HEADS, F_DV = 4, 128
NE, TOPK, NG, TOPG, FF = 32, 4, 4, 2, 256
EG = NE // NG
ROUTE_SCALE = 2.5
NBR = 4

SEG = {}
_at = 0
for _name, _n in (("cq", Q_LORA), ("ckv", KV_LORA + M_ROPE), ("gq", G_HEADS * HD), ("gkv", 2 * G_KV * HD),
                  ("rqk", 2 * R_HEADS * R_DK), ("rv", R_HEADS * R_DV), ("rg", R_HEADS * R_DV),
                  ("dq", F_HEADS * 2 * HD), ("dk", F_HEADS * 2 * HD), ("dv", F_HEADS * F_DV)):
    SEG[_name] = (_at, _n)
    _at += _n
ZC = _at
SEGS = list(SEG)
Z_CQ, Z_CKV, Z_KPE = 0, Q_LORA, Q_LORA + KV_LORA
Z_GQ, Z_GK = SEG["gq"][0], SEG["gkv"][0]
Z_GV = Z_GK + G_KV * HD
Z_RQ = SEG["rqk"][0]
Z_RK = Z_RQ + R_HEADS * R_DK
Z_RV, Z_RG = SEG["rv"][0], SEG["rg"][0]
Z_DQ, Z_DK, Z_DV = SEG["dq"][0], SEG["dk"][0], SEG["dv"][0]
OUT_COLS = [Z_CQ, Z_GQ, Z_RQ, Z_DQ]
Z_MERGED = Z_DK
Z_M = Z_RV

GAIN = {}
_at = 0
for _name, _n in (("q", Q_LORA), ("kv", KV_LORA), ("gq", HD), ("gk", HD), ("ret", R_HEADS * R_DV), ("diff", F_DV)):
    GAIN[_name] = slice(_at, _at + _n)
    _at += _n
GAINS = _at

K_ID, K_DF, K_DB, K_MF, K_MB, K_C64 = 0, 128, 256, 384, 512, 640
K_S64, K_C32, K_S32, K_POS, K_IOTA, K_EPS, K_N = 768, 896, 960, 1024, 1028, 1060, 1061
RANK_COLS = NE * NE


def constants():
    k = np.zeros((P, K_N), np.float32)
    k[:, K_ID:K_ID + P] = np.eye(P)
    j, i = np.meshgrid(np.arange(P), np.arange(P), indexing="ij")
    k[:, K_DF:K_DF + P] = np.maximum(i - j, 0)
    k[:, K_DB:K_DB + P] = np.maximum(j - i, 0)
    k[:, K_MF:K_MF + P] = i >= j
    k[:, K_MB:K_MB + P] = j >= i
    n = np.arange(2 * P)
    for d, at_c, at_s in ((64, K_C64, K_S64), (32, K_C32, K_S32)):
        quarter = d // 4
        freq = np.float32(10000.0) ** (-np.arange(quarter, dtype=np.float32) / np.float32(quarter))
        cos = np.zeros((2 * P, 2, 2, quarter), np.float32)
        sin = np.zeros_like(cos)
        for a, pos in enumerate((n // 64, n % 64)):
            ang = pos.astype(np.float32)[:, None] * freq[None]
            cos[:, a] = np.cos(ang)[:, None]
            sin[:, a, 0], sin[:, a, 1] = -np.sin(ang), np.sin(ang)
        for t in range(2):
            k[:, at_c + t * d:at_c + (t + 1) * d] = cos[t * P:(t + 1) * P].reshape(P, d)
            k[:, at_s + t * d:at_s + (t + 1) * d] = sin[t * P:(t + 1) * P].reshape(P, d)
    p = np.arange(P)
    k[:, K_POS:K_POS + 4] = np.stack([p + 1, P - p, P - 1 - p, p], 1)
    k[:, K_IOTA:K_IOTA + NE] = np.arange(NE)
    k[:, K_EPS] = EPS
    earlier = np.broadcast_to((np.arange(NE)[None, :] < np.arange(NE)[:, None]).reshape(1, -1), (P, NE * NE))
    lam = np.zeros((DEPTH, P, 2), np.float32)
    for layer in range(DEPTH):
        init = 0.8 - 0.6 * math.exp(-0.3 * layer)
        lam[layer] = [init, 1.0 - init]
    return k, np.ascontiguousarray(earlier.astype(np.float32)), lam


class PsumJobs:

    def __init__(self):
        self.number, self.taker, self.rank, self.banks, self.before = {}, {}, {}, {}, {}
        self.taken = {"act": 0, "dve": 0}
        self.last = {}

    def add(self, key, taker, bank=None):
        assert key not in self.number
        self.number[key] = len(self.number)
        self.taker[key] = taker
        self.taken[taker] += 1
        self.rank[key] = self.taken[taker]
        self.banks[key] = self.number[key] % 8 if bank is None else bank
        self.before[key] = self.last.get(self.banks[key])
        self.last[self.banks[key]] = key

    def filled(self, key):
        return self.number[key] + 1

    def bank(self, key):
        return self.banks[key]


def attention_maps():
    maps = {}
    for g, heads in (("ma", HALF), ("mb", HALF), ("g", G_HEADS), ("d", F_HEADS)):
        maps[g] = [(g, h, t) for h in range(heads) for t in range(T)]
    return maps


MAPS = attention_maps()
TURNED_NEXT = {"ma": [[]] * 4,
               "mb": [[("gqT", 0), ("gkT", 0)], [("gqT", 1), ("gkT", 1)], [("gqT", 2)], [("gqT", 3)]],
               "g": [[("dqT", b), ("dkT", b)] for b in range(4)],
               "d": [[("rqT", 0)], [("rqT", 1)], [("rkT", 0)], [("rkT", 1)]]}


def plan_jobs():
    jobs = PsumJobs()
    for m in range(12):
        jobs.add(("mod", m), "dve")
    jobs.add(("modT",), "dve")
    for k in range(KD):
        jobs.add(("h1", k), "act")
    for s in SEGS:
        for t in range(T):
            jobs.add(("z", s, t), "act")
    for k in range(3):
        jobs.add(("cqT", k), "dve")
    for k in range(2):
        jobs.add(("ckvT", k), "dve")

    def turned_next(g, step):
        for key in TURNED_NEXT[g][step]:
            jobs.add(key, "dve" if key[0] in ("gkT", "dkT") else "act")

    def softmax_maps(g):
        m = MAPS[g]
        for i in range(len(m) + 4):
            if i < len(m):
                jobs.add(("S",) + m[i], "act")
            if i >= 4:
                jobs.add(("O",) + m[i - 4], "dve")
            if 2 <= i < len(m) + 2:
                jobs.add(("PT",) + m[i - 2], "act" if i % 2 else "dve")
            if i >= len(m):
                turned_next(g, i - len(m))

    for c, g in enumerate(("ma", "mb")):
        for t in range(T):
            jobs.add(("qm", c, t), "act")
        for kt in range(4):
            jobs.add(("kv", c, kt), "dve")
        for h in range(HALF):
            jobs.add(("mkT", c, h), "dve")
        for h in range(HALF):
            jobs.add(("mqT", c, h), "act")
        softmax_maps(g)
    softmax_maps("g")
    m = MAPS["d"]
    for i in range(len(m) + 4):
        if i < len(m):
            jobs.add(("S1",) + m[i], "act")
            jobs.add(("S2",) + m[i], "act")
        if i >= 4:
            jobs.add(("O",) + m[i - 4], "act")
        if 2 <= i < len(m) + 2:
            jobs.add(("PT",) + m[i - 2], "act")
        if i >= len(m):
            turned_next("d", i - len(m))
    for h in range(R_HEADS):
        jobs.add(("qfbT", h), "act")
    for t in range(T):
        jobs.add(("KV", t), "dve")
    for t in range(T):
        for odd in range(2):
            jobs.add(("A", t, odd), "dve")
    for t in range(T):
        jobs.add(("R", t), "act")
    for n in range(NBR):
        for k in range(4):
            jobs.add(("oT", n, k), "dve")
        for c in range(2):
            for t in range(T):
                jobs.add(("gl", n, c, t), "act")
            if (n, c) == (NBR - 1, 1):
                for k in range(KD // 2):
                    jobs.add(("mgT", k), "dve")
            for t in range(T):
                jobs.add(("br", n, c, t), "dve")
    for k in range(KD // 2, KD):
        jobs.add(("mgT", k), "dve")
    for c in range(2):
        for t in range(T):
            jobs.add(("out", c, t), "act")
    for k in range(KD):
        jobs.add(("h2", k), "act")
    for t in range(T):
        for c in range(2):
            jobs.add(("hrow", t, c), "act" if c else "dve")
    jobs.add(("route",), "act")
    for t in range(T):
        jobs.add(("gu", "s", t), "dve")
    jobs.add(("place",), "act")
    for t in range(T):
        jobs.add(("aT", "s", t), "act")
        jobs.add(("y", "s", t, 0), "dve")
        jobs.add(("y", "s", t, 1), "dve")
    for i in range(2):
        for h in range(2):
            jobs.add(("xt", i, h), ("act", "dve")[h], BANK_XT + h)
    jobs.add(("gu", 0), "dve", BANK_GU)
    return jobs


CAP = 96
CHOICES = T * P * TOPK
MORE = (CHOICES - 1) // (CAP + 1)
TILES_MAX = T * P // CAP
assert TILES_MAX == 4 and MORE % 2
NT = NE + MORE + 1
BANK_XT, BANK_GU, BANK_AT, BANK_Y = 0, 2, 4, 5
STEP = (("xt0", "act"), ("xt1", "dve"), ("gu", "dve"), ("aT", "act"), ("y0", "act"), ("y1", "dve"))
TURN_JOBS, TURN_TAKEN = 2 * len(STEP), 6
JOBS = plan_jobs()

SLOTS = 3
SLOT = KD * C
RAW, HIGHS = 4, 2
PIECE = 4 * C
SPLITS = [("z", s, h) for s in SEGS for h in range(2)]
Z_PIECES = len(SPLITS)
PIECES = SPLITS + [(w, c) for c in range(2) for w in ("uq", "ukv")]
_gates = [p for n in range(NBR) for c in range(2) for p in (("gl", n, c, 0), ("gl", n, c, 1), ("br", n, c, 0))]
_out = [("out", c, h) for c in range(2) for h in range(2)]
SPLITS, PIECES = SPLITS + _gates + _out, PIECES + _gates + _out
OUT_PIECES = len(SPLITS) - len(_out)
PIECE_AT = {key: i for i, key in enumerate(PIECES)}
SPLIT_AT = {key: i for i, key in enumerate(SPLITS)}
FIRST_HALVES = [key for key in SPLITS if key[-1] == 0 and key[0] != "br"]

MAX_AT = {}
for _g in ("ma", "mb", "g", "d"):
    for _m in MAPS[_g]:
        for _key in ((("S1", *_m), ("S2", *_m)) if _g == "d" else (_m,)):
            MAX_AT[_key] = len(MAX_AT) + 1
GATES = [(n, c, t) for n in range(NBR) for c in range(2) for t in range(T)]
N_PARAMS = 21
POST, PRE = 24, 27



def trunk(nc, a):
    J = JOBS
    with ExitStack() as ctx:
        def sb(name, n, parts=P):
            return ctx.enter_context(nc.sbuf_tensor(name, [parts, n], F32))

        def sb_twice(name, n):
            at = -(-nc.sbuf_base // 32) * 32
            return sb(name, n), nc.alloc_sbuf_tensor_at(f"{name}_split", [P, n], F32R, offset=at)

        const = sb("const", K_N)
        x = sb("x", T * D)
        hT, hTr = sb_twice("hT", KD * T * P)
        zf = sb("zf", 13824)
        W, Wr = sb_twice("W", SLOTS * SLOT)
        silT = sb("silT", KD * 2)
        gains = sb("gains", GAINS)
        wr = sb("wr", KD * NE)
        brt = sb("brt", NE)
        gpre = sb("gpre", 2 * KD)
        modT = sb("modT", 4 * KD * 2)
        lamp = sb("lamp", 4 * HD)
        lamv = sb("lamv", 8)
        rdec = sb("rdec", 8)
        small = sb("small", 64)
        mu = sb("mu", 12)
        rrec = sb("rrec", 10)

        stat = sb("stat", 36)
        rs = sb("rs", 36)
        dec = sb("dec", 32)
        scratch, scratchr = sb_twice("scratch", 7 * HALF * M_HD + (G_HEADS + G_KV) * HD)
        km = scratch[:, 0:4 * HALF * M_HD]
        qm = scratch[:, 4 * HALF * M_HD:7 * HALF * M_HD]
        rtmp = scratch[:, 7 * HALF * M_HD:]
        vm = sb("vm", 4 * M_HEADS * M_V)
        qT, qTr = sb_twice("qT", 2 * 4 * T * P)
        kT, kTr = sb_twice("kT", 2 * 4 * 4 * P)
        Pb = sb("Pb", 3 * T * P)
        PTb = sb("PTb", 2 * T * P)
        nmax = sb("nmax", 6)
        rsum = sb("rsum", 8)
        c_ckv = sb("c_ckv", KV_LORA)
        c_kpe = sb("c_kpe", M_ROPE)
        c_gk = sb("c_gk", G_KV * HD)
        c_gv = sb("c_gv", G_KV * HD)
        c_dk = sb("c_dk", 2 * F_HEADS * HD)
        c_dv = sb("c_dv", F_HEADS * F_DV)
        state0 = sb("state0", R_HEADS * R_DV)
        kdup = sb("kdup", 4 * G_KV * 2 * HD)
        psum = ctx.enter_context(nc.psum_tensor("psum", [P, 8, C], F32))

        names = ["psum_filled", "act_emptied", "dve_emptied", "act_link", "dve_link", "pool_link"]
        names += ["params_in", "bmod_in", "x_squared", "var_ready", "root_ready", "xn_ready", "modT_ready", "gates_out",
                  "gates_in", "h_split"]
        names += ["absx_ready", "expx_ready", "u_ready", "ln_ready", "lg_ready", "dec_ready", "dec_scaled", "lam_dots",
                  "lam_exps"]
        names += ["halves_used", "high_ready", "low_ready"]
        names += ["head_rs", "cq_ready", "ckv_ready", "km_ready", "qm_roped", "kdup_ready", "diff_roped", "max_ready",
                  "pd_ready", "cache_out"]
        names += ["qkfb_ready", "masks_raw", "mask_ready", "state_ready", "mean_ready", "ret_squared", "branch_rs",
                  "head_normed"]
        names += ["oT_high", "merged_ready", "mgT_high", "post_root", "pre_root", "x_ready", "mixture_rows"]
        names += ["earlier_in", "ones_ready", "chosen_ready", "slots_ready", "tables_ready", "table_reset", "slots_out",
                  "table_in", "rows_out", "zeros_ready", "zeros_out"]
        names += ["silu_ready", "summed", "sp_steps", "gathers"]
        names += [f"{n}{i}" for n in ("x_landed", "y_written", "index_copied", "gu_landed", "dn_landed") for i in range(2)]
        names += [f"y_landed{i}" for i in range(6)]
        names += [f"mod_landed{i}" for i in range(SLOTS)] + [f"piece_landed{i}" for i in range(RAW)]
        sems = [nc.alloc_semaphore(n) for n in names]
        S = dict(zip(names, sems))
        const_in = nc.alloc_semaphore("const_in")
        silc_in = nc.alloc_semaphore("silc_in")
        silc_ready = nc.alloc_semaphore("silc_ready")
        y_out = nc.alloc_semaphore("y_out")

        def cview(at, n):
            return const[:, at:at + n]

        ident = cview(K_ID, P)
        xv = x[:, :].rearrange("p (t n) -> p t n", t=T)
        hTv = hT[:, :].rearrange("p (k n) -> p k n", k=KD)
        z = zf[:, 0:T * ZC].rearrange("p (t n) -> p t n", t=T)
        modrow = zf[0:2, 0:6 * D]
        xn = zf[:, 6 * D:9 * D].rearrange("p (t n) -> p t n", t=T)
        junk = zf[:, 9 * D:12 * D].rearrange("p (t n) -> p t n", t=T)
        silTv = silT[:, :].rearrange("p (k v) -> p k v", v=2)
        modTv = modT[:, :].rearrange("p (q k v) -> p q k v", q=4, v=2)
        qmv = qm[:, :].rearrange("p (t h d) -> p t h d", t=T, h=HALF)
        kmv = km[:, :].rearrange("p (t h d) -> p t h d", t=4, h=HALF)
        vmv = vm[:, :].rearrange("p (t h d) -> p t h d", t=4, h=M_HEADS)
        qTv = qT[:, :].rearrange("p (s b n) -> p s b n", s=2, b=4)
        kTv = kT[:, :].rearrange("p (s b n) -> p s b n", s=2, b=4)
        rsv = rs[:, :].rearrange("p (t n) -> p t n", t=T)
        statv = stat[:, :].rearrange("p (t n) -> p t n", t=T)
        kdv = kdup[:, :].rearrange("p (t k c d) -> p t k c d", t=4, k=G_KV, c=2)
        cqT = kT[:, 2048:2048 + 3 * T * P].rearrange("p (k n) -> p k n", k=3)
        ckvT = qT[:, 1536:1536 + 2 * 4 * P].rearrange("p (k n) -> p k n", k=2)
        qfb = vm[:, 0:T * R_HEADS * 2 * R_DK].rearrange("p (t h f d) -> p t h f d", t=T, h=R_HEADS, f=2)
        kfb = km[:, :].rearrange("p (t h f d) -> p t h f d", t=T, h=R_HEADS, f=2)
        qfbT = kTv[:, 0].rearrange("p b n -> p (b n)")[:, 0:4 * T * P].rearrange("p (h n) -> p h n", h=4)
        state1 = kTv[:, 0].rearrange("p b n -> p (b n)")[:, 1536:2048].rearrange("p (h v) -> p h v", h=R_HEADS)
        state2 = vm[:, 1536:2048].rearrange("p (h v) -> p h v", h=R_HEADS)
        state0v = state0[:, :].rearrange("p (h v) -> p h v", h=R_HEADS)
        state_ctx = c_dk
        mask = kdup[:, 0:512].rearrange("p (h n) -> p h n", h=R_HEADS)
        AT = [r.rearrange("p (h n) -> p h n", h=R_HEADS) for r in (PTb[:, 0:512], Pb[:, 0:512], Pb[:, 512:1024])]
        maskb = kdup[:, 512:1024].rearrange("p (h n) -> p h n", h=R_HEADS)
        first_map = Pb[:, :].rearrange("p (s n) -> p s n", s=3)
        second_map = qm[:, 0:2 * T * P].rearrange("p (s n) -> p s n", s=2)
        def split_rows(high, low, k):
            return [v.rearrange("p (k n) -> p k n", k=k) for v in (high, low)]

        N8 = KD * T * P
        h_split_z = split_rows(qTr[:, 0:N8], kTr[:, 0:N8], KD)
        h_split_gates = split_rows(scratchr[:, 0:N8], hTr[:, :], KD)
        merged_split = split_rows(hTr[:, :], scratchr[:, 0:N8], KD)
        oT_split = split_rows(qTr[:, 0:N8 // 2], qTr[:, N8 // 2:N8], 4)
        gs = [kTv[:, 0, i] for i in range(4)]
        gtmp = kTv[:, 1, 3]
        zero_row = kT[:, 2560:2560 + D]
        gp = kT[:, 0:2 * D].rearrange("p (v n) -> p v n", v=2)
        gpost = kT[:, 2 * D:3 * D]
        merged = z[:, :, Z_MERGED:Z_MERGED + D]
        m_row = z[:, :, Z_M:Z_M + D]
        acc = zf[:, 0:3 * D].rearrange("p (t n) -> p t n", t=T)
        xn2 = zf[:, 3 * D:6 * D].rearrange("p (t n) -> p t n", t=T)
        av = zf[:, 6144:6656].rearrange("p (s n) -> p s n", s=2)
        silu = zf[:, 6656:7168].rearrange("p (s n) -> p s n", s=2)
        aT = zf[:, 7168:7168 + 4 * CAP].rearrange("p (s f n) -> p s f n", s=2, f=2)
        shared = zf[:, 6144:6912].rearrange("p (t n) -> p t n", t=T)
        shared_T = zf[:, 6912:7680].rearrange("p (t f n) -> p t f n", t=T, f=2)
        cmp1 = zf[:, 7680:10752].rearrange("p (t i j) -> p t i j", t=T, i=NE)
        cmp2 = zf[:, 10752:13824].rearrange("p (t i j) -> p t i j", t=T, i=NE)
        cmpj = zf[:, 7680:10752].rearrange("p (t n) -> p t n", t=T)
        xg = zf[:, 7680:9728].rearrange("p (s n) -> p s n", s=2)
        xT = zf[:, 9728:9728 + 2 * KD * CAP].rearrange("p (s k n) -> p s k n", s=2, k=KD)
        yrow = zf[:, 11776:13824].rearrange("p (s n) -> p s n", s=2)
        ybuf = zf[:, 7680:13824].rearrange("p (s n) -> p s n", s=6)
        slot_f, weight, slot_u = vm[:, 1024:1036], vm[:, 1036:1048], vm[:, 1048:1060].bitcast(U32)
        token_f, token_u = vm[:, 1060:1063], vm[:, 1063:1066].bitcast(U32)
        tokens = vm[:, 1068:1068 + NT].bitcast(U32)
        index = vm[:, 1120:1122].bitcast(U32)
        expert_f, expert_u = vm[:, 1124:1124 + NT], vm[:, 1172:1172 + NT].bitcast(U32)
        turns_f, turns_u = vm[:, 1220:1221], vm[:, 1221:1222].bitcast(U32)
        ones = vm[:, 1232:1360]
        counted = vm[:, 1360:1360 + (T + 1) * NE]
        iota = const[:, K_IOTA:K_IOTA + NE]
        earlier = vm[:, 0:RANK_COLS]
        before = earlier.rearrange("p (i j) -> p i j", i=NE)
        rt = Pb[:, :].rearrange("p (s t e) -> p s t e", s=12, t=T)
        R_EXP, R_SC, R_SEL, R_RANK, R_COMB, R_MSEL, R_TOP, R_GRP, R_POS, R_SLOT, R_TMP, R_ROW = range(12)

        def mod_weights(m):
            at = m % SLOTS * SLOT
            return W[:, at:at + SLOT].rearrange("p (k n) -> p k n", k=KD)

        def piece_size(key):
            return {"uq": (3, HALF * M_HD), "ukv": (2, C)}.get(key[0], (4, SEG[key[1]][1] if key[0] == "z" else C))

        def piece(key, tensor=W):
            k, n = piece_size(key)
            at = PIECE_AT[key] % RAW * PIECE
            return tensor[:, at:at + k * n].rearrange("p (k n) -> p k n", k=k)

        def high(j, tensor=Wr):
            k, n = piece_size(SPLITS[j])
            at = (RAW + j % HIGHS) * PIECE
            return tensor[:, at:at + k * n].rearrange("p (k n) -> p k n", k=k)

        def piece_used(key):
            if key in FIRST_HALVES:
                return S["halves_used"], FIRST_HALVES.index(key) + 1
            return filled({"uq": ("qm", key[1], T - 1), "ukv": ("kv", key[1], 3)}.get(key[0], (*key[:-1], T - 1)))

        def expert_gu(s):
            return W[:, s * SLOT:(s + 1) * SLOT].rearrange("p (k n) -> p k n", k=KD)

        def expert_dn(s):
            return W[:, 2 * SLOT + s * SLOT // 2:2 * SLOT + (s + 1) * SLOT // 2].rearrange("p (k n) -> p k n", k=2)

        def landed(key):
            if key[0] == "mod":
                return S[f"mod_landed{key[1] % SLOTS}"], 16 * (key[1] // SLOTS + 1)
            return S[f"piece_landed{PIECE_AT[key] % RAW}"], 16 * (PIECE_AT[key] // RAW + 1)

        def filled(key):
            return S["psum_filled"], J.filled(key)

        def emptied(key):
            return S["act_emptied" if J.taker[key] == "act" else "dve_emptied"], J.rank[key]

        def bank(key, n=C, parts=slice(0, P)):
            return psum[parts, J.bank(key), 0:n]

        def rows(ap, l):
            r = ap[bass.ds(l, 1)]
            n = len(ap.shape)
            if n == 2:
                return r.rearrange("o n -> (o n)")
            return r.rearrange("o a b -> (o a) b") if n == 3 else r.rearrange("o a b c -> (o a) b c")

        def spread(ap1):
            return ap1.partition_broadcast(P)

        def in_turn(turn, e, name):
            order = [(i, n) for i in range(2) for n, _ in STEP]
            at = order.index((e, name))
            taker = dict(STEP)[name]
            rank = sum(dict(STEP)[n] == taker for _, n in order[:at + 1])
            return (len(J.number) + at + 1 + turn * TURN_JOBS,
                    S["act_emptied" if taker == "act" else "dve_emptied"], J.taken[taker] + rank + turn * TURN_TAKEN)

        def job_filled(turn, e, name, less=0):
            return S["psum_filled"], in_turn(turn, e, name)[0] - less

        def job_emptied(turn, e, name, less=0):
            _, sem, n = in_turn(turn, e, name)
            return sem, n - less

        def previous(turn, e):
            return (turn, 0) if e == 1 else (turn - 1, 1)

        LESS = {"filled": (2, 5), "act": (1, 2), "dve": (1, 3)}

        def turns_of(eng):
            eng.wait_ge(S["tables_ready"], 1)
            return eng.value_load(turns_u[0:1, 0:1], min_val=NE // 2, max_val=NT // 2)

        def linker(eng, sem):
            n = [0]

            def link(ins):
                n[0] += 1
                ins.then_inc(sem, 1)
                eng.wait_ge(sem, n[0])
            return link

        def rope(eng, link, t, v, tmp, heads, d, at_c, at_s):
            q = d // 4
            cos = cview(at_c + (t - 1) * d, d)
            sin = cview(at_s + (t - 1) * d, d).rearrange("p (a j i) -> p a j i", a=2, j=2)
            v4 = v.rearrange("p h (a j i) -> p h a j i", a=2, j=2)
            tm = tmp[:, 0:heads * d].rearrange("p (h d) -> p h d", d=d)
            t4 = tm.rearrange("p h (a j i) -> p h a j i", a=2, j=2)
            for j in range(2):
                ins = eng.tensor_tensor(t4[:, :, :, j, :], v4[:, :, :, 1 - j, :],
                                        sin[:, None, :, j, :].to_broadcast([P, heads, 2, q]), ALU.mult)
            link(ins)
            link(eng.tensor_tensor(v, v, cos[:, None, :].to_broadcast([P, heads, d]), ALU.mult))
            return eng.tensor_tensor(v, v, tm, ALU.add)

        def tile_rows(cache, col, n, kt):
            return cache[:, 0:n] if kt == 1 else z[:, (0, None, 1, 2)[kt], col:col + n]

        def keys_of(t):
            return (0,) if t == 0 else (1, 2, 3)

        def queries(g, h, t):
            if g in ("ma", "mb"):
                return qTv[0:M_HD, 0 if g == "ma" else 1, h, t * P:(t + 1) * P]
            return qTv[64 * (h % 2):64 * (h % 2) + 64, 0, h // 2, t * P:(t + 1) * P]

        def keys(g, h, t):
            cols = slice(0, P) if t == 0 else slice(P, 4 * P)
            if g in ("ma", "mb"):
                return kTv[0:M_HD, 0 if g == "ma" else 1, h, cols]
            return kTv[64 * (h % 2):64 * (h % 2) + 64, 0, h // (G_HEADS // G_KV), cols]

        def values(g, h, kt):
            if g in ("ma", "mb"):
                return vmv[:, kt, h + (HALF if g == "mb" else 0), :]
            if g == "g":
                return tile_rows(c_gv, Z_GV, P, kt)[:, HD * (h // 4):HD * (h // 4) + HD]
            return tile_rows(c_dv, Z_DV, 4 * P, kt)[:, F_DV * h:F_DV * (h + 1)]

        def out_cols(g, h, t):
            if g in ("ma", "mb"):
                h = h + (HALF if g == "mb" else 0)
                return z[:, t, Z_CQ + M_V * h:Z_CQ + M_V * (h + 1)]
            if g == "g":
                return z[:, t, Z_GQ + HD * h:Z_GQ + HD * (h + 1)]
            return z[:, t, Z_DQ + F_DV * h:Z_DQ + F_DV * (h + 1)]

        with nc.Block() as block:
            @block.sync
            def _(sp):
                sp.dma_start(silTv[:, :, 0], a["c_ctx"].rearrange("(k p) -> p k", p=P), allow_slow_non_contiguous=True).then_inc(silc_in, 16)
                sp.dma_start(silTv[:, :, 1], a["c"][0].rearrange("(k p) -> p k", p=P), allow_slow_non_contiguous=True).then_inc(silc_in, 16)

            @block.scalar
            def _(act):
                act.dma_start(const[:, :], a["consts"]).then_inc(const_in, 16)
                act.dma_start(xv[:, 0, :], a["x_prompt"][0]).then_inc(const_in, 16)
                act.dma_start(xv[:, 1:3, :], a["x_sample"][0].rearrange("(t p) n -> p t n", p=P)).then_inc(const_in, 16)
                act.wait_ge(silc_in, 32)
                nc.scalar.activation(silT[:, :], silT[:, :], ACT.Silu).then_inc(silc_ready, 1)

        with nc.Fori(0, DEPTH) as l:
            with nc.Block() as block:
                @block.sync
                def _(sp):
                    for m in range(12):
                        if m >= SLOTS:
                            sp.wait_ge(*filled(("mod", m - SLOTS)))
                        sp.dma_start(mod_weights(m), rows(a["w_mod"], l)[:, m * C:(m + 1) * C].rearrange("(k p) n -> p k n", p=P)
                                     ).then_inc(landed(("mod", m))[0], 16)

                    def source(key):
                        kind, c = key[0], key[-2]
                        if kind in ("uq", "ukv"):
                            n = piece_size(key)[1]
                            return rows(a["w_mla_" + kind], l)[:, key[1] * n:(key[1] + 1) * n]
                        half = slice(key[-1] * 4 * P, (key[-1] + 1) * 4 * P)
                        if kind == "z":
                            at, n = SEG[key[1]]
                            return rows(a["w_in"], l)[half, at:at + n]
                        if kind == "gl":
                            at = ZC + key[1] * D + c * C
                            return rows(a["w_in"], l)[half, at:at + C]
                        if kind == "br":
                            return rows(a["w_br"], l)[key[1]][:, c * C:(c + 1) * C]
                        return rows(a["w_out"], l)[half, c * C:(c + 1) * C]

                    for i, key in enumerate(PIECES):
                        sp.wait_ge(*(piece_used(PIECES[i - RAW]) if i >= RAW else filled(("mod", 9 + i // 2))))
                        sp.dma_start(piece(key), source(key).rearrange("(k p) n -> p k n", p=P)).then_inc(landed(key)[0], 16)

                    def load_gate_up(s, src):
                        sp.dma_start(expert_gu(s), src.rearrange("(k p) n -> p k n", p=P)).then_inc(S[f"gu_landed{s}"], 16)

                    def load_down(s, src):
                        sp.dma_start(expert_dn(s), src.rearrange("(k p) n -> p k n", p=P)).then_inc(S[f"dn_landed{s}"], 16)

                    def expert(name, e):
                        return a[name].rearrange("l e d n -> (l e) d n")[bass.ds(l * NE + e, 1)].rearrange("o d n -> (o d) n")

                    sp.wait_ge(*filled(("out", 1, T - 1)))
                    load_gate_up(1, rows(a["w_sh_gu"], l))
                    load_down(1, rows(a["w_sh_down"], l))
                    load_gate_up(0, expert("w_exp_gu", 0))
                    load_down(0, expert("w_exp_down", 0))
                    sp.wait_ge(*filled(("gu", "s", T - 1)))
                    load_gate_up(1, expert("w_exp_gu", 1))
                    sp.wait_ge(*filled(("y", "s", T - 1, 1)))
                    load_down(1, expert("w_exp_down", 1))
                    sp.wait_ge(*filled(("gu", 0)))
                    load_gate_up(0, expert("w_exp_gu", 2))
                    for e in range(2):
                        sp.sem_inc(S[f"y_written{e}"], 16)
                    turns = turns_of(sp)

                    def write_rows(turn, e, less=(0, 0)):
                        sp.wait_ge(*job_emptied(turn, e, "y0", less[0]))
                        sp.sem_inc(S["sp_steps"], 1)
                        sp.wait_ge(*job_emptied(turn, e, "y1", less[1]))
                        sp.sem_inc(S["sp_steps"], 1)
                        dst = a["y_slots"].rearrange("(p i) n -> p i n", i=NT)[:, bass.ds(turn * 2 + e, 1), :].rearrange("p o n -> p (o n)")
                        sp.dma_start(dst, yrow[0:CAP, e, :]).then_inc(S[f"y_written{e}"], 16)

                    def expert_of(tile):
                        sp.sem_inc(S["sp_steps"], 1)
                        return sp.value_load(expert_u[0:1, bass.ds(tile, 1)], min_val=0, max_val=NE - 1)

                    def steps(turn, last=False):
                        for e in range(2):
                            tile = turn * 2 + e
                            if not (last and e == 1):
                                sp.wait_ge(*job_filled(turn, e, "gu"))
                                load_gate_up(1 - e, expert("w_exp_gu", expert_of(tile + 3)))
                            sp.wait_ge(*job_filled(turn, e, "y1"))
                            load_down(e, expert("w_exp_down", expert_of(tile + 2)))
                            write_rows(turn, e)

                    with sp.Fori(0, turns - 2) as turn:
                        steps(turn)
                    steps(turns - 2, last=True)
                    for e in range(2):
                        write_rows(turns - 1, e, (LESS["act"][e], LESS["dve"][e]))

                @block.gpsimd
                def _(pool):
                    link = linker(pool, S["pool_link"])
                    out = a["outs"]

                    def row(name):
                        r = out[name][0][bass.ds(l, 1)]
                        return r.rearrange({3: "o s n -> (o s) n", 4: "o s k d -> (o s) (k d)",
                                            5: "o s h c d -> (o s) (h c d)"}[len(r.shape)])

                    pool.wait_ge(*emptied(("mod", 11)))
                    for n, at in enumerate((2 * D, 5 * D)):
                        pool.dma_start(a["gate_rows"][n], modrow[:, at:at + D]).then_inc(S["gates_out"], 16)
                    pool.wait_ge(*emptied(("z", "gkv", 0)))
                    pool.dma_start(row("mla_kpe"), z[:, 0, Z_KPE:Z_KPE + M_ROPE]).then_inc(S["cache_out"], 16)
                    pool.dma_start(row("gqa_v"), z[:, 0, Z_GV:Z_GV + P]).then_inc(S["cache_out"], 16)
                    pool.wait_ge(*emptied(("z", "dv", T - 1)))
                    pool.dma_start(row("diff_k"), z[:, 0, Z_DK:Z_DK + 512]).then_inc(S["cache_out"], 16)
                    pool.dma_start(row("diff_v"), z[:, 0, Z_DV:Z_DV + 512]).then_inc(S["cache_out"], 16)
                    heads = G_HEADS + G_KV
                    pool.wait_ge(S["head_rs"], 1)
                    qk = z[:, :, Z_GQ:Z_GQ + heads * HD].rearrange("p t (h d) -> p t h d", d=HD)
                    link(nc.gpsimd.tensor_tensor(qk, qk, rsv[:, :, 2:2 + heads, None].to_broadcast([P, T, heads, HD]), ALU.mult))
                    for g, h0, h1 in (("gq", 0, G_HEADS), ("gk", G_HEADS, heads)):
                        gain = gains[:, None, None, GAIN[g]].to_broadcast([P, T, h1 - h0, HD])
                        link(nc.gpsimd.tensor_tensor(qk[:, :, h0:h1], qk[:, :, h0:h1], gain, ALU.mult))
                    pool.wait_ge(S["ckv_ready"], 1)
                    pool.dma_start(row("mla_ckv"), z[:, 0, Z_CKV:Z_CKV + KV_LORA]).then_inc(S["cache_out"], 16)
                    pool.dma_start(row("gqa_k"), z[:, 0, Z_GK:Z_GK + P]).then_inc(S["cache_out"], 16)
                    for t in (1, 2):
                        link(rope(nc.gpsimd, link, t, qk[:, t], rtmp[:, :], heads, HD, K_C64, K_S64))
                    for kt in range(4):
                        src = tile_rows(c_gk, Z_GK, G_KV * HD, kt).rearrange("p (k d) -> p k d", d=HD)
                        if kt == 1:
                            pool.wait_ge(S["params_in"], 16 * N_PARAMS)
                        for c in range(2):
                            ins = nc.gpsimd.tensor_copy(kdv[:, kt, :, c, :], src)
                    ins.then_inc(S["kdup_ready"], 1)
                    for t in (1, 2):
                        for at in (Z_DQ, Z_DK):
                            ins = rope(nc.gpsimd, link, t, z[:, t, at:at + 512].rearrange("p (h d) -> p h d", d=HD), rtmp[:, :],
                                       2 * F_HEADS, HD, K_C64, K_S64)
                            if (t, at) != (2, Z_DK):
                                link(ins)
                    ins.then_inc(S["diff_roped"], 1)
                    pool.wait_ge(*filled(("O",) + MAPS["mb"][-1]))
                    pool.wait_ge(S["dec_scaled"], 1)
                    for dst, at, q in ((qfb, Z_RQ, 0), (kfb, Z_RK, 2)):
                        src = z[:, :, at:at + R_HEADS * R_DK].rearrange("p t (h d) -> p t h d", h=R_HEADS)
                        for f in range(2):
                            decay = dec[:, None, 4 * (q + f):4 * (q + f) + 4, None].to_broadcast([P, T, R_HEADS, R_DK])
                            ins = nc.gpsimd.tensor_tensor(dst[:, :, :, f, :], src, decay, ALU.mult)
                    ins.then_inc(S["qkfb_ready"], 1)
                    pool.wait_ge(S["masks_raw"], 1)
                    for m, at in ((mask, K_MF), (maskb, K_MB)):
                        link(nc.gpsimd.tensor_tensor(m, m, const[:, None, at:at + P].to_broadcast([P, R_HEADS, P]), ALU.mult))
                    link(nc.gpsimd.tensor_tensor(mask, mask, maskb, ALU.add))
                    nc.gpsimd.tensor_scalar(mask, mask, R_DK ** -0.5, None, ALU.mult).then_inc(S["mask_ready"], 1)
                    pool.wait_ge(*emptied(("KV", 0)))
                    for r in range(2):
                        so = out["state_ret"][0][bass.ds(l, 1)].rearrange("o r h k v -> (o r) k h v")[r]
                        pool.dma_start(so, state_ctx[64 * r:64 * r + 64, :].rearrange("p (h v) -> p h v", h=R_HEADS)
                                       ).then_inc(S["cache_out"], 16)
                    def head_rows(at):
                        return z[:, :, at:at + 512].rearrange("p t (h d) -> p t h d", d=128)

                    def of_heads(v):
                        return v.rearrange("p (t h) -> p t h", t=T)[:, :, :, None].to_broadcast([P, T, 4, 128])

                    ro, do, rr = head_rows(Z_RQ), head_rows(Z_DQ), z[:, :, Z_RQ:Z_RQ + 512]
                    pool.wait_ge(S["branch_rs"], 1)
                    link(nc.gpsimd.tensor_tensor(ro, ro, of_heads(mu[:, :]), ALU.add))
                    link(nc.gpsimd.tensor_tensor(ro, ro, of_heads(rs[:, 0:12]), ALU.mult))
                    link(nc.gpsimd.tensor_tensor(rr, rr, gains[:, None, GAIN["ret"]].to_broadcast([P, T, 512]), ALU.mult))
                    nc.gpsimd.tensor_tensor(rr, rr, z[:, :, Z_RG:Z_RG + 512], ALU.mult).then_inc(S["head_normed"], 1)
                    link(nc.gpsimd.tensor_tensor(do, do, of_heads(rs[:, 12:24]), ALU.mult))
                    nc.gpsimd.tensor_tensor(do, do, gains[:, None, None, GAIN["diff"]].to_broadcast([P, T, 4, 128]), ALU.mult
                                            ).then_inc(S["head_normed"], 1)

                    nc.gpsimd.memset(zero_row, 0.0).then_inc(S["zeros_ready"], 1)
                    pool.wait_ge(S["zeros_ready"], 1)
                    pool.dma_start(a["y_slots"].rearrange("(p i) n -> p i n", i=NT)[:, NE:, :],
                                   zero_row[0:CAP, None, :].to_broadcast([CAP, NT - NE, D])).then_inc(S["zeros_out"], 16)

                    def fetch_gates(n):
                        for v in range(2):
                            pool.dma_start(gp[:, v, :], spread(a["gate_rows"][n, v])).then_inc(S["gates_in"], 16)
                        pool.dma_start(gpost, spread(rows(a["g_post1" if n == 0 else "g_post2"], l))).then_inc(S["gates_in"], 16)

                    pool.wait_ge(*filled(("R", T - 1)))
                    nc.gpsimd.memset(ones, 1.0).then_inc(S["ones_ready"], 1)
                    pool.wait_ge(*filled(("mgT", KD // 2)))
                    pool.wait_ge(S["zeros_out"], 16)
                    fetch_gates(0)
                    pool.wait_ge(*filled(("gu", "s", 0)))
                    fetch_gates(1)
                    pool.wait_ge(S["table_reset"], 16)
                    pool.wait_ge(S["slots_ready"], 1)
                    for i in range(T * TOPK):
                        pool.indirect_dma_start(a["slot_tokens"], bass.IndirectOffsetOnAxis(ap=slot_u[:, i:i + 1], axis=0),
                                                token_u[:, i // TOPK:i // TOPK + 1], None).then_inc(S["slots_out"], 16)
                    pool.wait_ge(S["slots_out"], 16 * T * TOPK)
                    pool.dma_start(tokens[0:CAP], a["slot_tokens"].rearrange("(p i) o -> p (i o)", i=NT)).then_inc(S["table_in"], 16)
                    pool.wait_ge(S["table_in"], 16)
                    pool.wait_ge(S["rows_out"], 16 * T)

                    def gather(tile, e, n):
                        col = tokens[0:CAP, tile:tile + 1] if isinstance(tile, int) else tokens[0:CAP, bass.ds(tile, 1)]
                        nc.gpsimd.tensor_copy(index[0:CAP, e:e + 1], col).then_inc(S[f"index_copied{e}"], 1)
                        pool.wait_ge(S[f"index_copied{e}"], n)
                        pool.sem_inc(S["gathers"], 1)
                        pool.indirect_dma_start(xg[0:CAP, e, :], None, a["token_rows"],
                                                bass.IndirectOffsetOnAxis(ap=index[0:CAP, e:e + 1], axis=0)).then_inc(S[f"x_landed{e}"], 16)

                    for e in range(2):
                        gather(e, e, 1)
                    for e in range(2):
                        pool.wait_ge(*filled(("xt", e, 1)))
                        gather(2 + e, e, 2)
                    turns = turns_of(pool)
                    with pool.Fori(0, turns - 2) as turn:
                        for e in range(2):
                            pool.wait_ge(*job_filled(turn, e, "xt1"))
                            gather(turn * 2 + e + 4, e, turn + 3)
                    for e in range(2):
                        pool.wait_ge(S[f"y_written{e}"], turns * 16 + 16)
                        pool.sem_inc(S["gathers"], 1)
                    for i in range(T * TOPK):
                        if i >= 6:
                            pool.wait_ge(S["summed"], i - 5)
                        pool.indirect_dma_start(ybuf[:, i % 6, :], None, a["y_slots"],
                                                bass.IndirectOffsetOnAxis(ap=slot_u[:, i:i + 1], axis=0)).then_inc(S[f"y_landed{i % 6}"], 16)
                    pool.wait_ge(S["cache_out"], 16 * 8)
                    pool.wait_ge(S["summed"], T * TOPK)

                @block.scalar
                def _(act):
                    link = linker(act, S["act_link"])

                    def dma(dst, src, sem="params_in", scattered=False):
                        act.dma_start(dst, src, allow_slow_non_contiguous=scattered).then_inc(S[sem], 16)

                    dma(modrow, rows(a["b_mod"], l).partition_broadcast(2), "bmod_in")
                    for n, name in enumerate(("g_pre1", "g_pre2")):
                        dma(gpre[:, n * KD:(n + 1) * KD], rows(a[name], l).rearrange("(k p) -> p k", p=P), scattered=True)
                    for g, name in (("q", "g_mla_q"), ("kv", "g_mla_kv"), ("gq", "g_gqa_q"), ("gk", "g_gqa_k"),
                                    ("ret", "g_ret"), ("diff", "g_diff")):
                        dma(gains[:, GAIN[g]], spread(rows(a[name], l)))
                    dma(lamp[:, :], spread(rows(a["diff_lambda"], l).rearrange("a b -> (a b)")))
                    dma(lamv[:, 6:8], rows(a["lam_init"], l))
                    dma(rdec[:, :], spread(rows(a["ret_decay"], l).rearrange("a b -> (a b)")))
                    dma(brt[:, :], spread(rows(a["b_router"], l)))
                    dma(wr[:, :].rearrange("p (k n) -> p k n", k=KD), rows(a["w_router"], l).rearrange("(k p) n -> p k n", p=P))
                    for buf, name in ((c_ckv, "cache_mla_ckv"), (c_kpe, "cache_mla_kpe"), (c_gk, "cache_gqa_k"),
                                      (c_gv, "cache_gqa_v"), (c_dk, "cache_diff_k"), (c_dv, "cache_diff_v")):
                        src = a[name][0][bass.ds(l, 1)]
                        src = src.rearrange({3: "o s n -> (o s) n", 4: "o s k d -> (o s) (k d)",
                                             5: "o s h c d -> (o s) (h c d)"}[len(a[name].shape) - 1])
                        dma(buf[:, :], src)
                    for r in range(2):
                        src = a["state_ret"][0][bass.ds(l, 1)].rearrange("o r h k v -> (o r) k h v")[r]
                        dma(state0v[64 * r:64 * r + 64], src)

                    def square_rows(v, junk_rows, sem):
                        for t in range(T):
                            nc.scalar.activation(junk_rows[:, t], v[:, t], ACT.Square,
                                                 accum_out=stat[:, t:t + 1]).then_inc(S[sem], 1)

                    def root(n, site):
                        act.wait_ge(S["var_ready"], site + 1)
                        nc.scalar.activation(rs[:, 0:n], stat[:, 0:n], ACT.Sqrt).then_inc(S["root_ready"], 1)

                    act.wait_ge(const_in, 48)
                    square_rows(xv, junk, "x_squared")
                    root(T, 0)

                    def modulated(name, n):
                        for k in range(KD):
                            act.wait_ge(*filled((name, k)))
                            for v, cols in ((0, slice(0, P)), (1, slice(P, T * P))):
                                ins = nc.scalar.activation(hTv[:, k, cols], psum[:, J.bank((name, k)), cols], ACT.Identity,
                                                           scale=modTv[:, 2 * n + 1, k, v:v + 1], bias=modTv[:, 2 * n, k, v:v + 1])
                            ins.then_inc(S["act_emptied"], 1)

                    def decays():
                        act.wait_ge(S["absx_ready"], 1)
                        nc.scalar.activation(small[:, 8:16], small[:, 0:8], ACT.Exp, scale=-1.0).then_inc(S["expx_ready"], 1)
                        act.wait_ge(S["u_ready"], 1)
                        nc.scalar.activation(small[:, 24:32], small[:, 16:24], ACT.Ln).then_inc(S["ln_ready"], 1)
                        act.wait_ge(S["lg_ready"], 1)
                        for q in range(4):
                            f = q % 2
                            nc.scalar.activation(dec[:, 4 * q:4 * q + 4], small[:, 32 + 4 * f:36 + 4 * f], ACT.Exp,
                                                 scale=const[:, K_POS + q:K_POS + q + 1])
                        for f in range(2):
                            ins = nc.scalar.activation(dec[64 * f:64 * f + 64, 16:20], small[64 * f:64 * f + 64, 32 + 4 * f:36 + 4 * f],
                                                       ACT.Exp, scale=float(P))
                        ins.then_inc(S["dec_ready"], 1)
                        act.wait_ge(S["lam_dots"], 1)
                        nc.scalar.activation(lamv[:, 2:4], lamv[:, 0:2], ACT.Exp).then_inc(S["lam_exps"], 1)

                    decays()
                    def split_high(j):
                        act.wait_ge(*landed(SPLITS[j]))
                        act.wait_ge(*(piece_used(SPLITS[j - HIGHS]) if j >= HIGHS else filled(("mod", 11))))
                        nc.scalar.activation(high(j), piece(SPLITS[j]), ACT.Copy).then_inc(S["high_ready"], 1)

                    for j in range(HIGHS):
                        split_high(j)
                    act.wait_ge(S["modT_ready"], 1)
                    modulated("h1", 0)

                    act.wait_ge(S["gates_out"], 32)

                    def empty_z(s, t):
                        at, n = SEG[s]
                        act.wait_ge(*filled(("z", s, t)))
                        nc.scalar.activation(z[:, t, at:at + n], bank(("z", s, t), n),
                                             ACT.Silu if s == "rg" else ACT.Copy).then_inc(S["act_emptied"], 1)

                    for j in range(Z_PIECES):
                        _, s, half = SPLITS[j]
                        if half:
                            empty_z(s, 0)
                            empty_z(s, 1)
                        if j + HIGHS < Z_PIECES:
                            split_high(j + HIGHS)
                        if half:
                            empty_z(s, 2)
                        if (s, half) == ("rv", 1):
                            root(36, 1)

                    def empty_next(g, step):
                        for key in TURNED_NEXT[g][step]:
                            if J.taker[key] == "act":
                                kind, b = key
                                buffer, block, scale = {"gqT": (0, b, HD ** -0.5), "dqT": (1, b, HD ** -0.5),
                                                        "rqT": (0, b, 1.0), "rkT": (0, 2 + b, 1.0)}[kind]
                                act.wait_ge(*filled(key))
                                nc.scalar.activation(qTv[:, buffer, block, :], bank(key, 384), ACT.Copy, scale=scale).then_inc(S["act_emptied"], 1)

                    def softmax_maps(g):
                        m = MAPS[g]
                        for i in range(len(m) + 4):
                            if i < len(m):
                                key = m[i]
                                n = P * len(keys_of(key[2]))
                                act.wait_ge(S["max_ready"], MAX_AT[key])
                                if i >= 3:
                                    act.wait_ge(*filled(("PT",) + m[i - 3]))
                                if i >= 5:
                                    act.wait_ge(*emptied(("O",) + m[i - 5]))
                                nc.scalar.activation(Pb[:, (i % 3) * 384:(i % 3) * 384 + n], bank(("S",) + key, n), ACT.Exp,
                                                     bias=nmax[:, i % 4:i % 4 + 1], scale=1.0,
                                                     accum_out=rsum[:, i % 5:i % 5 + 1]).then_inc(S["act_emptied"], 1)
                            if 2 <= i < len(m) + 2 and J.taker[("PT",) + m[i - 2]] == "act":
                                empty_turned(i - 2, m)
                            if i >= len(m):
                                empty_next(g, i - len(m))

                    def empty_turned(i, m):
                        key = ("PT",) + m[i]
                        n = P * len(keys_of(m[i][2]))
                        act.wait_ge(*filled(key))
                        if i >= 2:
                            act.wait_ge(*filled(("O",) + m[i - 2]))
                        nc.scalar.activation(PTb[:, (i % 2) * 384:(i % 2) * 384 + n], bank(key, n),
                                             ACT.Copy).then_inc(S["act_emptied"], 1)

                    for c, g in enumerate(("ma", "mb")):
                        for t in range(T):
                            act.wait_ge(*filled(("qm", c, t)))
                            if c == 1:
                                act.wait_ge(*filled(("mqT", 0, HALF - 1)))
                            nc.scalar.activation(qmv[:, t], bank(("qm", c, t), 384).rearrange("p (h d) -> p h d", h=HALF),
                                                 ACT.Copy).then_inc(S["act_emptied"], 1)
                        for h in range(HALF):
                            act.wait_ge(*filled(("mqT", c, h)))
                            if c == 1:
                                act.wait_ge(*filled(("kv", 1, 3)))
                            nc.scalar.activation(qTv[0:M_HD, c, h, :], bank(("mqT", c, h), 384, slice(0, M_HD)), ACT.Copy,
                                                 scale=M_HD ** -0.5).then_inc(S["act_emptied"], 1)
                        softmax_maps(g)
                    softmax_maps("g")
                    act.wait_ge(*filled(("gkT", 1)))
                    for h in range(R_HEADS):
                        nc.scalar.activation(mask[:, h], cview(K_DF, P), ACT.Exp, scale=small[:, 32 + h:33 + h])
                        ins = nc.scalar.activation(maskb[:, h], cview(K_DB, P), ACT.Exp, scale=small[:, 36 + h:37 + h])
                    ins.then_inc(S["masks_raw"], 1)
                    m = MAPS["d"]
                    for i in range(len(m) + 4):
                        if i < len(m):
                            n = P * len(keys_of(m[i][2]))
                            for w in range(2):
                                r = 2 * (i % 3) + w
                                act.wait_ge(S["max_ready"], MAX_AT[("S1", "S2")[w], *m[i]])
                                if w == 0 and i >= 3:
                                    act.wait_ge(*filled(("PT",) + m[i - 3]))
                                if w == 1 and i >= 2:
                                    act.wait_ge(S["pd_ready"], i - 1)
                                dst = (first_map[:, i % 3], second_map[:, i % 2])[w]
                                nc.scalar.activation(dst[:, 0:n], bank((("S1", "S2")[w],) + m[i], n), ACT.Exp,
                                                     bias=nmax[:, r:r + 1], scale=1.0,
                                                     accum_out=rsum[:, r:r + 1]).then_inc(S["act_emptied"], 1)
                        if i >= 4:
                            key = m[i - 4]
                            scale = rrec[:, 2 * (i + 1) % 10:2 * (i + 1) % 10 + 1]
                            act.wait_ge(*filled(("O",) + key))
                            _, h, t = key
                            nc.scalar.activation(out_cols(*key), bank(("O",) + key, F_DV), ACT.Copy, scale=scale)
                            if i >= 6:
                                act.wait_ge(*emptied(("O",) + m[i - 6]))
                            nc.scalar.activation(c_ckv[:, (i % 2) * F_DV:(i % 2 + 1) * F_DV], bank(("O",) + key, F_DV), ACT.Square, scale=scale,
                                                 accum_out=stat[:, 12 + t * 4 + h:13 + t * 4 + h]).then_inc(S["act_emptied"], 1)
                        if 2 <= i < len(m) + 2:
                            empty_turned(i - 2, m)
                        if i >= len(m):
                            empty_next("d", i - len(m))
                    for j in range(Z_PIECES, Z_PIECES + HIGHS):
                        split_high(j)
                    for h in range(R_HEADS):
                        act.wait_ge(*filled(("qfbT", h)))
                        nc.scalar.activation(qfbT[:, h, :], bank(("qfbT", h), 384), ACT.Copy).then_inc(S["act_emptied"], 1)
                    for t in range(T):
                        act.wait_ge(*filled(("R", t)))
                        for h in range(R_HEADS):
                            ins = nc.scalar.activation(z[:, t, Z_RQ + h * R_DV:Z_RQ + (h + 1) * R_DV],
                                                       psum[:, J.bank(("R", t)), h * R_DV:(h + 1) * R_DV], ACT.Copy,
                                                       accum_out=mu[:, t * 4 + h:t * 4 + h + 1])
                        ins.then_inc(S["act_emptied"], 1)
                    act.wait_ge(S["mean_ready"], 1)
                    for i in range(T * R_HEADS):
                        t, h = divmod(i, R_HEADS)
                        ins = nc.scalar.activation(kT[:, 2048 + i * R_DV:2048 + (i + 1) * R_DV], z[:, t, Z_RQ + h * R_DV:Z_RQ + (h + 1) * R_DV],
                                                   ACT.Square, bias=mu[:, i:i + 1], scale=1.0, accum_out=stat[:, i:i + 1])
                    ins.then_inc(S["ret_squared"], 1)
                    dma(earlier, a["earlier"], "earlier_in")
                    root(24, 2)
                    def gate(n, c, t):
                        i = (n * 2 + c) * T + t
                        act.wait_ge(*filled(("gl", n, c, t)))
                        if i >= 4:
                            act.wait_ge(*emptied(("br", *GATES[i - 4])))
                        nc.scalar.activation(gs[i % 4], bank(("gl", n, c, t)), ACT.Sigmoid).then_inc(S["act_emptied"], 1)

                    def merged_high(k0, k1):
                        for k in range(k0, k1):
                            act.wait_ge(*filled(("mgT", k)))
                            nc.scalar.activation(merged_split[0][:, k], bank(("mgT", k), 384), ACT.Copy).then_inc(S["mgT_high"], 1)

                    for j in range(Z_PIECES, OUT_PIECES):
                        kind, n, c, half = SPLITS[j]
                        if (kind, c, half) == ("gl", 0, 0):
                            for k in range(4):
                                act.wait_ge(*filled(("oT", n, k)))
                                nc.scalar.activation(oT_split[0][:, k], bank(("oT", n, k), 384), ACT.Copy).then_inc(S["oT_high"], 1)
                        if (kind, half) == ("gl", 1):
                            gate(n, c, 0)
                            gate(n, c, 1)
                        if (kind, n, c) == ("br", NBR - 1, 1):
                            merged_high(0, KD // 2)
                        split_high(j + HIGHS)
                        if (kind, half) == ("gl", 1):
                            gate(n, c, 2)
                    merged_high(KD // 2, KD)

                    def empty_out(c, t):
                        act.wait_ge(*filled(("out", c, t)))
                        nc.scalar.activation(m_row[:, t, c * C:(c + 1) * C], bank(("out", c, t)), ACT.Copy).then_inc(S["act_emptied"], 1)

                    def row_root(v, junk_row, col, sem):
                        link(nc.scalar.activation(junk_row, v, ACT.Square, accum_out=stat[:, col:col + 1]))
                        nc.scalar.activation(rs[:, col:col + 1], stat[:, col:col + 1], ACT.Sqrt, scale=1.0 / D,
                                             bias=const[:, K_EPS:K_EPS + 1]).then_inc(S[sem], 1)

                    def post_root(t):
                        act.wait_ge(*emptied(("out", 1, t)))
                        row_root(m_row[:, t], merged[:, t], POST + t, "post_root")

                    def pre_root(t):
                        act.wait_ge(S["x_ready"], t + 1)
                        row_root(xv[:, t], cmpj[:, t], PRE + t, "pre_root")

                    for j in range(OUT_PIECES, len(SPLITS)):
                        _, c, half = SPLITS[j]
                        if half:
                            for t in range(T):
                                if t == 2 and c == 0:
                                    split_high(j + HIGHS)
                                empty_out(c, t)
                                if c == 1:
                                    post_root(t)
                                    if t:
                                        pre_root(t - 1)
                        elif j + HIGHS < len(SPLITS):
                            split_high(j + HIGHS)
                    pre_root(T - 1)
                    modulated("h2", 1)
                    for t in range(T):
                        act.wait_ge(*filled(("hrow", t, 1)))
                        nc.scalar.activation(xn2[:, t, C:], bank(("hrow", t, 1)), ACT.Copy).then_inc(S["act_emptied"], 1)
                    act.wait_ge(*filled(("route",)))
                    nc.scalar.activation(rt[:, R_EXP], bank(("route",), T * NE).rearrange("p (t e) -> p t e", t=T), ACT.Exp,
                                         scale=-1.0).then_inc(S["act_emptied"], 1)

                    act.dma_start(a["slot_tokens"].rearrange("(p i) o -> p (i o)", i=NT), a["no_tokens"]).then_inc(S["table_reset"], 16)
                    for t in range(T):
                        act.wait_ge(*emptied(("hrow", t, 0)))
                        act.wait_ge(*emptied(("hrow", t, 1)))
                        act.dma_start(a["token_rows"][t * P:(t + 1) * P, :], xn2[:, t, :]).then_inc(S["rows_out"], 16)
                    for t in range(T):
                        act.wait_ge(*filled(("gu", "s", t)))
                        nc.scalar.activation(shared[:, t], bank(("gu", "s", t), FF), ACT.Silu).then_inc(S["silu_ready"], 1)
                    act.wait_ge(*filled(("place",)))
                    nc.scalar.activation(counted, bank(("place",), (T + 1) * NE), ACT.Copy).then_inc(S["act_emptied"], 1)
                    for t in range(T):
                        act.wait_ge(*filled(("aT", "s", t)))
                        nc.scalar.activation(shared_T[:, t].rearrange("p f n -> p (f n)"), bank(("aT", "s", t), FF),
                                             ACT.Copy).then_inc(S["act_emptied"], 1)
                    for i in range(2):
                        act.wait_ge(*filled(("xt", i, 0)))
                        nc.scalar.activation(xT[:, i, 0:4].rearrange("p k n -> p (k n)"), psum[:, BANK_XT, 0:4 * CAP], ACT.Copy).then_inc(S["act_emptied"], 1)
                    act.wait_ge(*filled(("gu", 0)))
                    nc.scalar.activation(silu[0:CAP, 0, :], psum[0:CAP, BANK_GU, 0:FF], ACT.Silu).then_inc(S["silu_ready"], 1)
                    turns = turns_of(act)

                    def steps(turn, last=False):
                        for e in range(2):
                            less = LESS["filled"][e] if last else 0
                            if not last:
                                act.wait_ge(*job_filled(turn, e, "xt0"))
                                nc.scalar.activation(xT[:, e, 0:4].rearrange("p k n -> p (k n)"), psum[:, BANK_XT, 0:4 * CAP],
                                                     ACT.Copy).then_inc(S["act_emptied"], 1)
                            if not (last and e == 1):
                                act.wait_ge(*job_filled(turn, e, "gu", 2 if last else 0))
                                nc.scalar.activation(silu[0:CAP, 1 - e, :], psum[0:CAP, BANK_GU + 1 - e, 0:FF], ACT.Silu).then_inc(S["silu_ready"], 1)
                            act.wait_ge(*job_filled(turn, e, "aT", less))
                            nc.scalar.activation(aT[:, e].rearrange("p f n -> p (f n)"), psum[:, BANK_AT, 0:2 * CAP],
                                                 ACT.Copy).then_inc(S["act_emptied"], 1)
                            act.wait_ge(*job_filled(turn, e, "y0", less))
                            act.wait_ge(S[f"y_written{e}"], turn * 16 + 16)
                            nc.scalar.activation(yrow[0:CAP, e, 0:C], psum[0:CAP, BANK_Y, :], ACT.Copy).then_inc(S["act_emptied"], 1)

                    with act.Fori(0, turns - 1) as turn:
                        steps(turn)
                    steps(turns - 1, last=True)
                    for t in range(T):
                        act.wait_ge(S["summed"], (t + 1) * TOPK)
                        row_root(acc[:, t], xn2[:, t], POST + t, "post_root")

                @block.vector
                def _(dve):
                    V = nc.vector
                    link = linker(dve, S["dve_link"])

                    def variance(at, n, count, site):
                        V.tensor_scalar(stat[:, at:at + n], stat[:, at:at + n], 1.0 / count, EPS, ALU.mult,
                                        ALU.add).then_inc(S["var_ready"], 1)
                        dve.wait_ge(S["root_ready"], site + 1)
                        link(V.reciprocal(rs[:, 0:n], rs[:, 0:n]))

                    def empty(key, dst, src):
                        dve.wait_ge(*filled(key))
                        V.tensor_copy(dst, src).then_inc(S["dve_emptied"], 1)

                    dve.wait_ge(S["x_squared"], T)
                    variance(0, T, D, 0)
                    for t in range(T):
                        ins = V.tensor_scalar(xn[:, t], xv[:, t], rs[:, t:t + 1], None, ALU.mult)
                    ins.then_inc(S["xn_ready"], 1)
                    dve.wait_ge(S["params_in"], 16 * N_PARAMS)
                    V.scalar_tensor_tensor(small[:, 0:8], rdec[:, :], -1.0, rdec[:, :], ALU.mult, ALU.max).then_inc(S["absx_ready"], 1)
                    dve.wait_ge(S["expx_ready"], 1)
                    V.tensor_scalar(small[:, 16:24], small[:, 8:16], 1.0, None, ALU.add).then_inc(S["u_ready"], 1)
                    dve.wait_ge(S["u_ready"], 1)
                    link(V.scalar_tensor_tensor(small[:, 40:48], small[:, 16:24], -1.0, small[:, 8:16], ALU.add, ALU.subtract))
                    link(V.reciprocal(small[:, 48:56], small[:, 16:24]))
                    link(V.scalar_tensor_tensor(small[:, 40:48], small[:, 40:48], -1.0, small[:, 48:56], ALU.mult, ALU.mult))
                    dve.wait_ge(S["ln_ready"], 1)
                    link(V.tensor_tensor(small[:, 40:48], small[:, 40:48], small[:, 24:32], ALU.add))
                    V.scalar_tensor_tensor(small[:, 32:40], rdec[:, :], 0.0, small[:, 40:48], ALU.min, ALU.subtract).then_inc(S["lg_ready"], 1)
                    lp = lamp[:, :].rearrange("p (q c d) -> p q c d", q=2, c=2)
                    link(V.tensor_tensor(lp[:, :, 0], lp[:, :, 0], lp[:, :, 1], ALU.mult))
                    V.tensor_reduce(lamv[:, 0:2], lp[:, :, 0], AX, ALU.add).then_inc(S["lam_dots"], 1)
                    dve.wait_ge(S["lam_exps"], 1)
                    link(V.tensor_tensor(lamv[:, 4:5], lamv[:, 2:3], lamv[:, 3:4], ALU.subtract))
                    link(V.tensor_tensor(lamv[:, 4:5], lamv[:, 4:5], lamv[:, 6:7], ALU.add))
                    link(V.tensor_scalar(lamv[:, 5:6], lamv[:, 4:5], -1.0, None, ALU.mult))
                    link(V.tensor_scalar(gains[:, GAIN["diff"]], gains[:, GAIN["diff"]], lamv[:, 7:8], None, ALU.mult))
                    dve.wait_ge(S["dec_ready"], 1)
                    V.tensor_scalar(dec[:, 8:16], dec[:, 8:16], R_DK ** -0.5, None, ALU.mult).then_inc(S["dec_scaled"], 1)
                    dve.wait_ge(S["bmod_in"], 16)
                    for m in range(12):
                        dve.wait_ge(*filled(("mod", m)))
                        cols = modrow[:, m * C:(m + 1) * C]
                        V.tensor_tensor(cols, cols, bank(("mod", m), C, slice(0, 2)), ALU.add).then_inc(S["dve_emptied"], 1)
                    empty(("modT",), modT[:, :], bank(("modT",), 4 * KD * 2))
                    dve.wait_ge(*emptied(("modT",)))
                    for n in range(2):
                        g = gpre[:, n * KD:(n + 1) * KD, None].to_broadcast([P, KD, 2])
                        ins = V.scalar_tensor_tensor(modTv[:, 2 * n + 1], modTv[:, 2 * n + 1], 1.0, g, ALU.add, ALU.mult)
                    ins.then_inc(S["modT_ready"], 1)

                    def split_activations(parts, first):
                        high_part, low_part = parts
                        for k in range(KD):
                            if first:
                                dve.wait_ge(*emptied(("h1", k)))
                            link(V.tensor_copy(high_part[:, k], hTv[:, k]))
                            V.tensor_tensor(low_part[:, k], hTv[:, k], high_part[:, k].bitcast(F32), ALU.subtract).then_inc(S["h_split"], 1)

                    def split_low(j):
                        dve.wait_ge(S["high_ready"], j + 1)
                        V.tensor_tensor(piece(SPLITS[j], Wr), piece(SPLITS[j]), high(j).bitcast(F32), ALU.subtract).then_inc(S["low_ready"], 1)

                    heads = G_HEADS + G_KV

                    def squares_low_rank():
                        dve.wait_ge(*emptied(("z", "gkv", T - 1)))
                        for t in range(T):
                            for c, (at, n) in enumerate(((Z_CQ, Q_LORA), (Z_CKV, KV_LORA))):
                                at_junk = (t * Q_LORA, T * Q_LORA + t * KV_LORA)[c]
                                v = z[:, t, at:at + n]
                                ins = V.tensor_tensor_reduce(out=vm[:, at_junk:at_junk + n], in0=v, in1=v, scale=1.0, scalar=0.0,
                                                             op0=ALU.mult, op1=ALU.add, accum_out=statv[:, t, c:c + 1])
                        link(ins)

                    def squares_of_heads():
                        qk = z[:, :, Z_GQ:Z_GQ + heads * HD]
                        sq = vm[:, 0:T * heads * HD]
                        link(V.tensor_tensor(sq.rearrange("p (t n) -> p t n", t=T), qk, qk, ALU.mult))
                        link(V.tensor_reduce(statv[:, :, 2:12], sq.rearrange("p (t h d) -> p t h d", t=T, d=HD), AX, ALU.add))
                        for a0, a1, count in ((0, 1, Q_LORA), (1, 2, KV_LORA), (2, 12, HD)):
                            ins = V.tensor_scalar(statv[:, :, a0:a1], statv[:, :, a0:a1], 1.0 / count, EPS, ALU.mult, ALU.add)
                        ins.then_inc(S["var_ready"], 1)

                    def roots_of_heads():
                        dve.wait_ge(S["root_ready"], 2)
                        V.reciprocal(rs[:, 0:36], rs[:, 0:36]).then_inc(S["head_rs"], 1)
                        dve.wait_ge(S["head_rs"], 1)

                    def norm_low_rank(c):
                        at, n, g, done = ((Z_CQ, Q_LORA, "q", "cq_ready"), (Z_CKV, KV_LORA, "kv", "ckv_ready"))[c]
                        for t in range(T):
                            v = z[:, t, at:at + n]
                            ins = V.scalar_tensor_tensor(v, v, rsv[:, t, c:c + 1], gains[:, GAIN[g]], ALU.mult, ALU.mult)
                        ins.then_inc(S[done], 1)

                    split_low(0)
                    split_activations(h_split_z, True)
                    split_low(1)
                    for j in range(Z_PIECES):
                        if j + HIGHS < Z_PIECES:
                            split_low(j + HIGHS)
                        at_seg = SPLITS[j][1:]
                        if at_seg == ("rqk", 0):
                            squares_low_rank()
                        if at_seg == ("rqk", 1):
                            squares_of_heads()
                        if at_seg == ("rg", 0):
                            roots_of_heads()
                            norm_low_rank(0)
                        if at_seg == ("rg", 1):
                            norm_low_rank(1)

                    for k in range(3):
                        empty(("cqT", k), cqT[:, k, :], bank(("cqT", k), 384))
                    for k in range(2):
                        empty(("ckvT", k), ckvT[:, k, :], bank(("ckvT", k)))
                    tmp = kT[:, 0:M_ROPE], kT[:, M_ROPE:2 * M_ROPE]
                    for t in (1, 2):
                        v = z[:, t, Z_KPE:Z_KPE + M_ROPE].rearrange("p (h d) -> p h d", h=1)
                        link(rope(V, link, t, v, tmp[t - 1], 1, M_ROPE, K_C32, K_S32))
                    for kt in range(4):
                        src = c_kpe[:, :] if kt == 1 else z[:, (0, None, 1, 2)[kt], Z_KPE:Z_KPE + M_ROPE]
                        ins = V.tensor_copy(kmv[:, kt, :, M_NOPE:], src[:, None, :].to_broadcast([P, HALF, M_ROPE]))
                    ins.then_inc(S["km_ready"], 1)

                    def largest(key):
                        g, h, t = key[1:]
                        i = MAPS[g].index((g, h, t))
                        col = i % 4 if key[0] == "S" else 2 * (i % 3) + (key[0] == "S2")
                        dve.wait_ge(*filled(key))
                        V.tensor_reduce(nmax[:, col:col + 1], bank(key, P * len(keys_of(t))), AX, ALU.max,
                                        negate=True).then_inc(S["max_ready"], 1)

                    def softmax_maps(g):
                        m = MAPS[g]
                        for i in range(len(m) + 4):
                            if i < len(m):
                                largest(("S",) + m[i])
                            if i >= 4:
                                key, s = m[i - 4], (i - 4) % 5
                                dve.wait_ge(*emptied(("S",) + key))
                                link(V.reciprocal(rrec[:, s:s + 1], rsum[:, s:s + 1]))
                                dve.wait_ge(*filled(("O",) + key))
                                V.tensor_scalar(out_cols(*key), bank(("O",) + key, HD), rrec[:, s:s + 1], None,
                                                ALU.mult).then_inc(S["dve_emptied"], 1)
                            if 2 <= i < len(m) + 2 and J.taker[("PT",) + m[i - 2]] == "dve":
                                n = P * len(keys_of(m[i - 2][2]))
                                if i >= 4:
                                    dve.wait_ge(*filled(("O",) + m[i - 4]))
                                s = (i - 2) % 2
                                empty(("PT",) + m[i - 2], PTb[:, s * 384:s * 384 + n], bank(("PT",) + m[i - 2], n))
                            if i >= len(m):
                                for key in TURNED_NEXT[g][i - len(m)]:
                                    if J.taker[key] == "dve":
                                        empty(key, kTv[:, 1 if key[0] == "dkT" else 0, key[1], :], bank(key))

                    for c, g in enumerate(("ma", "mb")):
                        for kt in range(4):
                            key = ("kv", c, kt)
                            both = bank(key).rearrange("p (h d) -> p h d", h=HALF)
                            dve.wait_ge(*filled(key))
                            V.tensor_copy(kmv[:, kt, :, 0:M_NOPE], both[:, :, 0:M_NOPE])
                            V.tensor_copy(vmv[:, kt, c * HALF:(c + 1) * HALF, :], both[:, :, M_NOPE:]).then_inc(S["dve_emptied"], 1)
                        for t in (1, 2):
                            dve.wait_ge(*emptied(("qm", c, t)))
                            tmp = c_ckv[:, (t - 1) * 128:t * 128]
                            ins = rope(V, link, t, qmv[:, t, :, M_NOPE:], tmp, HALF, M_ROPE, K_C32, K_S32)
                            if t == 1:
                                link(ins)
                        ins.then_inc(S["qm_roped"], 1)
                        for h in range(HALF):
                            empty(("mkT", c, h), kTv[0:M_HD, c, h, :], bank(("mkT", c, h), C, slice(0, M_HD)))
                        if c == 1:
                            dve.wait_ge(S["cache_out"], 16 * 6)
                        softmax_maps(g)

                    softmax_maps("g")
                    m = MAPS["d"]

                    def difference(i):
                        n = P * len(keys_of(m[i][2]))
                        r = 2 * (i % 3)
                        p1, p2 = first_map[:, i % 3, 0:n], second_map[:, i % 2, 0:n]
                        dve.wait_ge(*emptied(("S2",) + m[i]))
                        q = 2 * (i % 5)
                        link(V.reciprocal(rrec[:, q:q + 2], rsum[:, r:r + 2]))
                        link(V.scalar_tensor_tensor(rrec[:, q + 1:q + 2], rrec[:, q + 1:q + 2], lamv[:, 5:6], rsum[:, r:r + 1],
                                                    ALU.mult, ALU.mult))
                        V.scalar_tensor_tensor(p1, p2, rrec[:, q + 1:q + 2], p1, ALU.mult, ALU.add).then_inc(S["pd_ready"], 1)

                    for i in range(len(m) + 1):
                        if i < len(m):
                            largest(("S1",) + m[i])
                            largest(("S2",) + m[i])
                        if i >= 1:
                            difference(i - 1)
                    for j in range(Z_PIECES, Z_PIECES + HIGHS):
                        split_low(j)
                    chunk = dec[:, 16:20, None].to_broadcast([P, R_HEADS, R_DV])
                    link(V.tensor_tensor(state1, state0v, chunk, ALU.mult))
                    link(V.tensor_copy(state2, state0v))
                    empty(("KV", 0), state_ctx[:, :], bank(("KV", 0)))
                    dve.wait_ge(*filled(("KV", 1)))
                    V.tensor_tensor(state2[0:64], state1[0:64], psum[0:64, J.bank(("KV", 1)), :].rearrange("p (h v) -> p h v", h=R_HEADS),
                                    ALU.add).then_inc(S["dve_emptied"], 1)
                    dve.wait_ge(*filled(("KV", 2)))
                    V.tensor_tensor(state1[64:128], state1[64:128], psum[64:128, J.bank(("KV", 2)), :].rearrange("p (h v) -> p h v", h=R_HEADS),
                                    ALU.add).then_inc(S["dve_emptied"], 1)
                    dve.wait_ge(*emptied(("KV", 2)))
                    V.tensor_copy(state1[0:64], state0v[0:64]).then_inc(S["state_ready"], 1)
                    dve.wait_ge(S["mask_ready"], 1)
                    for t in range(T):
                        for odd in range(2):
                            key = ("A", t, odd)
                            dve.wait_ge(*filled(key))
                            V.tensor_tensor(AT[t][:, odd::2], bank(key, 2 * P).rearrange("p (h n) -> p h n", h=2), mask[:, odd::2],
                                            ALU.mult).then_inc(S["dve_emptied"], 1)

                    split_activations(h_split_gates, False)
                    dve.wait_ge(*emptied(("R", T - 1)))
                    V.tensor_scalar(mu[:, :], mu[:, :], -1.0 / R_DV, None, ALU.mult).then_inc(S["mean_ready"], 1)
                    dve.wait_ge(S["ret_squared"], 1)
                    V.tensor_scalar(stat[:, 0:24], stat[:, 0:24], 1.0 / R_DV, EPS, ALU.mult, ALU.add).then_inc(S["var_ready"], 1)
                    dve.wait_ge(S["root_ready"], 3)
                    V.reciprocal(rs[:, 0:24], rs[:, 0:24]).then_inc(S["branch_rs"], 1)

                    def merge(n, c, t):
                        i = GATES.index((n, c, t))
                        dst = merged[:, t, c * C:(c + 1) * C]
                        dve.wait_ge(*emptied(("gl", n, c, t)))
                        dve.wait_ge(*filled(("br", n, c, t)))
                        V.tensor_tensor(dst if n == 0 else gtmp, bank(("br", n, c, t)), gs[i % 4],
                                        ALU.mult).then_inc(S["dve_emptied"], 1)
                        dve.wait_ge(*emptied(("br", n, c, t)))
                        if n:
                            link(V.tensor_tensor(dst, dst, gtmp, ALU.add))

                    def merged_low(k0, k1):
                        for k in range(k0, k1):
                            dve.wait_ge(S["mgT_high"], k + 1)
                            V.tensor_tensor(merged_split[1][:, k], bank(("mgT", k), 384), merged_split[0][:, k].bitcast(F32),
                                            ALU.subtract).then_inc(S["dve_emptied"], 1)

                    for j in range(Z_PIECES, OUT_PIECES):
                        kind, n, c, half = SPLITS[j]
                        if (kind, c, half) == ("gl", 0, 0):
                            for k in range(4):
                                dve.wait_ge(S["oT_high"], 4 * n + k + 1)
                                V.tensor_tensor(oT_split[1][:, k], bank(("oT", n, k), 384), oT_split[0][:, k].bitcast(F32),
                                                ALU.subtract).then_inc(S["dve_emptied"], 1)
                        if (kind, n, c) == ("br", NBR - 1, 1):
                            merged_low(0, KD // 2)
                        if kind == "br":
                            merge(n, c, 0)
                            merge(n, c, 1)
                        if (kind, n, c) != ("br", NBR - 1, 1):
                            split_low(j + HIGHS)
                        if kind == "br":
                            merge(n, c, 2)
                            if n == NBR - 1:
                                V.tensor_copy(rrec[:, c:c + 1], merged[:, 0, 0:1]).then_inc(S["merged_ready"], 1)
                    split_low(OUT_PIECES + 1)
                    merged_low(KD // 2, KD)
                    for j in range(OUT_PIECES + HIGHS, len(SPLITS)):
                        split_low(j)

                    def post_gains(n):
                        dve.wait_ge(S["gates_in"], 48 * (n + 1))
                        for v in range(2):
                            ins = V.tensor_tensor(gp[:, v], gp[:, v], gpost, ALU.mult)
                        link(ins)

                    def residual(rows_m, n, t):
                        dve.wait_ge(S["post_root"], n * T + t + 1)
                        r = rs[:, POST + t:POST + t + 1]
                        link(V.reciprocal(r, r))
                        link(V.scalar_tensor_tensor(rows_m[:, t], rows_m[:, t], r, gp[:, min(t, 1)], ALU.mult, ALU.mult))
                        V.tensor_tensor(xv[:, t], xv[:, t], rows_m[:, t], ALU.add).then_inc(S["x_ready"], 1)

                    def pre_norm(t):
                        dve.wait_ge(S["pre_root"], t + 1)
                        r = rs[:, PRE + t:PRE + t + 1]
                        link(V.reciprocal(r, r))
                        V.tensor_scalar(xn2[:, t], xv[:, t], r, None, ALU.mult).then_inc(S["mixture_rows"], 1)

                    post_gains(0)
                    for t in range(T):
                        residual(m_row, 0, t)
                        if t:
                            pre_norm(t - 1)
                    pre_norm(T - 1)
                    for t in range(T):
                        empty(("hrow", t, 0), xn2[:, t, 0:C], bank(("hrow", t, 0)))
                    dve.wait_ge(*emptied(("route",)))
                    link(V.tensor_scalar(rt[:, R_SC], rt[:, R_EXP], 1.0, None, ALU.add))
                    link(V.reciprocal(rt[:, R_SC], rt[:, R_SC]))
                    link(V.tensor_tensor(rt[:, R_SEL], rt[:, R_SC], brt[:, None, :].to_broadcast([P, T, NE]), ALU.add))
                    for t in range(T):
                        for g in range(NG):
                            ins = V.max(rt[:, R_TOP, t, g * EG:(g + 1) * EG], rt[:, R_SEL, t, g * EG:(g + 1) * EG])
                    link(ins)
                    top = rt[:, R_TOP].rearrange("p t (g e) -> p t g e", g=NG)
                    grp = rt[:, R_GRP, :, 0:NG]
                    link(V.tensor_tensor(grp, top[:, :, :, 0], top[:, :, :, 1], ALU.add))
                    dve.wait_ge(S["earlier_in"], 16)

                    def rank(v, largest, dst, n):
                        m = largest.shape[-1]
                        c1, c2 = cmp1[:, :, 0:n, 0:m], cmp2[:, :, 0:n, 0:n]
                        vj, vi = v[:, :, None, :].to_broadcast([P, T, n, n]), v[:, :, :, None].to_broadcast([P, T, n, n])
                        V.tensor_tensor(c1, largest[:, :, None, :].to_broadcast([P, T, n, m]), v[:, :, :, None].to_broadcast([P, T, n, m]),
                                        ALU.is_gt)
                        link(V.tensor_tensor(c2, vj, vi, ALU.is_equal))
                        link(V.tensor_tensor(c2, c2, before[:, None, 0:n, 0:n].to_broadcast([P, T, n, n]), ALU.mult))
                        V.tensor_reduce(rt[:, R_TMP, :, 0:n], c1, AX, ALU.add)
                        link(V.tensor_reduce(dst, c2, AX, ALU.add))
                        link(V.tensor_tensor(dst, dst, rt[:, R_TMP, :, 0:n], ALU.add))

                    gr = rt[:, R_GRP, :, NG:2 * NG]
                    gm = rt[:, R_GRP, :, 2 * NG:3 * NG]
                    go = rt[:, R_GRP, :, 3 * NG:4 * NG]
                    rank(grp, grp, gr, NG)
                    link(V.tensor_scalar(gm, gr, float(TOPG), None, ALU.is_lt))
                    link(V.tensor_scalar(go, gm, -1.0, 1e30, ALU.add, ALU.mult))
                    sel4 = rt[:, R_SEL].rearrange("p t (g e) -> p t g e", g=NG)
                    ms4 = rt[:, R_MSEL].rearrange("p t (g e) -> p t g e", g=NG)
                    link(V.tensor_tensor(ms4, sel4, gm[:, :, :, None].to_broadcast([P, T, NG, EG]), ALU.mult))
                    link(V.tensor_tensor(ms4, ms4, go[:, :, :, None].to_broadcast([P, T, NG, EG]), ALU.add))
                    for t in range(T):
                        ins = V.max(rt[:, R_TOP, t, 0:8], rt[:, R_MSEL, t])
                    link(ins)
                    rank(rt[:, R_MSEL], rt[:, R_TOP, :, 0:TOPK], rt[:, R_RANK], NE)
                    chosen = rt[:, R_TOP]
                    V.tensor_scalar(chosen, rt[:, R_RANK], float(TOPK), None, ALU.is_lt).then_inc(S["chosen_ready"], 1)
                    dve.wait_ge(S["chosen_ready"], 1)
                    link(V.tensor_tensor(rt[:, R_COMB], rt[:, R_SC], chosen, ALU.mult))
                    link(V.tensor_reduce(mu[:, 0:3], rt[:, R_COMB], AX, ALU.add))
                    link(V.reciprocal(mu[:, 0:3], mu[:, 0:3]))
                    link(V.scalar_tensor_tensor(rt[:, R_COMB], rt[:, R_COMB], ROUTE_SCALE,
                                                mu[:, 0:3, None].to_broadcast([P, T, NE]), ALU.mult, ALU.mult))

                    def product(gu, s, n):
                        dve.wait_ge(S["silu_ready"], n)
                        V.tensor_tensor(av[0:CAP, s], psum[0:CAP, gu, FF:2 * FF], silu[0:CAP, s], ALU.mult).then_inc(S["dve_emptied"], 1)

                    counts = counted.rearrange("p (t e) -> p t e", t=T + 1)
                    row_more, row_base, row_end = (rt[:, R_ROW, i] for i in range(3))
                    pos, slot, tmp = rt[:, R_POS], rt[:, R_SLOT], rt[:, R_TMP]
                    dve.wait_ge(*emptied(("place",)))
                    link(V.tensor_scalar(pos, counts[:, 0:T], -1.0, None, ALU.add))
                    link(V.tensor_scalar(row_base, counts[:, T], float(3 * CAP), None, ALU.is_gt))
                    link(V.scalar_tensor_tensor(row_base, counts[:, T], float(2 * CAP), row_base, ALU.is_gt, ALU.add))
                    link(V.scalar_tensor_tensor(row_more, counts[:, T], float(CAP), row_base, ALU.is_gt, ALU.add))
                    link(V.tensor_tensor_scan(row_end, row_more, row_more, 0.0, ALU.add, ALU.max))
                    link(V.tensor_tensor(row_base, row_end, row_more, ALU.subtract))
                    q1, q2 = rt[:, R_GRP], rt[:, R_EXP]
                    link(V.tensor_scalar(q1, pos, float(CAP), None, ALU.is_ge))
                    link(V.tensor_scalar(q2, pos, float(3 * CAP), None, ALU.is_ge))
                    link(V.scalar_tensor_tensor(q2, pos, float(2 * CAP), q2, ALU.is_ge, ALU.add))
                    link(V.scalar_tensor_tensor(slot, pos, float(NT), iota[:, None, :].to_broadcast([P, T, NE]), ALU.mult, ALU.add))
                    link(V.scalar_tensor_tensor(rt[:, R_SEL, 0], row_base, float(NE - CAP * NT), iota, ALU.add, ALU.subtract))
                    link(V.tensor_tensor(tmp, q1, rt[:, R_SEL, 0:1].to_broadcast([P, T, NE]), ALU.mult))
                    link(V.tensor_tensor(slot, slot, tmp, ALU.add))
                    link(V.scalar_tensor_tensor(slot, q2, float(1 - CAP * NT), slot, ALU.mult, ALU.add))
                    hot = zf[:, 11776:11776 + T * TOPK * NE].rearrange("p (t k e) -> p t k e", t=T, k=TOPK)
                    val = zf[:, 12288:12288 + T * TOPK * NE].rearrange("p (t k e) -> p t k e", t=T, k=TOPK)
                    for k in range(TOPK):
                        ins = V.tensor_scalar(hot[:, :, k], rt[:, R_RANK], float(k), None, ALU.is_equal)
                    link(ins)
                    for src, dst in ((slot, slot_f), (rt[:, R_COMB], weight)):
                        link(V.tensor_tensor(val, hot, src[:, :, None, :].to_broadcast([P, T, TOPK, NE]), ALU.mult))
                        link(V.tensor_reduce(dst.rearrange("p (t k) -> p t k", t=T), val, AX, ALU.add))
                    for t in range(T):
                        ins = V.tensor_scalar(token_f[:, t:t + 1], const[:, K_POS + 3:K_POS + 4], float(t * P), None, ALU.add)
                    link(ins)
                    V.tensor_copy(token_u, token_f)
                    V.tensor_copy(slot_u, slot_f).then_inc(S["slots_ready"], 1)
                    for t in range(T):
                        dve.wait_ge(S["silu_ready"], t + 1)
                        V.tensor_tensor(shared[:, t], bank(("gu", "s", t))[:, FF:2 * FF], shared[:, t], ALU.mult).then_inc(S["dve_emptied"], 1)
                    within = zf[:, 12800:12800 + NE * (MORE + 1)].rearrange("p (j e) -> p j e", e=NE)
                    below = zf[:, 13312:13312 + NE * (MORE + 1)].rearrange("p (j e) -> p j e", e=NE)
                    shape = [P, MORE + 1, NE]
                    j = iota[:, 0:MORE + 1, None].to_broadcast(shape)
                    link(V.tensor_tensor(within, row_base[:, None, :].to_broadcast(shape), j, ALU.is_le))
                    link(V.tensor_tensor(below, row_end[:, None, :].to_broadcast(shape), j, ALU.is_gt))
                    link(V.tensor_tensor(within, within, below, ALU.mult))
                    link(V.tensor_tensor(within, within, iota[:, None, :].to_broadcast(shape), ALU.mult))
                    link(V.tensor_copy(expert_f[:, 0:NE], iota))
                    link(V.tensor_reduce(expert_f[:, NE:NT], within, AX, ALU.add))
                    link(V.tensor_scalar(tmp[:, 0, 0:NT // 2 - NE // 2], iota[:, 0:MORE + 1:2], row_end[:, NE - 1:NE], None, ALU.is_lt))
                    link(V.tensor_reduce(turns_f, tmp[:, 0, 0:NT // 2 - NE // 2], AX, ALU.add))
                    link(V.tensor_scalar(turns_f, turns_f, float(NE // 2), None, ALU.add))
                    V.tensor_copy(expert_u, expert_f)
                    V.tensor_copy(turns_u, turns_f).then_inc(S["tables_ready"], 1)
                    for t in range(T):
                        for c in range(2):
                            empty(("y", "s", t, c), acc[:, t, c * C:(c + 1) * C], bank(("y", "s", t, c)))
                    dve.wait_ge(S["tables_ready"], 1)
                    for i in range(2):
                        empty(("xt", i, 1), xT[:, i, 4:8].rearrange("p k n -> p (k n)"), psum[:, BANK_XT + 1, 0:4 * CAP])
                    product(BANK_GU, 0, T + 1)
                    turns = turns_of(dve)

                    def steps(turn, last=False):
                        for e in range(2):
                            less = LESS["filled"][e] if last else 0
                            if not last:
                                dve.wait_ge(*job_filled(turn, e, "xt1"))
                                V.tensor_copy(xT[:, e, 4:8].rearrange("p k n -> p (k n)"), psum[:, BANK_XT + 1, 0:4 * CAP]).then_inc(S["dve_emptied"], 1)
                            if not (last and e == 1):
                                product(BANK_GU + 1 - e, 1 - e, turn * 2 + e + T + 2)
                            dve.wait_ge(*job_filled(turn, e, "y1", less))
                            dve.wait_ge(S[f"y_written{e}"], turn * 16 + 16)
                            V.tensor_copy(yrow[0:CAP, e, C:], psum[0:CAP, BANK_Y + 1, :]).then_inc(S["dve_emptied"], 1)

                    with dve.Fori(0, turns - 1) as turn:
                        steps(turn)
                    steps(turns - 1, last=True)
                    post_gains(1)
                    for i in range(T * TOPK):
                        dve.wait_ge(S[f"y_landed{i % 6}"], 16 * (i // 6 + 1))
                        V.scalar_tensor_tensor(acc[:, i // TOPK], ybuf[:, i % 6], weight[:, i:i + 1], acc[:, i // TOPK], ALU.mult,
                                               ALU.add).then_inc(S["summed"], 1)
                        dve.wait_ge(S["summed"], i + 1)
                        if i % TOPK == 1 and i > TOPK:
                            residual(acc, 1, i // TOPK - 1)
                    residual(acc, 1, T - 1)

                @block.tensor
                def _(pe):
                    def bank_free(key):
                        if J.before[key] is not None:
                            pe.wait_ge(*emptied(J.before[key]))

                    def multiply(dst, pairs):
                        for i, (lhsT, rhs) in enumerate(pairs):
                            ins = nc.tensor.matmul(dst, lhsT, rhs, start=(i == 0), stop=(i == len(pairs) - 1))
                        return ins

                    def turn_rows(key, sources, n=P):
                        bank_free(key)
                        for i, src in enumerate(sources):
                            ins = nc.tensor.transpose(psum[0:n, J.bank(key), i * P:(i + 1) * P], src, ident)
                        ins.then_inc(S["psum_filled"], 1)

                    def project(key, t, w, at, n, k_tiles, src=hTv):
                        bank_free(key)
                        multiply(bank(key, n), [(src[:, k, t * P:(t + 1) * P], w[:, k, at:at + n])
                                                     for k in range(k_tiles)]).then_inc(S["psum_filled"], 1)

                    pe.wait_ge(silc_ready, 1)
                    for m in range(12):
                        pe.wait_ge(*landed(("mod", m)))
                        w = mod_weights(m)
                        bank_free(("mod", m))
                        multiply(bank(("mod", m), C, slice(0, 2)),
                                 [(silTv[:, k, :], w[:, k, :]) for k in range(KD)]).then_inc(S["psum_filled"], 1)
                    pe.wait_ge(*emptied(("mod", 11)))
                    for q, at in enumerate((0, D, 3 * D, 4 * D)):
                        for k in range(KD):
                            col = (q * KD + k) * 2
                            ins = nc.tensor.transpose(psum[:, J.bank(("modT",)), col:col + 2], modrow[:, at + k * P:at + (k + 1) * P],
                                                      const[0:2, K_ID:K_ID + 2])
                    ins.then_inc(S["psum_filled"], 1)
                    pe.wait_ge(S["xn_ready"], 1)
                    for k in range(KD):
                        turn_rows(("h1", k), [xn[:, t, k * P:(k + 1) * P] for t in range(T)])
                    pe.wait_ge(*emptied(("h1", KD - 1)))

                    def project_split(j, src, k0):
                        key = SPLITS[j]
                        first = key[-1] == 0
                        last = key[-1] == 1 or key[0] == "br"
                        parts = [(src[a], (high(j), piece(key, Wr))[b]) for a, b in ((0, 0), (0, 1), (1, 0))]
                        pe.wait_ge(S["low_ready"], j + 1)
                        for t in range(T):
                            job = (*key[:-1], t)
                            if first:
                                bank_free(job)
                            for k in range(4):
                                for i, (act_part, w_part) in enumerate(parts):
                                    ins = nc.tensor.matmul(bank(job, piece_size(key)[1]), act_part[:, k0 + k, t * P:(t + 1) * P], w_part[:, k, :],
                                                           start=first and (k, i) == (0, 0), stop=last and (k, i) == (3, 2))
                            if last:
                                ins.then_inc(S["psum_filled"], 1)
                        if not last:
                            ins.then_inc(S["halves_used"], 1)

                    for j in range(Z_PIECES):
                        if j < 2:
                            pe.wait_ge(S["h_split"], 4 * (j + 1))
                        project_split(j, h_split_z, 4 * SPLITS[j][-1])
                    pe.wait_ge(S["cq_ready"], 1)
                    for k in range(3):
                        turn_rows(("cqT", k), [z[:, t, Z_CQ + k * P:Z_CQ + (k + 1) * P] for t in range(T)])
                    pe.wait_ge(S["ckv_ready"], 1)
                    pe.wait_ge(S["params_in"], 16 * N_PARAMS)
                    for k in range(2):
                        turn_rows(("ckvT", k), [tile_rows(c_ckv, Z_CKV, KV_LORA, kt)[:, k * P:(k + 1) * P] for kt in range(4)])

                    def softmax_maps(g):
                        m = MAPS[g]
                        for i in range(len(m) + 4):
                            if i < len(m):
                                key = ("S",) + m[i]
                                bank_free(key)
                                multiply(bank(key, P * len(keys_of(m[i][2]))), [(queries(*m[i]), keys(*m[i]))]).then_inc(S["psum_filled"], 1)
                            if i >= 4:
                                weigh_values(m[i - 4], i % 2)
                            if 2 <= i < len(m) + 2:
                                j = i - 2
                                pe.wait_ge(*emptied(("S",) + m[j]))
                                base = (j % 3) * 384
                                turn_rows(("PT",) + m[j], [Pb[:, base + b * P:base + (b + 1) * P] for b in range(len(keys_of(m[j][2])))])
                            if i >= len(m):
                                turn_next(g, i - len(m))

                    def turn_next(g, step):
                        if step == 0 and g in ("mb", "g"):
                            pe.wait_ge(S["kdup_ready" if g == "mb" else "diff_roped"], 1)
                        for key in TURNED_NEXT[g][step]:
                            kind, b = key
                            if kind == "gkT":
                                sources = [kdv[:, kt, b].rearrange("p c d -> p (c d)") for kt in range(4)]
                            elif kind == "dkT":
                                sources = [tile_rows(c_dk, Z_DK, 512, kt)[:, b * P:(b + 1) * P] for kt in range(4)]
                            else:
                                at = {"gqT": Z_GQ, "dqT": Z_DQ, "rqT": Z_RQ, "rkT": Z_RK}[kind] + b * P
                                sources = [z[:, t, at:at + P] for t in range(T)]
                            turn_rows(key, sources)

                    def weigh_values(mp, s):
                        key = ("O",) + mp
                        g, h, t = mp
                        bank_free(key)
                        pe.wait_ge(*emptied(("PT",) + mp))
                        multiply(bank(key, F_DV if g == "d" else HD),
                                 [(PTb[:, s * 384 + b * P:s * 384 + (b + 1) * P], values(g, h, kt))
                                  for b, kt in enumerate(keys_of(t))]).then_inc(S["psum_filled"], 1)

                    for c, g in enumerate(("ma", "mb")):
                        if c == 0:
                            pe.wait_ge(*emptied(("cqT", 2)))
                        pe.wait_ge(*landed(("uq", c)))
                        for t in range(T):
                            project(("qm", c, t), t, piece(("uq", c)), 0, 384, 3, cqT)
                        if c == 0:
                            pe.wait_ge(*emptied(("ckvT", 1)))
                        pe.wait_ge(*landed(("ukv", c)))
                        for kt in range(4):
                            project(("kv", c, kt), kt, piece(("ukv", c)), 0, C, 2, ckvT)
                        pe.wait_ge(S["km_ready"], 1)
                        pe.wait_ge(*emptied(("kv", c, 3)))
                        for h in range(HALF):
                            turn_rows(("mkT", c, h), [kmv[:, kt, h, :] for kt in range(4)], M_HD)
                        pe.wait_ge(S["qm_roped"], c + 1)
                        pe.wait_ge(*emptied(("qm", c, 2)))
                        for h in range(HALF):
                            turn_rows(("mqT", c, h), [qmv[:, t, h, :] for t in range(T)], M_HD)
                        pe.wait_ge(*emptied(("mkT", c, HALF - 1)))
                        pe.wait_ge(*emptied(("mqT", c, HALF - 1)))
                        softmax_maps(g)
                    pe.wait_ge(*emptied(("gqT", 3)))
                    pe.wait_ge(*emptied(("gkT", 1)))
                    softmax_maps("g")
                    pe.wait_ge(*emptied(("dqT", 3)))
                    pe.wait_ge(*emptied(("dkT", 3)))
                    m = MAPS["d"]
                    for i in range(len(m) + 4):
                        if i < len(m):
                            _, h, t = m[i]
                            cols = slice(0, P) if t == 0 else slice(P, 4 * P)
                            for s in range(2):
                                half = slice(64 * s, 64 * s + 64)
                                key = (("S1", "S2")[s],) + m[i]
                                bank_free(key)
                                multiply(bank(key, P * len(keys_of(t))), [(qTv[half, 1, h, t * P:(t + 1) * P], kTv[half, 1, h, cols])]
                                         ).then_inc(S["psum_filled"], 1)
                        if i >= 4:
                            weigh_values(m[i - 4], i % 2)
                        if 2 <= i < len(m) + 2:
                            j = i - 2
                            pe.wait_ge(S["pd_ready"], j + 1)
                            turn_rows(("PT",) + m[j], [first_map[:, j % 3, b * P:(b + 1) * P] for b in range(len(keys_of(m[j][2])))])
                        if i >= len(m):
                            turn_next("d", i - len(m))
                    pe.wait_ge(S["qkfb_ready"], 1)
                    for h in range(R_HEADS):
                        turn_rows(("qfbT", h), [qfb[:, t, h].rearrange("p f d -> p (f d)") for t in range(T)])

                    def retained(t, h):
                        return z[:, t, Z_RV + h * R_DV:Z_RV + (h + 1) * R_DV]

                    def part(key, h):
                        return psum[:, J.bank(key), h * P:(h + 1) * P]

                    for t in range(T):
                        bank_free(("KV", t))
                        for h in range(R_HEADS):
                            ins = multiply(part(("KV", t), h), [(kfb[:, t, h].rearrange("p f d -> p (f d)"), retained(t, h))])
                        ins.then_inc(S["psum_filled"], 1)
                    pe.wait_ge(*emptied(("rkT", 1)))
                    for t in range(T):
                        for odd in range(2):
                            key = ("A", t, odd)
                            bank_free(key)
                            for pair in range(2):
                                half, cols = slice(64 * odd, 64 * odd + 64), slice(t * P, (t + 1) * P)
                                ins = multiply(part(key, pair), [(qTv[half, 0, 2 + pair, cols], qTv[half, 0, pair, cols])])
                            ins.then_inc(S["psum_filled"], 1)
                    pe.wait_ge(*emptied(("qfbT", R_HEADS - 1)))
                    pe.wait_ge(S["state_ready"], 1)
                    for t in range(T):
                        bank_free(("R", t))
                        pe.wait_ge(*emptied(("A", t, 1)))
                        for h in range(R_HEADS):
                            pairs = [(AT[t][:, h, :], retained(t, h))]
                            if t:
                                pairs.append((qfbT[:, h, t * P:(t + 1) * P], (state1, state2)[t - 1][:, h, :]))
                            ins = multiply(part(("R", t), h), pairs)
                        ins.then_inc(S["psum_filled"], 1)
                    def turn_merged(c):
                        pe.wait_ge(S["merged_ready"], c + 1)
                        for k in range(4 * c, 4 * c + 4):
                            turn_rows(("mgT", k), [merged[:, t, k * P:(k + 1) * P] for t in range(T)])

                    for n in range(NBR):
                        if n >= 2:
                            pe.wait_ge(S["head_normed"], n - 1)
                        for k in range(4):
                            turn_rows(("oT", n, k), [z[:, t, OUT_COLS[n] + k * P:OUT_COLS[n] + (k + 1) * P] for t in range(T)])
                        pe.wait_ge(S["h_split"], 2 * KD)
                        for c in range(2):
                            for half in range(2):
                                project_split(SPLIT_AT["gl", n, c, half], h_split_gates, 4 * half)
                            if (n, c) == (NBR - 1, 1):
                                turn_merged(0)
                            pe.wait_ge(*emptied(("oT", n, 3)))
                            project_split(SPLIT_AT["br", n, c, 0], oT_split, 0)
                    turn_merged(1)
                    pe.wait_ge(*emptied(("mgT", KD - 1)))
                    for j in range(OUT_PIECES, len(SPLITS)):
                        project_split(j, merged_split, 4 * SPLITS[j][-1])
                    pe.wait_ge(S["mixture_rows"], T)
                    for k in range(KD):
                        turn_rows(("h2", k), [xn2[:, t, k * P:(k + 1) * P] for t in range(T)])
                    pe.wait_ge(*emptied(("h2", KD - 1)))
                    for t in range(T):
                        for c in range(2):
                            turn_rows(("hrow", t, c), [hTv[:, 4 * c + k, t * P:(t + 1) * P] for k in range(4)])
                    bank_free(("route",))
                    for t in range(T):
                        ins = multiply(psum[:, J.bank(("route",)), t * NE:(t + 1) * NE],
                                       [(hTv[:, k, t * P:(t + 1) * P], wr[:, k * NE:(k + 1) * NE]) for k in range(KD)])
                    ins.then_inc(S["psum_filled"], 1)

                    def turn_product(dst, product, n):
                        for f in range(2):
                            ins = nc.tensor.transpose(psum[:, dst, f * n:(f + 1) * n], product[:, f * P:(f + 1) * P], ident[0:n, 0:n])
                        ins.then_inc(S["psum_filled"], 1)

                    def down(dst, turned, w, c, n):
                        multiply(psum[0:n, dst, :], [(turned[:, f, :], expert_dn(w)[:, f, c * C:(c + 1) * C]) for f in range(2)]
                                 ).then_inc(S["psum_filled"], 1)

                    pe.wait_ge(S["gu_landed1"], 16)
                    for t in range(T):
                        bank_free(("gu", "s", t))
                        multiply(bank(("gu", "s", t)), [(hTv[:, k, t * P:(t + 1) * P], expert_gu(1)[:, k, :]) for k in range(KD)]
                                 ).then_inc(S["psum_filled"], 1)
                    pe.wait_ge(S["chosen_ready"], 1)
                    pe.wait_ge(S["ones_ready"], 1)
                    bank_free(("place",))
                    chosen = rt[:, R_TOP]
                    for q in range(T + 1):
                        pairs = [(ones, chosen[:, b, :]) for b in range(min(q, T))]
                        if q < T:
                            pairs.append((cview(K_MF, P), chosen[:, q, :]))
                        ins = multiply(psum[:, J.bank(("place",)), q * NE:(q + 1) * NE], pairs)
                    ins.then_inc(S["psum_filled"], 1)
                    pe.wait_ge(S["dn_landed1"], 16)
                    for t in range(T):
                        pe.wait_ge(*emptied(("gu", "s", t)))
                        bank_free(("aT", "s", t))
                        turn_product(J.bank(("aT", "s", t)), shared[:, t], P)
                        pe.wait_ge(*emptied(("aT", "s", t)))
                        for c in range(2):
                            bank_free(("y", "s", t, c))
                            down(J.bank(("y", "s", t, c)), shared_T[:, t], 1, c, P)

                    def turn_gathered(s):
                        for h in range(2):
                            for k in range(4):
                                ins = nc.tensor.transpose(psum[:, BANK_XT + h, k * CAP:(k + 1) * CAP], xg[0:CAP, s, (4 * h + k) * P:(4 * h + k + 1) * P],
                                                          ident[0:CAP, 0:CAP])
                            ins.then_inc(S["psum_filled"], 1)

                    def gate_up(s):
                        multiply(psum[0:CAP, BANK_GU + s, :], [(xT[:, s, k, :], expert_gu(s)[:, k, :]) for k in range(KD)]
                                 ).then_inc(S["psum_filled"], 1)

                    for i in range(2):
                        pe.wait_ge(S[f"x_landed{i}"], 16)
                        for h in range(2):
                            bank_free(("xt", i, h))
                        turn_gathered(i)
                    pe.wait_ge(*emptied(("xt", 0, 0)))
                    pe.wait_ge(*emptied(("xt", 0, 1)))
                    pe.wait_ge(S["gu_landed0"], 16)
                    bank_free(("gu", 0))
                    gate_up(0)
                    pe.wait_ge(S["act_emptied"], J.taken["act"])
                    pe.wait_ge(S["dve_emptied"], J.taken["dve"])
                    turns = turns_of(pe)

                    def steps(turn, last=False):
                        for e in range(2):
                            less = {"act": LESS["act"][e], "dve": LESS["dve"][e]} if last else {"act": 0, "dve": 0}
                            before = previous(turn, e)
                            gone = (1 if last and e == 1 else 0)
                            if not last:
                                pe.wait_ge(S[f"x_landed{e}"], turn * 16 + 32)
                                pe.wait_ge(*job_emptied(*before, "xt0"))
                                pe.wait_ge(*job_emptied(*before, "xt1"))
                                turn_gathered(e)
                            if not (last and e == 1):
                                if last:
                                    pe.wait_ge(*job_emptied(*before, "xt0"))
                                    pe.wait_ge(*job_emptied(*before, "xt1"))
                                pe.wait_ge(S[f"gu_landed{1 - e}"], turn * 16 + 32)
                                gate_up(1 - e)
                            pe.wait_ge(*job_emptied(*before, "gu", gone))
                            pe.wait_ge(*job_emptied(*before, "aT", gone))
                            turn_product(BANK_AT, av[0:CAP, e], CAP)
                            pe.wait_ge(*job_emptied(turn, e, "aT", less["act"]))
                            pe.wait_ge(S[f"dn_landed{e}"], turn * 16 + 16 * (e + 1))
                            pe.wait_ge(*job_emptied(*before, "y0", gone))
                            down(BANK_Y, aT[:, e], e, 0, CAP)
                            pe.wait_ge(*job_emptied(*before, "y1", gone))
                            down(BANK_Y + 1, aT[:, e], e, 1, CAP)

                    with pe.Fori(0, turns - 1) as turn:
                        steps(turn)
                    steps(turns - 1, last=True)

            nc.gpsimd.dma_reset(range(sems[0].num, sems[-1].num + 1))
            nc.gpsimd.sem_clear(range(sems[0].num, sems[-1].num + 1))
            nc.all_engine_barrier()

        with nc.Block() as block:
            @block.sync
            def _(sp):
                sp.dma_start(a["outs"]["y_prompt"][0], xv[:, 0, :]).then_inc(y_out, 16)
                sp.dma_start(a["outs"]["y_sample"][0].rearrange("(t p) n -> p t n", p=P), xv[:, 1:3, :]).then_inc(y_out, 16)
                sp.wait_ge(y_out, 32)


INPUTS = ["x_prompt", "x_sample", "cache_mla_ckv", "cache_mla_kpe", "cache_gqa_k", "cache_gqa_v", "cache_diff_k",
          "cache_diff_v", "state_ret", "c", "c_ctx", "w_mod", "b_mod", "g_pre1", "g_post1", "g_pre2", "g_post2", "w_in",
          "g_mla_q", "w_mla_uq", "g_mla_kv", "w_mla_ukv", "g_gqa_q", "g_gqa_k", "ret_decay", "g_ret", "diff_lambda",
          "g_diff", "w_br", "w_out", "w_router", "b_router", "w_exp_gu", "w_exp_down", "w_sh_gu", "w_sh_down"]
OUTPUTS = [("y_prompt", (1, P, D)), ("y_sample", (1, 2 * P, D)), ("mla_ckv", (1, DEPTH, P, KV_LORA)),
           ("mla_kpe", (1, DEPTH, P, M_ROPE)), ("gqa_k", (1, DEPTH, P, G_KV, HD)), ("gqa_v", (1, DEPTH, P, G_KV, HD)),
           ("diff_k", (1, DEPTH, P, F_HEADS, 2, HD)), ("diff_v", (1, DEPTH, P, F_HEADS, F_DV)),
           ("state_ret", (1, DEPTH, 2, R_HEADS, R_DK, R_DV))]


def kernel(**inputs):
    import concourse.bacc as bacc
    from concourse.bass_utils import run_bass_kernel_spmd

    nc = bacc.Bacc("TRN2", target_bir_lowering=False, num_devices=1)
    consts, earlier, lam_init = constants()
    no_tokens = np.ascontiguousarray(np.broadcast_to(np.arange(CAP, dtype=np.uint32)[:, None], (CAP, NT)))
    arrays = {name: np.ascontiguousarray(inputs[name]) for name in INPUTS}
    arrays.update(consts=consts, earlier=earlier, lam_init=lam_init, no_tokens=no_tokens)
    a = {name: nc.dram_tensor(f"in_{name}", v.shape, U32 if name == "no_tokens" else F32, kind="ExternalInput").ap() for name, v in arrays.items()}
    a["gate_rows"] = nc.dram_tensor("gate_rows", (2, 2, D), F32, kind="Internal").ap()
    a["token_rows"] = nc.dram_tensor("token_rows", (T * P, D), F32, kind="Internal").ap()
    a["y_slots"] = nc.dram_tensor("y_slots", (CAP * NT, D), F32, kind="Internal").ap()
    a["slot_tokens"] = nc.dram_tensor("slot_tokens", (CAP * NT, 1), U32, kind="Internal").ap()
    a["outs"] = {name: nc.dram_tensor(f"out_{name}", shape, F32, kind="ExternalOutput").ap() for name, shape in OUTPUTS}
    trunk(nc, a)
    r = run_bass_kernel_spmd(nc, [{f"in_{name}": v for name, v in arrays.items()}], core_ids=[0])
    return tuple(r.results[0][f"out_{name}"] for name, _ in OUTPUTS)
```
